# Optimizing a Trainium2 kernel written in Bass

```python
import math
import jax, jax.numpy as jnp
from jax import lax
import numpy as np

D_MODEL = 1024
BATCH = 1
SEQ = 512
DEPTH = 1

MEM_LEN = 256
EPS = 1e-6
CONV_WIDTH = 4
SSD_EXPAND = 2
SSD_WIDTH = SSD_EXPAND * D_MODEL
SSD_HEAD_DIM = 64
SSD_HEADS = SSD_WIDTH // SSD_HEAD_DIM
SSD_GROUPS = 4
SSD_STATE = 128
SSD_CHUNK = 128
SSD_CONV_CH = SSD_WIDTH + 2 * SSD_GROUPS * SSD_STATE
LRU_WIDTH = 3 * D_MODEL // 2
LRU_BLOCKS = 16
LRU_BLOCK = LRU_WIDTH // LRU_BLOCKS
LRU_C = 8.0
MEM_HEADS = 4
MEM_HEAD_DIM = D_MODEL // MEM_HEADS
N_BRANCH = 3
SPLIT_POINTS = (
    SSD_WIDTH,
    SSD_WIDTH + SSD_CONV_CH,
    SSD_WIDTH + SSD_CONV_CH + SSD_HEADS,
    SSD_WIDTH + SSD_CONV_CH + SSD_HEADS + LRU_WIDTH,
    SSD_WIDTH + SSD_CONV_CH + SSD_HEADS + 2 * LRU_WIDTH,
    SSD_WIDTH + SSD_CONV_CH + SSD_HEADS + 2 * LRU_WIDTH + D_MODEL,
)
IN_WIDTH = SSD_WIDTH + SSD_CONV_CH + SSD_HEADS + 2 * LRU_WIDTH + D_MODEL + N_BRANCH * D_MODEL


def rms_norm(x, g):
    xf = x.astype(jnp.float32)
    y = xf * lax.rsqrt(jnp.mean(xf * xf, axis=-1, keepdims=True) + EPS)
    return (y * g.astype(jnp.float32)).astype(x.dtype)

def causal_dwconv(x, w, b):
    k = w.shape[0]
    y = lax.conv_general_dilated(
        x, w[:, None, :].astype(x.dtype), window_strides=(1,), padding=[(k - 1, 0)],
        dimension_numbers=('NWC', 'WIO', 'NWC'), feature_group_count=x.shape[-1])
    return y + b

def ssd_scan(x, dt, a_neg, b_in, c_in):
    f32 = jnp.float32
    bsz, s, h, p = x.shape
    g, n = b_in.shape[2], b_in.shape[3]
    k = h // g
    l = SSD_CHUNK
    nc = s // l
    x = x.astype(f32).reshape(bsz, nc, l, g, k, p)
    dt = dt.astype(f32).reshape(bsz, nc, l, g, k)
    bm = b_in.astype(f32).reshape(bsz, nc, l, g, n)
    cm = c_in.astype(f32).reshape(bsz, nc, l, g, n)
    xdt = x * dt[..., None]
    a_cs = jnp.cumsum(dt * a_neg.astype(f32).reshape(g, k), axis=2)
    causal = jnp.tril(jnp.ones((l, l), dtype=bool))
    seg = a_cs[:, :, :, None] - a_cs[:, :, None, :]
    decay = jnp.exp(jnp.where(causal[:, :, None, None], seg, -jnp.inf))
    cb = jnp.einsum('bclgn,bcsgn->bclsg', cm, bm)
    y_diag = jnp.einsum('bclsgk,bcsgkp->bclgkp', decay * cb[..., None], xdt)
    decay_to_end = jnp.exp(a_cs[:, :, -1:] - a_cs)
    states = jnp.einsum('bclgn,bclgkp->bcgkpn', bm, xdt * decay_to_end[..., None])
    chunk_decay = jnp.exp(a_cs[:, :, -1])

    def step(carry, inp):
        st, dec = inp
        return carry * dec[..., None, None] + st, carry

    init = jnp.zeros((bsz, g, k, p, n), f32)
    _, prev = lax.scan(step, init, (jnp.moveaxis(states, 1, 0), jnp.moveaxis(chunk_decay, 1, 0)))
    prev = jnp.moveaxis(prev, 0, 1)
    y_off = jnp.einsum('bclgn,bcgkpn->bclgkp', cm, prev) * jnp.exp(a_cs)[..., None]
    return (y_diag + y_off).reshape(bsz, s, h, p)

def rg_lru(x, w_a, b_a, w_x, b_x, lam):
    f32 = jnp.float32
    bsz, s, w = x.shape
    xb = x.reshape(bsz, s, LRU_BLOCKS, LRU_BLOCK)
    r = jax.nn.sigmoid(jnp.einsum('bsni,nij->bsnj', xb, w_a) + b_a).reshape(bsz, s, w)
    i = jax.nn.sigmoid(jnp.einsum('bsni,nij->bsnj', xb, w_x) + b_x).reshape(bsz, s, w)
    log_a = (-LRU_C * r.astype(f32)) * jax.nn.softplus(-lam.astype(f32))
    a = jnp.exp(log_a)
    mult = jnp.sqrt(-jnp.expm1(2.0 * log_a))
    u = mult * (i * x).astype(f32)

    def combine(left, right):
        a1, b1 = left
        a2, b2 = right
        return a1 * a2, a2 * b1 + b2

    _, hs = lax.associative_scan(combine, (a, u), axis=1)
    return hs.astype(x.dtype)

def memory_attention(q, mem_n, w_kv):
    bsz, s, _ = q.shape
    m = mem_n.shape[1]
    kv = mem_n @ w_kv
    k, v = jnp.split(kv, 2, axis=-1)
    q = q.reshape(bsz, s, MEM_HEADS, MEM_HEAD_DIM)
    k = k.reshape(bsz, m, MEM_HEADS, MEM_HEAD_DIM)
    v = v.reshape(bsz, m, MEM_HEADS, MEM_HEAD_DIM)
    scores = jnp.einsum('bshd,bmhd->bhsm', q, k).astype(jnp.float32) * (MEM_HEAD_DIM ** -0.5)
    probs = jax.nn.softmax(scores, axis=-1).astype(v.dtype)
    return jnp.einsum('bhsm,bmhd->bshd', probs, v).reshape(bsz, s, D_MODEL)

def first_inputs(seed: int = 0) -> dict:
    key = jax.random.key(seed)
    ks = jax.random.split(key, 24)
    f32 = jnp.float32
    nrm = lambda k, shape, scale: jax.random.normal(k, shape, f32) * scale
    x = jax.random.normal(ks[0], (BATCH, SEQ, D_MODEL), f32)
    mem = jax.random.normal(ks[1], (BATCH, MEM_LEN, D_MODEL), f32)
    norm_g = 1.0 + nrm(ks[2], (DEPTH, D_MODEL), 0.02)
    w_in = nrm(ks[3], (DEPTH, D_MODEL, IN_WIDTH), D_MODEL ** -0.5)
    ssd_conv_w = nrm(ks[4], (DEPTH, CONV_WIDTH, SSD_CONV_CH), CONV_WIDTH ** -0.5)
    ssd_conv_b = nrm(ks[5], (DEPTH, SSD_CONV_CH), 0.02)
    dt0 = jnp.exp(jax.random.uniform(ks[6], (DEPTH, SSD_HEADS), f32, math.log(1e-3), math.log(1e-1)))
    ssd_dt_bias = dt0 + jnp.log(-jnp.expm1(-dt0))
    ssd_a_log = jnp.log(jax.random.uniform(ks[7], (DEPTH, SSD_HEADS), f32, 1.0, 16.0))
    ssd_d = 1.0 + nrm(ks[8], (DEPTH, SSD_HEADS), 0.02)
    ssd_norm_g = 1.0 + nrm(ks[9], (DEPTH, SSD_GROUPS, SSD_WIDTH // SSD_GROUPS), 0.02)
    lru_conv_w = nrm(ks[10], (DEPTH, CONV_WIDTH, LRU_WIDTH), CONV_WIDTH ** -0.5)
    lru_conv_b = nrm(ks[11], (DEPTH, LRU_WIDTH), 0.02)
    lru_w_a = nrm(ks[12], (DEPTH, LRU_BLOCKS, LRU_BLOCK, LRU_BLOCK), LRU_BLOCK ** -0.5)
    lru_b_a = nrm(ks[13], (DEPTH, LRU_BLOCKS, LRU_BLOCK), 0.02)
    lru_w_x = nrm(ks[14], (DEPTH, LRU_BLOCKS, LRU_BLOCK, LRU_BLOCK), LRU_BLOCK ** -0.5)
    lru_b_x = nrm(ks[15], (DEPTH, LRU_BLOCKS, LRU_BLOCK), 0.02)
    a8 = jax.random.uniform(ks[16], (DEPTH, LRU_WIDTH), f32, 0.9, 0.999)
    sig = a8 ** (1.0 / LRU_C)
    lru_lambda = jnp.log(sig) - jnp.log1p(-sig)
    mem_norm_g = 1.0 + nrm(ks[17], (DEPTH, D_MODEL), 0.02)
    w_kv = nrm(ks[18], (DEPTH, D_MODEL, 2 * D_MODEL), D_MODEL ** -0.5)
    w_br_ssd = nrm(ks[19], (DEPTH, SSD_WIDTH, D_MODEL), SSD_WIDTH ** -0.5)
    w_br_lru = nrm(ks[20], (DEPTH, LRU_WIDTH, D_MODEL), LRU_WIDTH ** -0.5)
    w_br_mem = nrm(ks[21], (DEPTH, D_MODEL, D_MODEL), D_MODEL ** -0.5)
    w_out = nrm(ks[22], (DEPTH, D_MODEL, D_MODEL), D_MODEL ** -0.5)
    final_g = 1.0 + nrm(ks[23], (D_MODEL,), 0.02)
    return {"x": x, "mem": mem, "norm_g": norm_g, "w_in": w_in,
            "ssd_conv_w": ssd_conv_w, "ssd_conv_b": ssd_conv_b, "ssd_dt_bias": ssd_dt_bias,
            "ssd_a_log": ssd_a_log, "ssd_d": ssd_d, "ssd_norm_g": ssd_norm_g,
            "lru_conv_w": lru_conv_w, "lru_conv_b": lru_conv_b, "lru_w_a": lru_w_a,
            "lru_b_a": lru_b_a, "lru_w_x": lru_w_x, "lru_b_x": lru_b_x, "lru_lambda": lru_lambda,
            "mem_norm_g": mem_norm_g, "w_kv": w_kv, "w_br_ssd": w_br_ssd, "w_br_lru": w_br_lru,
            "w_br_mem": w_br_mem, "w_out": w_out, "final_g": final_g}

def first_block(x, mem, norm_g, w_in, ssd_conv_w, ssd_conv_b, ssd_dt_bias, ssd_a_log, ssd_d,
              ssd_norm_g, lru_conv_w, lru_conv_b, lru_w_a, lru_b_a, lru_w_x, lru_b_x, lru_lambda,
              mem_norm_g, w_kv, w_br_ssd, w_br_lru, w_br_mem, w_out, final_g):
    bsz, s, _ = x.shape
    for l in range(DEPTH):
        h = rms_norm(x, norm_g[l])
        proj = h @ w_in[l]
        z, xbc, dt_raw, lru_gate, lru_x, q, gate_logits = jnp.split(proj, SPLIT_POINTS, axis=-1)

        xbc = jax.nn.silu(causal_dwconv(xbc, ssd_conv_w[l], ssd_conv_b[l]))
        xs, bs, cs = jnp.split(xbc, [SSD_WIDTH, SSD_WIDTH + SSD_GROUPS * SSD_STATE], axis=-1)
        xs = xs.reshape(bsz, s, SSD_HEADS, SSD_HEAD_DIM)
        dt = jax.nn.softplus((dt_raw + ssd_dt_bias[l]).astype(jnp.float32))
        y = ssd_scan(xs, dt, -jnp.exp(ssd_a_log[l].astype(jnp.float32)),
                     bs.reshape(bsz, s, SSD_GROUPS, SSD_STATE), cs.reshape(bsz, s, SSD_GROUPS, SSD_STATE))
        y = (y + xs.astype(jnp.float32) * ssd_d[l][:, None].astype(jnp.float32)).astype(x.dtype)
        y = y.reshape(bsz, s, SSD_WIDTH) * jax.nn.silu(z)
        y_ssd = rms_norm(y.reshape(bsz, s, SSD_GROUPS, SSD_WIDTH // SSD_GROUPS),
                         ssd_norm_g[l]).reshape(bsz, s, SSD_WIDTH)

        xl = causal_dwconv(lru_x, lru_conv_w[l], lru_conv_b[l])
        y_lru = rg_lru(xl, lru_w_a[l], lru_b_a[l], lru_w_x[l], lru_b_x[l], lru_lambda[l]) * jax.nn.silu(lru_gate)

        mem_n = rms_norm(mem, mem_norm_g[l])
        y_mem = memory_attention(q, mem_n, w_kv[l])

        gates = jax.nn.sigmoid(gate_logits).reshape(bsz, s, N_BRANCH, D_MODEL)
        merged = (gates[:, :, 0] * (y_ssd @ w_br_ssd[l])
                  + gates[:, :, 1] * (y_lru @ w_br_lru[l])
                  + gates[:, :, 2] * (y_mem @ w_br_mem[l]))
        x = x + merged @ w_out[l]
    return rms_norm(x, final_g)


_first_inputs = first_inputs


def first_inputs(seed=0):
    import zlib

    import numpy as np

    out = dict(_first_inputs(seed))
    spreads = {}
    factors = {'norm_g': 3.614,
     'ssd_conv_b': 17.533,
     'ssd_d': 64.0,
     'ssd_norm_g': 33.697,
     'lru_b_a': 33.029,
     'lru_b_x': 27.249,
     'mem_norm_g': 8.0,
     'final_g': 8.42,
     'lru_conv_b': 3.408}
    for name, (base, spread) in spreads.items():
        noise = np.random.default_rng([zlib.crc32(name.encode()), seed]).standard_normal(out[name].shape)
        drawn = base * np.exp(spread * noise) if base else spread * noise
        out[name] = __import__('jax').numpy.asarray(drawn.astype(out[name].dtype))
    for name, factor in factors.items():
        out[name] = (out[name] * factor).astype(out[name].dtype)
    return out


_narrow_inputs = first_inputs


def first_inputs(seed=0):

    out = dict(_narrow_inputs(seed))
    wider = {'ssd_d': 11.34,
     'ssd_norm_g': 3.36,
     'lru_conv_b': 3.27,
     'lru_b_a': 3.33,
     'lru_b_x': 3.3,
     'final_g': 3.28}
    for name, times in wider.items():
        mean = out[name].mean()
        out[name] = (mean + times * (out[name] - mean)).astype(out[name].dtype)
    return out


DEPTH_2 = 4

N_MIXERS = 4
N_A = (DEPTH_2 + 3) // 4
N_B = (DEPTH_2 + 2) // 4
N_C = (DEPTH_2 + 1) // 4
N_D = DEPTH_2 // 4
NEG_INF = -1e30

SSM_WIDTH = D_MODEL
SSM_GROUP = 16
SSM_GROUPS = SSM_WIDTH // SSM_GROUP
SSM_STATE = 64
DT_MIN = 1e-3
DT_MAX = 1e-1

HEAD_DIM = 64
SWA_HEADS = D_MODEL // HEAD_DIM
SWA_KV_HEADS = SWA_HEADS // 8
SWA_WIDTH = SWA_HEADS * HEAD_DIM
WINDOW = 128

REL_BUCKETS = 32
REL_MAX_DIST = 128

MLA_HEADS = 16
MLA_NOPE = 64
MLA_ROPE = 32
MLA_V = 64
MLA_KV_RANK = 256
MLA_Q_RANK = 768
MLA_WIDTH = MLA_HEADS * MLA_V
ROPE_BASE = 10000.0
Q_BLOCK = 128

SGU_WIDTH = D_MODEL
SGU_CHUNK = 128
SGU_GROUPS = 16
SGU_GROUP_DIM = SGU_WIDTH // SGU_GROUPS


def rmsnorm(x, g):
    xf = x.astype(jnp.float32)
    y = xf * lax.rsqrt(jnp.mean(xf * xf, axis=-1, keepdims=True) + EPS)
    return (y * g.astype(jnp.float32)).astype(x.dtype)

def layernorm(x, g, b):
    xf = x.astype(jnp.float32)
    mu = jnp.mean(xf, axis=-1, keepdims=True)
    var = jnp.mean(jnp.square(xf - mu), axis=-1, keepdims=True)
    y = (xf - mu) * lax.rsqrt(var + EPS) * g.astype(jnp.float32) + b.astype(jnp.float32)
    return y.astype(x.dtype)

def _ssm_combine(left, right):
    a1r, a1i, b1r, b1i = left
    a2r, a2i, b2r, b2i = right
    return (a2r * a1r - a2i * a1i,
            a2r * a1i + a2i * a1r,
            a2r * b1r - a2i * b1i + b2r,
            a2r * b1i + a2i * b1r + b2i)

def s5_mixer(u, lam_re, lam_im, log_dt, b_re, b_im, c_re, c_im, d_skip, w_glu, b_glu):
    f32 = jnp.float32
    bsz, L, _ = u.shape
    ug = u.astype(f32).reshape(bsz, L, SSM_GROUPS, SSM_GROUP)
    lr = lam_re.astype(f32)
    li = lam_im.astype(f32)
    dt = jnp.exp(log_dt.astype(f32))[:, None]
    mag = jnp.exp(lr * dt)
    ab_re = mag * jnp.cos(li * dt)
    ab_im = mag * jnp.sin(li * dt)
    den = lr * lr + li * li
    nr = ab_re - 1.0
    f_re = (nr * lr + ab_im * li) / den
    f_im = (ab_im * lr - nr * li) / den
    br = b_re.astype(f32)
    bi = b_im.astype(f32)
    bb_re = f_re[..., None] * br - f_im[..., None] * bi
    bb_im = f_re[..., None] * bi + f_im[..., None] * br
    bu_re = jnp.einsum('blgh,gph->blgp', ug, bb_re)
    bu_im = jnp.einsum('blgh,gph->blgp', ug, bb_im)
    a_re = jnp.broadcast_to(ab_re, (1, L) + ab_re.shape)
    a_im = jnp.broadcast_to(ab_im, (1, L) + ab_im.shape)
    _, _, s_re, s_im = lax.associative_scan(_ssm_combine, (a_re, a_im, bu_re, bu_im), axis=1)
    y = (jnp.einsum('blgp,ghp->blgh', s_re, c_re.astype(f32))
         - jnp.einsum('blgp,ghp->blgh', s_im, c_im.astype(f32)))
    y = y.reshape(bsz, L, SSM_WIDTH) + d_skip.astype(f32) * u.astype(f32)
    y = jax.nn.gelu(y).astype(u.dtype)
    return y * jax.nn.sigmoid(y @ w_glu + b_glu)

def s5_branch(h, w_in, lam_re, lam_im, log_dt, b_re, b_im, c_re, c_im, d_skip, w_glu, b_glu, w_out):
    u, z = jnp.split(h @ w_in, [SSM_WIDTH], axis=-1)
    y = s5_mixer(u, lam_re, lam_im, log_dt, b_re, b_im, c_re, c_im, d_skip, w_glu, b_glu)
    return (y * jax.nn.silu(z)) @ w_out

def t5_bucket(dist):
    max_exact = REL_BUCKETS // 2
    dist_f = jnp.maximum(dist, 1).astype(jnp.float32)
    large = max_exact + (jnp.log(dist_f / max_exact) / math.log(REL_MAX_DIST / max_exact)
                         * (REL_BUCKETS - max_exact)).astype(jnp.int32)
    large = jnp.minimum(large, REL_BUCKETS - 1)
    return jnp.where(dist < max_exact, dist, large)

def sliding_window_attention(q, k, v, sinks, rel_bias):
    bsz, L = q.shape[0], q.shape[1]
    nb = L // WINDOW
    grp = SWA_HEADS // SWA_KV_HEADS
    qb = q.reshape(bsz, nb, WINDOW, SWA_KV_HEADS, grp, HEAD_DIM)

    def band(t):
        prev = jnp.pad(t, ((0, 0), (WINDOW, 0), (0, 0), (0, 0)))[:, :L]
        shp = (bsz, nb, WINDOW, SWA_KV_HEADS, HEAD_DIM)
        return jnp.concatenate([prev.reshape(shp), t.reshape(shp)], axis=2)

    kb = band(k)
    vb = band(v)
    s = jnp.einsum('bnqhgd,bnkhd->bnhgqk', qb, kb).astype(jnp.float32) * (HEAD_DIM ** -0.5)
    qi = jnp.arange(WINDOW)[:, None]
    kj = jnp.arange(2 * WINDOW)[None, :]
    dist = qi + WINDOW - kj
    blk = jnp.arange(nb)[:, None, None]
    valid = (dist >= 0) & (dist < WINDOW) & (blk * WINDOW + kj - WINDOW >= 0)
    bias = rel_bias[t5_bucket(jnp.maximum(dist, 0))]
    bias = jnp.transpose(bias, (2, 0, 1)).reshape(SWA_KV_HEADS, grp, WINDOW, 2 * WINDOW).astype(jnp.float32)
    s = jnp.where(valid[None, :, None, None], s + bias, NEG_INF)
    sink = jnp.broadcast_to(sinks.astype(jnp.float32).reshape(SWA_KV_HEADS, grp, 1, 1), s.shape[:-1] + (1,))
    p = jax.nn.softmax(jnp.concatenate([s, sink], axis=-1), axis=-1)[..., :-1]
    o = jnp.einsum('bnhgqk,bnkhd->bnqhgd', p.astype(v.dtype), vb)
    return o.reshape(bsz, L, SWA_WIDTH)

def swa_branch(h, w_in, sinks, w_out, rel_bias):
    bsz, L, _ = h.shape
    kv_w = SWA_KV_HEADS * HEAD_DIM
    q, k, v, z = jnp.split(h @ w_in, [SWA_WIDTH, SWA_WIDTH + kv_w, SWA_WIDTH + 2 * kv_w], axis=-1)
    q = q.reshape(bsz, L, SWA_HEADS, HEAD_DIM)
    k = k.reshape(bsz, L, SWA_KV_HEADS, HEAD_DIM)
    v = v.reshape(bsz, L, SWA_KV_HEADS, HEAD_DIM)
    o = sliding_window_attention(q, k, v, sinks, rel_bias)
    return (o * jax.nn.silu(z)) @ w_out

def rope_tables(L):
    inv = ROPE_BASE ** (-jnp.arange(0, MLA_ROPE, 2, dtype=jnp.float32) / MLA_ROPE)
    ang = jnp.arange(L, dtype=jnp.float32)[:, None] * inv[None, :]
    return jnp.cos(ang), jnp.sin(ang)

def apply_rope(x, cos, sin):
    xf = x.astype(jnp.float32)
    x1, x2 = jnp.split(xf, 2, axis=-1)
    return jnp.concatenate([x1 * cos - x2 * sin, x2 * cos + x1 * sin], axis=-1).astype(x.dtype)

def causal_block_attention(q, k, v):
    bsz, L, H, dk = q.shape
    nb = L // Q_BLOCK
    scale = dk ** -0.5
    qb = q.reshape(bsz, nb, Q_BLOCK, H, dk).transpose(1, 0, 2, 3, 4)
    kpos = jnp.arange(L)

    def one_block(args):
        qi, n = args
        s = jnp.einsum('bqhd,bkhd->bhqk', qi, k).astype(jnp.float32) * scale
        qpos = n * Q_BLOCK + jnp.arange(Q_BLOCK)
        s = jnp.where(kpos[None, :] <= qpos[:, None], s, NEG_INF)
        p = jax.nn.softmax(s, axis=-1).astype(v.dtype)
        return jnp.einsum('bhqk,bkhd->bqhd', p, v)

    o = lax.map(one_block, (qb, jnp.arange(nb)))
    return o.transpose(1, 0, 2, 3, 4).reshape(bsz, L, H, v.shape[-1])

def mla_branch(h, w_in, q_norm, kv_norm, w_uq, w_ukv, w_out):
    bsz, L, _ = h.shape
    c_q, c_kv, k_rope, z = jnp.split(
        h @ w_in, [MLA_Q_RANK, MLA_Q_RANK + MLA_KV_RANK, MLA_Q_RANK + MLA_KV_RANK + MLA_ROPE], axis=-1)
    q = (rmsnorm(c_q, q_norm) @ w_uq).reshape(bsz, L, MLA_HEADS, MLA_NOPE + MLA_ROPE)
    kv = (rmsnorm(c_kv, kv_norm) @ w_ukv).reshape(bsz, L, MLA_HEADS, MLA_NOPE + MLA_V)
    cos, sin = rope_tables(L)
    q = jnp.concatenate([q[..., :MLA_NOPE], apply_rope(q[..., MLA_NOPE:], cos[:, None], sin[:, None])], axis=-1)
    k_rope = apply_rope(k_rope, cos, sin)
    k = jnp.concatenate([kv[..., :MLA_NOPE],
                         jnp.broadcast_to(k_rope[:, :, None, :], (bsz, L, MLA_HEADS, MLA_ROPE))], axis=-1)
    o = causal_block_attention(q, k, kv[..., MLA_NOPE:])
    return (o.reshape(bsz, L, MLA_WIDTH) * jax.nn.silu(z)) @ w_out

def sgu_branch(h, w_in, ln_g, ln_b, w_s, b_s, w_out):
    bsz, L, _ = h.shape
    uv, z = jnp.split(h @ w_in, [2 * SGU_WIDTH], axis=-1)
    u, v = jnp.split(jax.nn.gelu(uv), 2, axis=-1)
    v = layernorm(v, ln_g, ln_b).reshape(bsz, L // SGU_CHUNK, SGU_CHUNK, SGU_GROUPS, SGU_GROUP_DIM)
    tril = jnp.tril(jnp.ones((SGU_CHUNK, SGU_CHUNK), dtype=bool))
    w = jnp.where(tril[None], w_s, 0.0)
    s = jnp.einsum('gts,bnsgc->bntgc', w, v) + b_s.T[:, :, None]
    s = s.reshape(bsz, L, SGU_WIDTH)
    return (u * s * jax.nn.silu(z)) @ w_out

def second_inputs(seed: int = 0) -> dict:
    key = jax.random.key(seed)
    ks = iter(jax.random.split(key, 40))
    f32 = jnp.float32

    def nrm(shape, scale):
        return jax.random.normal(next(ks), shape, f32) * scale

    x = nrm((BATCH, SEQ, D_MODEL), 1.0)
    pre_norm = 1.0 + nrm((DEPTH_2, D_MODEL), 0.05)
    post_norm = 1.0 + nrm((DEPTH_2, D_MODEL), 0.05)
    rel_bias = nrm((REL_BUCKETS, SWA_HEADS), 0.5)
    a_w_in = nrm((N_A, D_MODEL, 2 * SSM_WIDTH), D_MODEL ** -0.5)
    n_idx = jnp.arange(SSM_STATE, dtype=f32)
    a_lam_re = -0.5 + nrm((N_A, SSM_GROUPS, SSM_STATE), 0.01)
    a_lam_im = jnp.pi * n_idx + nrm((N_A, SSM_GROUPS, SSM_STATE), 0.01)
    a_log_dt = jax.random.uniform(next(ks), (N_A, SSM_GROUPS), f32, math.log(DT_MIN), math.log(DT_MAX))
    a_b_re = nrm((N_A, SSM_GROUPS, SSM_STATE, SSM_GROUP), (2 * SSM_GROUP) ** -0.5)
    a_b_im = nrm((N_A, SSM_GROUPS, SSM_STATE, SSM_GROUP), (2 * SSM_GROUP) ** -0.5)
    a_c_re = nrm((N_A, SSM_GROUPS, SSM_GROUP, SSM_STATE), SSM_STATE ** -0.5)
    a_c_im = nrm((N_A, SSM_GROUPS, SSM_GROUP, SSM_STATE), SSM_STATE ** -0.5)
    a_d = nrm((N_A, SSM_WIDTH), 1.0)
    a_w_glu = nrm((N_A, SSM_WIDTH, SSM_WIDTH), SSM_WIDTH ** -0.5)
    a_b_glu = nrm((N_A, SSM_WIDTH), 0.02)
    a_w_out = nrm((N_A, SSM_WIDTH, D_MODEL), SSM_WIDTH ** -0.5)
    b_w_in = nrm((N_B, D_MODEL, 2 * SWA_WIDTH + 2 * SWA_KV_HEADS * HEAD_DIM), D_MODEL ** -0.5)
    b_sinks = nrm((N_B, SWA_HEADS), 1.0)
    b_w_out = nrm((N_B, SWA_WIDTH, D_MODEL), SWA_WIDTH ** -0.5)
    c_w_in = nrm((N_C, D_MODEL, MLA_Q_RANK + MLA_KV_RANK + MLA_ROPE + MLA_WIDTH), D_MODEL ** -0.5)
    c_q_norm = 1.0 + nrm((N_C, MLA_Q_RANK), 0.05)
    c_kv_norm = 1.0 + nrm((N_C, MLA_KV_RANK), 0.05)
    c_w_uq = nrm((N_C, MLA_Q_RANK, MLA_HEADS * (MLA_NOPE + MLA_ROPE)), MLA_Q_RANK ** -0.5)
    c_w_ukv = nrm((N_C, MLA_KV_RANK, MLA_HEADS * (MLA_NOPE + MLA_V)), MLA_KV_RANK ** -0.5)
    c_w_out = nrm((N_C, MLA_WIDTH, D_MODEL), MLA_WIDTH ** -0.5)
    d_w_in = nrm((N_D, D_MODEL, 3 * SGU_WIDTH), D_MODEL ** -0.5)
    d_ln_g = 1.0 + nrm((N_D, SGU_WIDTH), 0.05)
    d_ln_b = nrm((N_D, SGU_WIDTH), 0.02)
    d_w_s = nrm((N_D, SGU_GROUPS, SGU_CHUNK, SGU_CHUNK), 0.5 * SGU_CHUNK ** -0.5)
    d_b_s = 1.0 + nrm((N_D, SGU_GROUPS, SGU_CHUNK), 0.1)
    d_w_out = nrm((N_D, SGU_WIDTH, D_MODEL), SGU_WIDTH ** -0.5)
    return {'x': x, 'pre_norm': pre_norm, 'post_norm': post_norm, 'rel_bias': rel_bias,
            'a_w_in': a_w_in, 'a_lam_re': a_lam_re, 'a_lam_im': a_lam_im, 'a_log_dt': a_log_dt,
            'a_b_re': a_b_re, 'a_b_im': a_b_im, 'a_c_re': a_c_re, 'a_c_im': a_c_im, 'a_d': a_d,
            'a_w_glu': a_w_glu, 'a_b_glu': a_b_glu, 'a_w_out': a_w_out,
            'b_w_in': b_w_in, 'b_sinks': b_sinks, 'b_w_out': b_w_out,
            'c_w_in': c_w_in, 'c_q_norm': c_q_norm, 'c_kv_norm': c_kv_norm, 'c_w_uq': c_w_uq,
            'c_w_ukv': c_w_ukv, 'c_w_out': c_w_out,
            'd_w_in': d_w_in, 'd_ln_g': d_ln_g, 'd_ln_b': d_ln_b, 'd_w_s': d_w_s, 'd_b_s': d_b_s,
            'd_w_out': d_w_out}

def second_block(x, pre_norm, post_norm, rel_bias,
              a_w_in, a_lam_re, a_lam_im, a_log_dt, a_b_re, a_b_im, a_c_re, a_c_im, a_d,
              a_w_glu, a_b_glu, a_w_out,
              b_w_in, b_sinks, b_w_out,
              c_w_in, c_q_norm, c_kv_norm, c_w_uq, c_w_ukv, c_w_out,
              d_w_in, d_ln_g, d_ln_b, d_w_s, d_b_s, d_w_out):
    for i in range(DEPTH_2):
        kind = i % N_MIXERS
        j = i // N_MIXERS
        h = rmsnorm(x, pre_norm[i])
        if kind == 0:
            y = s5_branch(h, a_w_in[j], a_lam_re[j], a_lam_im[j], a_log_dt[j], a_b_re[j], a_b_im[j],
                          a_c_re[j], a_c_im[j], a_d[j], a_w_glu[j], a_b_glu[j], a_w_out[j])
        elif kind == 1:
            y = swa_branch(h, b_w_in[j], b_sinks[j], b_w_out[j], rel_bias)
        elif kind == 2:
            y = mla_branch(h, c_w_in[j], c_q_norm[j], c_kv_norm[j], c_w_uq[j], c_w_ukv[j], c_w_out[j])
        else:
            y = sgu_branch(h, d_w_in[j], d_ln_g[j], d_ln_b[j], d_w_s[j], d_b_s[j], d_w_out[j])
        x = x + rmsnorm(y, post_norm[i])
    return x


_first_inputs_2 = second_inputs


def second_inputs(seed=0):
    import zlib

    import numpy as np

    out = dict(_first_inputs_2(seed))
    spreads = {}
    factors = {'a_lam_re': 8.0, 'a_b_glu': 5.028, 'c_q_norm': 3.589, 'd_ln_g': 7.844, 'd_ln_b': 8.0}
    for name, (base, spread) in spreads.items():
        noise = np.random.default_rng([zlib.crc32(name.encode()), seed]).standard_normal(out[name].shape)
        drawn = base * np.exp(spread * noise) if base else spread * noise
        out[name] = __import__('jax').numpy.asarray(drawn.astype(out[name].dtype))
    for name, factor in factors.items():
        out[name] = (out[name] * factor).astype(out[name].dtype)
    return out


_narrow_inputs_2 = second_inputs


def second_inputs(seed=0):
    out = dict(_narrow_inputs_2(seed))
    wider = {'a_lam_re': 12.0, 'd_ln_g': 3.29, 'd_ln_b': 8.55, 'd_b_s': 3.35}
    for name, times in wider.items():
        mean = out[name].mean()
        out[name] = (mean + times * (out[name] - mean)).astype(out[name].dtype)
    return out


def setup_inputs(seed=0):
    out = dict(first_inputs(seed))
    for name, value in second_inputs(seed + 1).items():
        if name != "x":
            out[name + "_2"] = value
    return out


def reference(
    x, mem, norm_g, w_in, ssd_conv_w, ssd_conv_b, ssd_dt_bias, ssd_a_log, ssd_d, ssd_norm_g,
    lru_conv_w, lru_conv_b, lru_w_a, lru_b_a, lru_w_x, lru_b_x, lru_lambda, mem_norm_g, w_kv,
    w_br_ssd, w_br_lru, w_br_mem, w_out, final_g, pre_norm_2, post_norm_2, rel_bias_2, a_w_in_2,
    a_lam_re_2, a_lam_im_2, a_log_dt_2, a_b_re_2, a_b_im_2, a_c_re_2, a_c_im_2, a_d_2,
    a_w_glu_2, a_b_glu_2, a_w_out_2, b_w_in_2, b_sinks_2, b_w_out_2, c_w_in_2, c_q_norm_2,
    c_kv_norm_2, c_w_uq_2, c_w_ukv_2, c_w_out_2, d_w_in_2, d_ln_g_2, d_ln_b_2, d_w_s_2, d_b_s_2,
    d_w_out_2,
):
    x = first_block(
        x, mem, norm_g, w_in, ssd_conv_w, ssd_conv_b, ssd_dt_bias, ssd_a_log, ssd_d, ssd_norm_g,
        lru_conv_w, lru_conv_b, lru_w_a, lru_b_a, lru_w_x, lru_b_x, lru_lambda, mem_norm_g,
        w_kv, w_br_ssd, w_br_lru, w_br_mem, w_out, final_g,
    )
    return second_block(
        x, pre_norm_2, post_norm_2, rel_bias_2, a_w_in_2, a_lam_re_2, a_lam_im_2, a_log_dt_2,
        a_b_re_2, a_b_im_2, a_c_re_2, a_c_im_2, a_d_2, a_w_glu_2, a_b_glu_2, a_w_out_2,
        b_w_in_2, b_sinks_2, b_w_out_2, c_w_in_2, c_q_norm_2, c_kv_norm_2, c_w_uq_2, c_w_ukv_2,
        c_w_out_2, d_w_in_2, d_ln_g_2, d_ln_b_2, d_w_s_2, d_b_s_2, d_w_out_2,
    )


_drawn_inputs = setup_inputs


def setup_inputs(seed=0):
    import zlib

    import numpy as np

    out = dict(_drawn_inputs(seed))
    spreads = {}
    factors = {'post_norm_2': 4.68,
     'a_lam_re_2': 64.0,
     'a_lam_im_2': 64.0,
     'a_log_dt_2': 64.0,
     'a_b_re_2': 64.0,
     'a_b_im_2': 64.0,
     'a_c_re_2': 64.0,
     'a_c_im_2': 64.0,
     'a_b_glu_2': 8.0,
     'b_sinks_2': 8.0,
     'c_q_norm_2': 5.661,
     'c_kv_norm_2': 5.461,
     'd_ln_g_2': 3.391,
     'd_ln_b_2': 3.193,
     'd_b_s_2': 3.542}
    for name, (base, spread) in spreads.items():
        noise = np.random.default_rng([zlib.crc32(name.encode()), seed]).standard_normal(out[name].shape)
        drawn = base * np.exp(spread * noise) if base else spread * noise
        out[name] = __import__('jax').numpy.asarray(drawn.astype(out[name].dtype))
    for name, factor in factors.items():
        out[name] = (out[name] * factor).astype(out[name].dtype)
    return out
```

```python
from contextlib import ExitStack

import numpy as np

import concourse.bass as bass
from concourse import mybir

F32 = mybir.dt.float32
I32 = mybir.dt.int32
ALU = mybir.AluOpType
ACT = mybir.ActivationFunctionType
AX = mybir.AxisListType

P = 128
T = 512
TC = T // P
DM = 1024
KD = DM // P
EPS = 1e-6
SSD_W, SSD_H, SSD_G, SSD_P = 2048, 32, 4, 64
KS = SSD_W // P
LRU_W, LRU_B = 1536, 96
KL = LRU_W // P
MEM = 256
C_Z = 0
C_XBC = SSD_W
C_DT = C_XBC + SSD_W + 2 * SSD_G * P
C_LG = C_DT + SSD_H
C_LX = C_LG + LRU_W
C_Q = C_LX + LRU_W
C_GATE = C_Q + DM
NEG = -1e30

SLAB = 16
RING = 4


def span(a, n=P):
    return np.arange(a, a + n)


def weight_sections():
    sec = {}

    def add(name, blocks):
        sec.setdefault(name, []).extend(blocks)

    def tile(w, nk, cols):
        return [(w, span(k * P), cols) for k in range(nk)]

    add("dt", tile("w_in", KD, np.r_[span(C_DT, SSD_H), np.full(P - SSD_H, -1)]))
    for m in range(24):
        add("xbc", tile("w_in", KD, span(C_XBC + m * P)))
    for m in range(KS):
        add("z", tile("w_in", KD, span(C_Z + m * P)))
    for m in range(KD):
        add("merge0", tile("w_in", KD, span(C_GATE + m * P)))
        add("merge0", tile("w_br_ssd", KS, span(m * P)))
    for m in range(KL):
        add("lru_x", tile("w_in", KD, span(C_LX + m * P)))
    for w in ("lru_w_a", "lru_w_x"):
        for m in range(KL):
            for k in lru_inputs(m):
                add("lru_gates_" + w, [(w, span(k * P), span(m * P))])
    for m in range(KL):
        add("lru_g", tile("w_in", KD, span(C_LG + m * P)))
    for m in range(KD):
        add("merge1", tile("w_in", KD, span(C_GATE + DM + m * P)))
        add("merge1", tile("w_br_lru", KL, span(m * P)))
    for m in range(KD):
        add("mem_k", tile("w_kv", KD, span(m * P)))
    for half in range(2):
        for k in range(KD):
            for j in range(4):
                add("mem_v", [("w_kv", span(k * P), span(DM + half * 512 + j * P))])
    for m in range(KD):
        add("q", tile("w_in", KD, span(C_Q + m * P)))
    for m in range(KD):
        add("merge2", tile("w_in", KD, span(C_GATE + 2 * DM + m * P)))
        add("merge2", tile("w_br_mem", KD, span(m * P)))
    for m in range(KD):
        add("out", tile("w_out", KD, span(m * P)))
    more_sections(add, tile)
    return sec


def lru_inputs(m):
    first = (m * P) // LRU_B * LRU_B
    last = ((m * P + P - 1) // LRU_B + 1) * LRU_B
    return range(first // P, (last - 1) // P + 1)


def swa_heads(j):
    return np.r_[span(j * 64, 64), span((j + 8) * 64, 64)]


def more_sections(add, tile):
    for m in range(KD):
        add("s5_u", tile("a_w_in", KD, span(m * P)))
    for m in range(KD):
        add("s5_z", tile("a_w_in", KD, span(DM + m * P)))
    for m in range(KD):
        add("s5_glu", tile("a_w_glu", KD, span(m * P)))
    for m in range(KD):
        add("s5_out", tile("a_w_out", KD, span(m * P)))
    for m in range(KD):
        add("swa_q", tile("b_w_in", KD, swa_heads(m)))
    add("swa_k", tile("b_w_in", KD, span(DM)))
    add("swa_v", tile("b_w_in", KD, span(DM + P)))
    for m in range(KD):
        add("swa_z", tile("b_w_in", KD, DM + 2 * P + swa_heads(m)))
    for m in range(KD):
        add("swa_out", [("b_w_out", swa_heads(k), span(m * P)) for k in range(KD)])
    for m in range(8):
        add("mla_c", tile("c_w_in", KD, span(m * P)))
    swap = np.r_[span(16, 16), span(0, 16)]
    add("mla_kr", tile("c_w_in", KD, np.tile(1024 + span(0, 32), 4)))
    add("mla_kr", tile("c_w_in", KD, np.tile(1024 + swap, 4)))
    for h in range(16):
        nope, rope, swapped = 96 * h + span(0, 64), 96 * h + 64 + span(0, 32), 96 * h + 64 + swap
        cols = np.r_[nope, rope, swapped] if h % 2 == 0 else np.r_[rope, swapped, nope]
        add("mla_q", [("c_w_uq", span(k * P), cols) for k in range(6)])
    for half in range(2):
        for k in range(2):
            for j in range(4):
                h = 8 * half + 2 * j
                add("mla_v", [("c_w_ukv", span(k * P), np.r_[128 * h + 64 + span(0, 64), 128 * h + 192 + span(0, 64)])])
    for j in range(8):
        cols = np.r_[256 * j + span(0, 64), 256 * j + 128 + span(0, 64)]
        add("mla_kz", [("c_w_ukv", span(k * P), cols) for k in range(2)])
        add("mla_kz", tile("c_w_in", KD, span(1056 + j * P)))
    for m in range(KD):
        add("mla_out", tile("c_w_out", KD, span(m * P)))
    for half in range(2):
        for k in range(KD):
            for j in range(4):
                add("sgu_v", [("d_w_in", span(k * P), span(DM + half * 512 + j * P))])
    for m in range(KD):
        add("sgu_u", tile("d_w_in", KD, span(m * P)))
    for m in range(KD):
        add("sgu_z", tile("d_w_in", KD, span(2 * DM + m * P)))
    for m in range(KD):
        add("sgu_out", tile("d_w_out", KD, span(m * P)))


COLS = [("norm_g", 8), ("conv_w", 96), ("conv_b", 24), ("ssd_d", 16), ("ssd_norm_g", 16), ("dt_bias", 1), ("a_log", 1),
        ("lru_conv_w", 48), ("lru_conv_b", 12), ("b_a", 12), ("b_x", 12), ("lam", 12), ("mem_norm_g", 8), ("final_g", 8),
        ("pre_norm", 32), ("post_norm", 32), ("a_d", 8), ("b_glu", 8), ("lam_re", 32), ("lam_im", 32), ("log_dt", 32),
        ("q_norm", 6), ("kv_norm", 2), ("sinks", 16)]
COL_AT = {}
_n = 0
for _name, _k in COLS:
    COL_AT[_name] = _n
    _n += _k
NCOL = _n


class Span:

    def __init__(self, sem, base):
        self.sem, self.base = sem, base

    def at(self, i):
        return self.base + i + 1


class Counter:

    def __init__(self, nc, name):
        self.sem, self.total = nc.alloc_semaphore(name), 0

    def take(self, n):
        s = Span(self.sem, self.total)
        self.total += n
        return s


class Chain:

    def __init__(self, nc, name):
        self.sem, self.n = nc.alloc_semaphore(name), 0

    def link(self, eng, ins):
        self.n += 1
        ins.then_inc(self.sem, 1)
        eng.wait_ge(self.sem, self.n)


    def together(self, eng, ops):
        for ins in ops:
            self.n += 1
            ins.then_inc(self.sem, 1)
        eng.wait_ge(self.sem, self.n)


class Use:

    def __init__(self, b, n):
        self.b, self.n = b, n


class Core:

    def __init__(self, nc, io):
        self.nc, self.io = nc, io
        self.off = 16512
        self.names = 0
        self.bank = [nc.alloc_psum_tensor(f"bank{b}", [P, 512], F32) for b in range(8)]
        self.bank_full = [nc.alloc_semaphore(f"bank_full{b}") for b in range(8)]
        self.bank_read = [nc.alloc_semaphore(f"bank_read{b}") for b in range(8)]
        self.bank_uses = [0] * 8
        self.next_bank = 0
        self.pinned = ()
        self.slab_loaded = [nc.alloc_semaphore(f"slab_loaded{s}") for s in range(RING)]
        self.vchain, self.achain, self.gchain = Chain(nc, "vchain"), Chain(nc, "achain"), Chain(nc, "gchain")
        self.totals = {}
        self.block_no = 0
        self.slab_issued = 0
        self.slab_use = {}
        self.nslab = io["slabs"].shape[0]

    def fixed(self, name, shape, dt=F32):
        t = self.at(name, shape, self.off, dt)
        n = 1
        for d in shape[1:]:
            n *= d
        self.off += (n * 4 + 63) // 64 * 64
        return t

    def at(self, name, shape, off, dt=F32):
        self.names += 1
        return self.nc.alloc_sbuf_tensor_at(f"{name}_{self.names}", shape, dt, offset=off)

    def reserve(self, name, n):
        if name not in self.totals:
            self.totals[name] = Counter(self.nc, name)
        return self.totals[name].take(n)

    def take_bank(self):
        while self.next_bank in self.pinned:
            self.next_bank = (self.next_bank + 1) % 8
        b = self.next_bank
        self.next_bank = (b + 1) % 8
        self.bank_uses[b] += 1
        return Use(b, self.bank_uses[b])

    def take_given(self, b):
        self.bank_uses[b] += 1
        return Use(b, self.bank_uses[b])

    def open(self, pe, u):
        if u.n > 1:
            pe.wait_ge(self.bank_read[u.b], u.n - 1)

    def full(self, eng, u):
        eng.wait_ge(self.bank_full[u.b], u.n)

    def read(self, eng, u):
        eng.wait_ge(self.bank_read[u.b], u.n)

    def take_tile(self, nk):
        u = self.take_bank()
        blocks = self.take_blocks(nk, u)
        return u, blocks

    def take_blocks(self, n, u):
        out = []
        for _ in range(n):
            s, i = divmod(self.block_no, SLAB)
            out.append((s, i))
            self.block_no += 1
            if i == SLAB - 1:
                self.slab_use[s] = u
        return out

    def block(self, s, i, n=1):
        return self.ring[:, s % RING, i * P:(i + n) * P]

    def wait_slab(self, pe, s, seen):
        if s not in seen:
            pe.wait_ge(self.slab_loaded[s % RING], 16 * (s // RING + 1))
            seen.add(s)

    def load_slabs(self, sp):
        upto = min(self.block_no // SLAB + RING, self.nslab)
        while self.slab_issued < upto:
            s = self.slab_issued
            if s >= RING:
                self.full(sp, self.slab_use[s - RING])
            sp.dma_start(self.ring[:, s % RING, :], self.io["slabs"][s]).then_inc(self.slab_loaded[s % RING], 16)
            self.slab_issued += 1

    def gemm(self, pe, tile, moving, seen, n=T, rows=P, ready=None):
        u, blocks = tile
        self.open(pe, u)
        for k, (s, i) in enumerate(blocks):
            if ready is not None:
                ready(k)
            self.wait_slab(pe, s, seen)
            mm = pe.matmul(self.bank[u.b][0:rows, 0:n], self.block(s, i)[:, 0:rows], moving[k],
                           start=(k == 0), stop=(k == len(blocks) - 1))
        mm.then_inc(self.bank_full[u.b], 1)

    def col(self, name, i, n=1, rows=P):
        a = COL_AT[name] + i
        return self.cols[0:rows, a:a + n]


def stage_load(C):
    nc, io = C.nc, C.io
    loaded = C.reserve("loaded", 16 * 5)
    made = C.reserve("made", 16)
    with nc.Block(no_gpsimd_drain=True) as block:
        @block.sync
        def _(sp):
            sp.dma_start(C.X[:], io["xT"]).then_inc(loaded.sem, 16)
            C.load_slabs(sp)

        @block.scalar
        def _(act):
            act.dma_start(C.cols[:], io["cols"]).then_inc(loaded.sem, 16)
            act.wait_ge(loaded.sem, loaded.base + 32)

        @block.vector
        def _(dve):
            dve.memset(C.ones[:], 1.0)
            dve.memset(C.eps[:], EPS)

        @block.gpsimd
        def _(pool):
            pool.memset(C.ident[:], 0.0).then_inc(made.sem, 1)
            pool.memset(C.mask[:], 1.0).then_inc(made.sem, 1)
            pool.wait_ge(made.sem, made.at(1))
            pool.affine_select(out=C.ident[:], in_=C.ident[:], compare_op=ALU.not_equal, fill=1.0, base=0,
                               pattern=[[-1, P]], channel_multiplier=1).then_inc(made.sem, 1)
            pool.affine_select(out=C.mask[:], in_=C.mask[:], compare_op=ALU.is_ge, fill=0.0, base=0,
                               pattern=[[1, P]], channel_multiplier=-1).then_inc(made.sem, 1)
            pool.wait_ge(made.sem, made.at(3))


def stage_norm(C, groups, g, dst, dim, post=False, n=T):
    nc = C.nc
    src = [t for grp in groups for t in grp]
    banks = [C.take_bank() for _ in groups]
    squared = C.reserve("squared", len(src))
    summed = C.reserve("summed", len(src))
    rooted = C.reserve("rooted", len(groups))
    with nc.Block(no_gpsimd_drain=True) as block:
        @block.scalar
        def _(act):
            i = 0
            for gi, grp in enumerate(groups):
                for t in grp:
                    if i >= 4:
                        act.wait_ge(summed.sem, summed.at(i - 4))
                    act.activation(C.sq[:, i % 4, 0:n], t, ACT.Square).then_inc(squared.sem, 1)
                    i += 1
            for gi, u in enumerate(banks):
                C.full(act, u)
                act.activation(C.root[:, gi % 4, 0:n], C.bank[u.b][:, 0:n], ACT.Sqrt, bias=C.eps[:], scale=1.0 / dim)\
                    .then_inc(C.bank_read[u.b], 1)

        @block.tensor
        def _(pe):
            i = 0
            for gi, grp in enumerate(groups):
                u = banks[gi]
                C.open(pe, u)
                for k in range(len(grp)):
                    pe.wait_ge(squared.sem, squared.at(i))
                    pe.matmul(C.bank[u.b][:, 0:n], C.ones[:], C.sq[:, i % 4, 0:n], start=(k == 0),
                              stop=(k == len(grp) - 1)).then_inc(summed.sem, 1)
                    i += 1
                pe.wait_ge(summed.sem, summed.at(i - 1))
                pe.sem_inc(C.bank_full[u.b], 1)

        @block.vector
        def _(dve):
            i = 0
            for gi, grp in enumerate(groups):
                C.read(dve, banks[gi])
                C.vchain.link(dve, dve.reciprocal(C.root[:, gi % 4, 0:n], C.root[:, gi % 4, 0:n]))
                for t in grp:
                    if post:
                        C.vchain.link(dve, dve.scalar_tensor_tensor(
                            out=t, in0=t, scalar=g(i), in1=C.root[:, gi % 4, 0:n], op0=ALU.mult, op1=ALU.mult))
                        C.vchain.link(dve, dve.tensor_tensor(dst(i), dst(i), t, ALU.add))
                    else:
                        C.vchain.link(dve, dve.scalar_tensor_tensor(
                            out=dst(i), in0=t, scalar=g(i), in1=C.root[:, gi % 4, 0:n], op0=ALU.mult, op1=ALU.mult))
                    i += 1

        @block.sync
        def _(sp):
            C.load_slabs(sp)


def conv_tile(C, dve, u, w, b, acc):
    x = C.bank[u.b]
    C.vchain.link(dve, dve.tensor_scalar(acc, x[:], w(3), b, ALU.mult, ALU.add))
    for d in range(1, 4):
        ins = dve.scalar_tensor_tensor(out=acc[:, d:T], in0=x[:, 0:T - d], scalar=w(3 - d), in1=acc[:, d:T],
                                       op0=ALU.mult, op1=ALU.add)
        if d == 3:
            ins.then_inc(C.bank_read[u.b], 1)
        else:
            C.vchain.link(dve, ins)


def log1p_small(C, dve, e, s, s2, acc):
    ln = C.vchain.link
    ln(dve, dve.tensor_scalar(s, e, 2.0, None, ALU.add))
    ln(dve, dve.reciprocal(s, s))
    ln(dve, dve.tensor_tensor(s, s, e, ALU.mult))
    ln(dve, dve.tensor_tensor(s2, s, s, ALU.mult))
    ln(dve, dve.tensor_scalar(acc, s2, 2.0 / 17, None, ALU.mult))
    for k in range(15, 1, -2):
        ln(dve, dve.scalar_tensor_tensor(out=acc, in0=acc, scalar=2.0 / k, in1=s2, op0=ALU.add, op1=ALU.mult))
    ln(dve, dve.scalar_tensor_tensor(out=e, in0=acc, scalar=2.0, in1=s, op0=ALU.add, op1=ALU.mult))


def stage_xbc(C, L, batches):
    nc = C.nc
    dt = C.take_tile(KD)
    tiles = [C.take_tile(KD) for _ in range(24)]
    tables = Tables(C, L, batches)
    convolved = C.reserve("conv", 24)
    dts = C.reserve("dts", 9)
    tb = [C.take_bank() for _ in range(3)]
    with nc.Block(no_gpsimd_drain=True) as block:
        @block.sync
        def _(sp):
            C.load_slabs(sp)
            tables.store(sp)

        @block.gpsimd
        def _(pool):
            tables.make(pool)

        @block.tensor
        def _(pe):
            seen = set()
            C.gemm(pe, dt, [C.H[:, k, :] for k in range(KD)], seen)
            for t in tiles:
                C.gemm(pe, t, [C.H[:, k, :] for k in range(KD)], seen)
            pe.wait_ge(dts.sem, dts.at(5))
            for u, src in ((tb[0], L.DT), (tb[1], L.ACS)):
                C.open(pe, u)
                for c in range(TC):
                    t = pe.transpose(C.bank[u.b][:, c * 32:c * 32 + 32], src[:, c * P:(c + 1) * P], C.ident[0:32, 0:32])
                t.then_inc(C.bank_full[u.b], 1)
            u = tb[2]
            C.open(pe, u)
            pe.wait_ge(dts.sem, dts.at(6))
            pe.matmul(C.bank[u.b][:, 0:P], C.ones[0:32, :], L.END[:], start=True, stop=True)\
                .then_inc(C.bank_full[u.b], 1)

        @block.vector
        def _(dve):
            ln = C.vchain.link
            u = dt[0]
            C.full(dve, u)
            dve.tensor_scalar(L.DT[:], C.bank[u.b][0:32, :], C.col("dt_bias", 0, rows=32), None, ALU.add)\
                .then_inc(C.bank_read[u.b], 1)
            C.read(dve, u)
            ln(dve, dve.tensor_scalar(L.S1[:], L.DT[:], -1.0, None, ALU.mult))
            dve.tensor_tensor(L.S1[:], L.S1[:], L.DT[:], ALU.min).then_inc(dts.sem, 1)
            dve.wait_ge(dts.sem, dts.at(1))
            log1p_small(C, dve, L.S1[:], L.S2[:], L.S3[:], L.S4[:])
            ln(dve, dve.tensor_scalar(L.DT[:], L.DT[:], 0.0, None, ALU.max))
            ln(dve, dve.tensor_tensor(L.DT[:], L.DT[:], L.S1[:], ALU.add))
            ln(dve, dve.tensor_scalar(L.S1[:], L.DT[:], L.AN[0:32, :], -1.0, ALU.mult, ALU.mult))
            ln(dve, dve.memset(L.S2[:], 1.0))
            for c in range(TC):
                cs = slice(c * P, (c + 1) * P)
                dve.tensor_tensor_scan(L.ACS[:, cs], L.S2[:, cs], L.S1[:, cs], 0.0, ALU.mult, ALU.add)\
                    .then_inc(dts.sem, 1)
            dve.wait_ge(dts.sem, dts.at(5))
            ends = L.ACS[:].rearrange("h (c l) -> h c l", c=TC)[:, :, P - 1:P].to_broadcast([32, TC, 32])
            dve.tensor_tensor(L.END[:].rearrange("h (c k) -> h c k", c=TC), ends,
                              C.ident[0:32, 0:32].unsqueeze(1).to_broadcast([32, TC, 32]), ALU.mult)\
                .then_inc(dts.sem, 1)
            for i, (u, _) in enumerate(tiles):
                C.full(dve, u)
                if i >= 4:
                    dve.wait_ge(convolved.sem, convolved.at(i - 4))
                conv_tile(C, dve, u, lambda j: C.col("conv_w", 24 * j + i), C.col("conv_b", i), C.sq[:, i % 4, :])
            C.full(dve, tb[0])
            dve.tensor_copy(L.DTT[:], C.bank[tb[0].b][:, 0:P]).then_inc(C.bank_read[tb[0].b], 1)
            C.full(dve, tb[1])
            dve.tensor_copy(L.ACST[:], C.bank[tb[1].b][:, 0:P]).then_inc(C.bank_read[tb[1].b], 1)
            C.read(dve, tb[1])
            C.full(dve, tb[2])
            dve.tensor_copy(L.CD[:], C.bank[tb[2].b][:, 0:P]).then_inc(C.bank_read[tb[2].b], 1)
            C.read(dve, tb[2])
            dve.tensor_tensor(L.DTE[:], L.CD[:], L.ACST[:], ALU.subtract).then_inc(dts.sem, 1)
            C.read(dve, tb[0])
            dve.wait_ge(dts.sem, dts.at(8))
            ln(dve, dve.tensor_tensor(L.DTE[:], L.DTE[:], L.DTT[:], ALU.mult))

        @block.scalar
        def _(act):
            act.wait_ge(dts.sem, dts.at(0))
            C.achain.link(act, act.activation(L.AN[:], C.col("a_log", 0), ACT.Exp))
            act.activation(L.S1[:], L.S1[:], ACT.Exp).then_inc(dts.sem, 1)
            for i, (u, _) in enumerate(tiles):
                C.read(act, u)
                dst = L.XS[:, i, :] if i < 16 else L.BC[:, i - 16, :]
                act.activation(dst, C.sq[:, i % 4, :], ACT.Silu).then_inc(convolved.sem, 1)
            act.wait_ge(dts.sem, dts.at(7))
            C.achain.link(act, act.activation(L.DTE[:], L.DTE[:], ACT.Exp))
            act.activation(L.CD[:], L.CD[:], ACT.Exp).then_inc(dts.sem, 1)


def stage_ssd(C, L):
    nc = C.nc
    G, NH = SSD_G, 8
    B = {}
    for g in range(G):
        B["bt", g] = C.take_bank()
        for c in range(TC):
            B["xt", g, c] = C.take_bank()
        B["cb", g] = C.take_bank()
        for c in range(3):
            B["st", g, c] = C.take_bank()
        for j in range(4):
            for e in range(2):
                B["abc", g, 2 * j + e] = C.take_bank()
            B["z", g, j] = C.take_tile(KD)
            B["y", g, j] = C.take_bank()
    ea = C.reserve("ea", 32)
    ce = C.reserve("ce", 32)
    seg = C.reserve("seg", 32)
    dec = C.reserve("dec", 32)
    mr = C.reserve("mr", 32)
    xd = C.reserve("xd", G * 8)
    pv = C.reserve("pv", G * 6)

    def prev(c):
        return L.PV[:, c - 1, :]

    with nc.Block(no_gpsimd_drain=True) as block:
        @block.sync
        def _(sp):
            C.load_slabs(sp)

        @block.tensor
        def _(pe):
            seen = set()
            for g in range(G):
                bg, cg = L.BC[:, g, :], L.BC[:, 4 + g, :]
                u = B["bt", g]
                C.open(pe, u)
                for c in range(TC):
                    t = pe.transpose(C.bank[u.b][:, c * P:(c + 1) * P], bg[:, c * P:(c + 1) * P], C.ident[:])
                t.then_inc(C.bank_full[u.b], 1)
                for c in range(TC):
                    u = B["xt", g, c]
                    C.open(pe, u)
                    for j in range(4):
                        t = pe.transpose(C.bank[u.b][:, j * P:(j + 1) * P], L.XS[:, 4 * g + j, c * P:(c + 1) * P],
                                         C.ident[:])
                    t.then_inc(C.bank_full[u.b], 1)
                u = B["cb", g]
                C.open(pe, u)
                for c in range(TC):
                    cs = slice(c * P, (c + 1) * P)
                    t = pe.matmul(C.bank[u.b][:, cs], bg[:, cs], cg[:, cs], start=True, stop=True)
                t.then_inc(C.bank_full[u.b], 1)
                C.read(pe, B["bt", g])
                for c in range(3):
                    u = B["st", g, c]
                    C.open(pe, u)
                    pe.wait_ge(xd.sem, xd.at(8 * g + 2 * c + 1))
                    pe.matmul(C.bank[u.b][:], L.BT[:, c * P:(c + 1) * P], L.XDE[:, c, :], start=True, stop=True)\
                        .then_inc(C.bank_full[u.b], 1)
                for j in range(4):
                    for e in range(2):
                        h = 8 * g + 2 * j + e
                        u = B["abc", g, 2 * j + e]
                        C.open(pe, u)
                        pe.matmul(C.bank[u.b][:], C.ident[0:32, h:h + 1].to_broadcast([32, P]), L.ACS[:], start=True,
                                  stop=True).then_inc(C.bank_full[u.b], 1)
                    C.gemm(pe, B["z", g, j], [C.H[:, k, :] for k in range(KD)], seen)
                    u = B["y", g, j]
                    C.open(pe, u)
                    pe.wait_ge(xd.sem, xd.at(8 * g + 7))
                    pe.wait_ge(pv.sem, pv.at(6 * g + 5))
                    for e in range(2):
                        h = 8 * g + 2 * j + e
                        pe.wait_ge(mr.sem, mr.at(h))
                        pe.wait_ge(ce.sem, ce.at(h))
                        hp = slice((2 * j + e) * 64, (2 * j + e) * 64 + 64)
                        for c in range(TC):
                            cs = slice(c * P, (c + 1) * P)
                            dst = C.bank[u.b][64 * e:64 * e + 64, cs]
                            t = pe.matmul(dst, L.XDT[:, c, hp], L.DEC[:, h % 4, cs], start=True, stop=(c == 0))
                            if c > 0:
                                t = pe.matmul(dst, prev(c)[:, hp], L.CE[:, h % 4, cs], start=False, stop=True)
                    t.then_inc(C.bank_full[u.b], 1)

        @block.vector
        def _(dve):
            ln = C.vchain.link

            def heads(v, c, g):
                return v[:, c * 32 + 8 * g:c * 32 + 8 * g + 8].unsqueeze(2).to_broadcast([P, 8, 64])

            def v3(ap):
                return ap.rearrange("p (h q) -> p h q", h=8)

            def add_y(g, j):
                u = B["y", g, j]
                C.full(dve, u)
                xs = L.XS[:, 4 * g + j, :]
                dve.scalar_tensor_tensor(out=xs, in0=xs, scalar=C.col("ssd_d", 4 * g + j), in1=C.bank[u.b][:],
                                         op0=ALU.mult, op1=ALU.add).then_inc(C.bank_read[u.b], 1)

            for g in range(G):
                if g > 0:
                    add_y(g - 1, 3)
                for c in range(TC):
                    u = B["xt", g, c]
                    C.full(dve, u)
                    dve.tensor_tensor(v3(L.XDT[:, c, :]), v3(C.bank[u.b][:]), heads(L.DTT[:], c, g), ALU.mult)\
                        .then_inc(xd.sem, 1)
                    dve.wait_ge(xd.sem, xd.at(8 * g + 2 * c))
                    dve.tensor_tensor(v3(L.XDE[:, c, :]), v3(C.bank[u.b][:]), heads(L.DTE[:], c, g), ALU.mult)\
                        .then_inc(xd.sem, 1)
                    dve.wait_ge(xd.sem, xd.at(8 * g + 2 * c + 1))
                    dve.sem_inc(C.bank_read[u.b], 1)
                u = B["cb", g]
                C.full(dve, u)
                dve.tensor_tensor(L.CBM[:].rearrange("s (c l) -> s c l", c=TC),
                                  C.bank[u.b][:].rearrange("s (c l) -> s c l", c=TC),
                                  C.mask[:].unsqueeze(1).to_broadcast([P, TC, P]), ALU.mult)\
                    .then_inc(C.bank_read[u.b], 1)
                for c in range(3):
                    u = B["st", g, c]
                    C.full(dve, u)
                    if c > 0:
                        dve.tensor_tensor(v3(prev(c + 1)), v3(prev(c)), heads(L.CD[:], c, g), ALU.mult)\
                            .then_inc(pv.sem, 1)
                        dve.wait_ge(pv.sem, pv.at(6 * g + 2 * c))
                        dve.tensor_tensor(prev(c + 1), prev(c + 1), C.bank[u.b][:], ALU.add).then_inc(pv.sem, 1)
                        dve.wait_ge(pv.sem, pv.at(6 * g + 2 * c + 1))
                    else:
                        dve.tensor_copy(prev(1), C.bank[u.b][:]).then_inc(pv.sem, 1)
                        dve.wait_ge(pv.sem, pv.at(6 * g))
                        dve.sem_inc(pv.sem, 1)
                    dve.sem_inc(C.bank_read[u.b], 1)
                C.read(dve, B["cb", g])
                for j in range(4):
                    for e in range(2):
                        h = 8 * g + 2 * j + e
                        u = B["abc", g, 2 * j + e]
                        dve.wait_ge(ea.sem, ea.at(h))
                        if h >= 4:
                            C.full(dve, B["y", (h - 4) // 8, (h - 4) % 8 // 2])
                        acs = L.ACST[:].rearrange("s (c h) -> s c h", c=TC)[:, :, h:h + 1].to_broadcast([P, TC, P])
                        dve.tensor_tensor(L.DEC[:, h % 4, :].rearrange("s (c l) -> s c l", c=TC),
                                          C.bank[u.b][:].rearrange("s (c l) -> s c l", c=TC), acs, ALU.min)\
                            .then_inc(C.bank_read[u.b], 1)
                    if j > 0:
                        add_y(g, j - 1)
                    for e in range(2):
                        h = 8 * g + 2 * j + e
                        dve.wait_ge(dec.sem, dec.at(h))
                        dve.tensor_tensor(L.DEC[:, h % 4, :], L.DEC[:, h % 4, :], L.CBM[:], ALU.mult)\
                            .then_inc(mr.sem, 1)
            add_y(G - 1, 3)

        @block.gpsimd
        def _(pool):
            for g in range(G):
                for j in range(4):
                    for e in range(2):
                        h = 8 * g + 2 * j + e
                        acs = L.ACST[:].rearrange("s (c h) -> s c h", c=TC)[:, :, h:h + 1].to_broadcast([P, TC, P])
                        d = L.DEC[:, h % 4, :].rearrange("s (c l) -> s c l", c=TC)
                        C.read(pool, B["abc", g, 2 * j + e])
                        pool.tensor_tensor(d, d, acs, ALU.subtract).then_inc(seg.sem, 1)
                    for e in range(2):
                        h = 8 * g + 2 * j + e
                        pool.wait_ge(ea.sem, ea.at(h))
                        pool.tensor_tensor(L.CE[:, h % 4, :], L.CE[:, h % 4, :], L.BC[:, 4 + g, :], ALU.mult)\
                            .then_inc(ce.sem, 1)

        @block.scalar
        def _(act):
            for g in range(G):
                u = B["bt", g]
                C.full(act, u)
                act.activation(L.BT[:], C.bank[u.b][:], ACT.Copy).then_inc(C.bank_read[u.b], 1)
                for j in range(4):
                    for e in range(2):
                        h = 8 * g + 2 * j + e
                        u = B["abc", g, 2 * j + e]
                        C.full(act, u)
                        if h >= 4:
                            C.full(act, B["y", (h - 4) // 8, (h - 4) % 8 // 2])
                        act.activation(L.CE[:, h % 4, :], C.bank[u.b][:], ACT.Exp).then_inc(ea.sem, 1)
                    for e in range(2):
                        h = 8 * g + 2 * j + e
                        act.wait_ge(seg.sem, seg.at(h))
                        act.activation(L.DEC[:, h % 4, :], L.DEC[:, h % 4, :], ACT.Exp).then_inc(dec.sem, 1)
                    u = B["z", g, j][0]
                    C.full(act, u)
                    act.activation(L.SZ[:, 4 * g + j, :], C.bank[u.b][:], ACT.Silu).then_inc(C.bank_read[u.b], 1)


def stage_mul(C, pairs):
    with C.nc.Block(no_gpsimd_drain=True) as block:
        @block.vector
        def _(dve):
            for dst, src in pairs:
                dve.tensor_tensor(dst, dst, src, ALU.mult)


def stage_merge(C, L, br, moving, batches=()):
    nc = C.nc
    nk = len(moving)
    gate, prod = [], []
    for m in range(KD):
        gate.append(C.take_tile(KD))
        prod.append(C.take_tile(nk))
    tables = Tables(C, L, batches)
    with nc.Block(no_gpsimd_drain=True) as block:
        @block.sync
        def _(sp):
            C.load_slabs(sp)
            tables.store(sp)

        @block.gpsimd
        def _(pool):
            tables.make(pool)

        @block.tensor
        def _(pe):
            seen = set()
            for m in range(KD):
                C.gemm(pe, gate[m], [C.H[:, k, :] for k in range(KD)], seen)
                C.gemm(pe, prod[m], moving, seen)

        @block.scalar
        def _(act):
            for m in range(KD):
                u = gate[m][0]
                C.full(act, u)
                if m >= 4:
                    C.read(act, prod[m - 4][0])
                act.activation(C.sq[:, m % 4, :], C.bank[u.b][:], ACT.Sigmoid).then_inc(C.bank_read[u.b], 1)

        @block.vector
        def _(dve):
            for m in range(KD):
                u = prod[m][0]
                C.full(dve, u)
                C.read(dve, gate[m][0])
                if br == 0:
                    dve.tensor_tensor(C.MG[:, m, :], C.sq[:, m % 4, :], C.bank[u.b][:], ALU.mult)\
                        .then_inc(C.bank_read[u.b], 1)
                else:
                    g = C.sq[:, m % 4, :]
                    C.vchain.link(dve, dve.tensor_tensor(g, g, C.bank[u.b][:], ALU.mult))
                    dve.tensor_tensor(C.MG[:, m, :], C.MG[:, m, :], g, ALU.add).then_inc(C.bank_read[u.b], 1)


def stage_gemm(C, nt, moving, evac, engine="scalar", n=T, then=None):
    nc = C.nc
    tiles = [C.take_tile(len(moving)) for _ in range(nt)]
    with nc.Block(no_gpsimd_drain=True) as block:
        @block.sync
        def _(sp):
            C.load_slabs(sp)

        @block.tensor
        def _(pe):
            seen = set()
            for t in tiles:
                C.gemm(pe, t, moving, seen, n=n)

        def program(eng):
            for i, (u, _) in enumerate(tiles):
                C.full(eng, u)
                evac(eng, i, C.bank[u.b]).then_inc(C.bank_read[u.b], 1)

        if engine == "scalar":
            block.scalar(program)
        else:
            block.vector(program)
        if then is not None:
            @block.vector
            def _(dve):
                for i, (u, _) in enumerate(tiles):
                    C.read(dve, u)
                    then(dve, i)


def stage_tokmajor(C, wide, src, dst, n_tok, act_fn=ACT.Copy):
    nc = C.nc
    nk = len(src)
    halves = []
    for _ in range(2 if wide == 4 else 1):
        us = [C.take_bank() for _ in range(n_tok)]
        halves.append((us, C.take_blocks(wide * nk, us[-1])))
    with nc.Block(no_gpsimd_drain=True) as block:
        @block.sync
        def _(sp):
            C.load_slabs(sp)

        @block.tensor
        def _(pe):
            seen = set()
            for us, blocks in halves:
                for u in us:
                    C.open(pe, u)
                for k in range(nk):
                    s, i = blocks[wide * k]
                    C.wait_slab(pe, s, seen)
                    for t, u in enumerate(us):
                        mm = pe.matmul(C.bank[u.b][:, 0:wide * P], src[k][:, t * P:(t + 1) * P], C.block(s, i, wide),
                                       start=(k == 0), stop=(k == nk - 1))
                        if k == nk - 1:
                            mm.then_inc(C.bank_full[u.b], 1)

        @block.scalar
        def _(act):
            for half, (us, _) in enumerate(halves):
                for t, u in enumerate(us):
                    C.full(act, u)
                    act.activation(dst(half, t), C.bank[u.b][:, 0:wide * P], act_fn).then_inc(C.bank_read[u.b], 1)


def stage_lru(C, L):
    nc = C.nc

    def evac(dve, i, bank):
        acc = L.XL[:, i, :]
        C.vchain.link(dve, dve.tensor_scalar(acc, bank[:], C.col("lru_conv_w", 36 + i), C.col("lru_conv_b", i),
                                             ALU.mult, ALU.add))
        for d in range(1, 4):
            ins = dve.scalar_tensor_tensor(out=acc[:, d:T], in0=bank[:, 0:T - d],
                                           scalar=C.col("lru_conv_w", 12 * (3 - d) + i), in1=acc[:, d:T],
                                           op0=ALU.mult, op1=ALU.add)
            if d < 3:
                C.vchain.link(dve, ins)
        return ins

    stage_gemm(C, KL, [C.H[:, k, :] for k in range(KD)], evac, "vector")

    sp_ = C.reserve("sps", 2)
    with nc.Block(no_gpsimd_drain=True) as block:
        @block.vector
        def _(dve):
            ln = C.vchain.link
            lam = C.col("lam", 0, 12)
            ln(dve, dve.tensor_scalar(L.SPA[:], lam, -1.0, None, ALU.mult))
            dve.tensor_tensor(L.SPB[:], L.SPA[:], lam, ALU.min).then_inc(sp_.sem, 1)
            dve.wait_ge(sp_.sem, sp_.at(1))
            log1p_small(C, dve, L.SPB[:], L.SPC[:], L.SPD[:], L.SPE[:])
            ln(dve, dve.tensor_scalar(L.SPA[:], L.SPA[:], 0.0, None, ALU.max))
            ln(dve, dve.tensor_tensor(L.SPA[:], L.SPA[:], L.SPB[:], ALU.add))
            ln(dve, dve.tensor_scalar(L.SPA[:], L.SPA[:], -8.0, None, ALU.mult))

        @block.scalar
        def _(act):
            act.wait_ge(sp_.sem, sp_.at(0))
            act.activation(L.SPB[:], L.SPB[:], ACT.Exp).then_inc(sp_.sem, 1)

    for w, b, dst in (("a", "b_a", L.R), ("x", "b_x", L.I)):
        tiles = [C.take_tile(len(lru_inputs(m))) for m in range(KL)]
        with nc.Block(no_gpsimd_drain=True) as block:
            @block.sync
            def _(sp):
                C.load_slabs(sp)

            @block.tensor
            def _(pe):
                seen = set()
                for m, t in enumerate(tiles):
                    C.gemm(pe, t, [L.XL[:, k, :] for k in lru_inputs(m)], seen)

            @block.scalar
            def _(act):
                for m, (u, _) in enumerate(tiles):
                    C.full(act, u)
                    act.activation(dst[:, m, :], C.bank[u.b][:], ACT.Sigmoid, bias=C.col(b, m))\
                        .then_inc(C.bank_read[u.b], 1)

    g = [C.take_tile(KD) for _ in range(KL)]
    ix = C.reserve("ix", 1)
    la, th, rt, sr = [C.reserve(n, KL) for n in ("la", "th", "rt", "sr")]
    NB = 4
    with nc.Block(no_gpsimd_drain=True) as block:
        @block.sync
        def _(sp):
            C.load_slabs(sp)

        @block.tensor
        def _(pe):
            seen = set()
            for t in g:
                C.gemm(pe, t, [C.H[:, k, :] for k in range(KD)], seen)

        @block.gpsimd
        def _(pool):
            for m in range(KL):
                C.gchain.link(pool, pool.tensor_tensor(L.I[:, m, :], L.I[:, m, :], L.XL[:, m, :], ALU.mult))
            pool.sem_inc(ix.sem, 1)

        @block.vector
        def _(dve):
            ln = C.vchain.link
            for m in range(KL):
                a = L.R[:, m, :]
                dve.tensor_scalar(a, a, L.SPA[:, m:m + 1], None, ALU.mult).then_inc(la.sem, 1)
            for b in range(0, KL, NB):
                for m in range(b, b + NB):
                    t, q = C.sq[:, m % NB, :], C.root[:, m % NB, :]
                    dve.wait_ge(th.sem, th.at(m))
                    ln(dve, dve.tensor_scalar(q, t, 1.0, None, ALU.add))
                    ln(dve, dve.reciprocal(q, q))
                    dve.scalar_tensor_tensor(out=q, in0=t, scalar=2.0, in1=q, op0=ALU.mult, op1=ALU.mult)\
                        .then_inc(rt.sem, 1)
                if b == 0:
                    dve.wait_ge(ix.sem, ix.at(0))
                for m in range(b, b + NB):
                    q = C.root[:, m % NB, :]
                    dve.wait_ge(sr.sem, sr.at(m))
                    ln(dve, dve.tensor_tensor(q, q, L.I[:, m, :], ALU.mult))
                    ln(dve, dve.tensor_tensor_scan(L.XL[:, m, :], L.R[:, m, :], q, 0.0, ALU.mult, ALU.add))
                for m in range(b, b + NB):
                    C.read(dve, g[m][0])
                    ln(dve, dve.tensor_tensor(L.XL[:, m, :], L.XL[:, m, :], L.G[:, m, :], ALU.mult))

        @block.scalar
        def _(act):
            for b in range(0, KL, NB):
                for m in range(b, b + NB):
                    t = C.sq[:, m % NB, :]
                    act.wait_ge(la.sem, la.at(m))
                    if m >= NB:
                        act.wait_ge(rt.sem, rt.at(m - NB))
                    C.achain.link(act, act.activation(t, L.R[:, m, :], ACT.Tanh, scale=-1.0))
                    act.activation(L.R[:, m, :], L.R[:, m, :], ACT.Exp).then_inc(th.sem, 1)
                for m in range(b, b + NB):
                    u = g[m][0]
                    C.full(act, u)
                    act.activation(L.G[:, m, :], C.bank[u.b][:], ACT.Silu).then_inc(C.bank_read[u.b], 1)
                for m in range(b, b + NB):
                    q = C.root[:, m % NB, :]
                    act.wait_ge(rt.sem, rt.at(m))
                    act.activation(q, q, ACT.Sqrt).then_inc(sr.sem, 1)


def stage_memnorm(C, L):
    nc = C.nc
    ld = C.reserve("memload", 16)
    with nc.Block(no_gpsimd_drain=True) as block:
        @block.sync
        def _(sp):
            sp.dma_start(L.M[:], C.io["memT"]).then_inc(ld.sem, 16)
            sp.wait_ge(ld.sem, ld.base + 16)
    stage_norm(C, [[L.M[:, k, :] for k in range(KD)]], lambda i: C.col("mem_norm_g", i), lambda i: L.M[:, i, :], DM, n=MEM)


def stage_mem_attention(C, L):
    nc = C.nc
    H, D = 4, 256
    sc = [[C.take_bank() for _ in range(2)] + [C.take_bank() for _ in range(4)] for _ in range(H)]
    mx = C.reserve("mx", 2 * H)
    ex = C.reserve("ex", 4 * H)
    pn = C.reserve("pn", 4 * H)
    with nc.Block(no_gpsimd_drain=True) as block:
        @block.sync
        def _(sp):
            C.load_slabs(sp)

        @block.tensor
        def _(pe):
            def scores(h):
                for t in range(TC):
                    u = sc[h][t // 2]
                    if t % 2 == 0:
                        C.open(pe, u)
                    for d in range(2):
                        mm = pe.matmul(C.bank[u.b][:, t % 2 * MEM:t % 2 * MEM + MEM], L.Q[:, 2 * h + d, t * P:(t + 1) * P],
                                       L.K[:, 2 * h + d, :], start=(d == 0), stop=(d == 1))
                    if t % 2:
                        mm.then_inc(C.bank_full[u.b], 1)

            scores(0)
            for h in range(H):
                if h + 1 < H:
                    scores(h + 1)
                for mt in range(2):
                    u = sc[h][2 + mt]
                    C.open(pe, u)
                    for t in range(TC):
                        pe.wait_ge(pn.sem, pn.at(4 * h + t))
                        mm = pe.transpose(C.bank[u.b][:, t * P:(t + 1) * P], L.PR[:, t, mt * P:(mt + 1) * P], C.ident[:])
                    mm.then_inc(C.bank_full[u.b], 1)
                for d in range(2):
                    u = sc[h][4 + d]
                    C.open(pe, u)
                    for mt in range(2):
                        C.read(pe, sc[h][2 + mt])
                        a = h * D + d * P
                        mm = pe.matmul(C.bank[u.b][:], L.V[:, mt, a:a + P], L.PT[:, mt, :], start=(mt == 0), stop=(mt == 1))
                    mm.then_inc(C.bank_full[u.b], 1)

        @block.vector
        def _(dve):
            ln = C.vchain.link
            for h in range(H):
                for t in (0, 2):
                    u = sc[h][t // 2]
                    C.full(dve, u)
                    ln(dve, dve.tensor_reduce(C.st[:, 0, t:t + 2], C.bank[u.b][:].rearrange("p (t m) -> p t m", t=2),
                                              AX.X, ALU.max))
                    dve.tensor_scalar(C.st[:, 1, t:t + 2], C.st[:, 0, t:t + 2], -(D ** -0.5), None, ALU.mult)\
                        .then_inc(mx.sem, 1)
                for t in range(TC):
                    dve.wait_ge(ex.sem, ex.at(4 * h + t))
                    ln(dve, dve.reciprocal(C.st[:, 3, t:t + 1], C.st[:, 2, t:t + 1]))
                    dve.tensor_scalar(L.PR[:, t, :], L.PR[:, t, :], C.st[:, 3, t:t + 1], None, ALU.mult)\
                        .then_inc(pn.sem, 1)
                for mt in range(2):
                    u = sc[h][2 + mt]
                    C.full(dve, u)
                    dve.tensor_copy(L.PT[:, mt, :], C.bank[u.b][:]).then_inc(C.bank_read[u.b], 1)

        @block.scalar
        def _(act):
            for h in range(H):
                for t in range(TC):
                    u = sc[h][t // 2]
                    act.wait_ge(mx.sem, mx.at(2 * h + t // 2))
                    if h > 0:
                        C.full(act, sc[h - 1][3])
                    act.activation(L.PR[:, t, :], C.bank[u.b][:, t % 2 * MEM:t % 2 * MEM + MEM], ACT.Exp,
                                   bias=C.st[:, 1, t:t + 1], scale=D ** -0.5, accum_out=C.st[:, 2, t:t + 1])\
                        .then_inc(ex.sem, 1)
                    if t % 2:
                        act.wait_ge(ex.sem, ex.at(4 * h + t))
                        act.sem_inc(C.bank_read[u.b], 1)
                for d in range(2):
                    u = sc[h][4 + d]
                    C.full(act, u)
                    act.activation(L.Y[:, 2 * h + d, :], C.bank[u.b][:], ACT.Copy).then_inc(C.bank_read[u.b], 1)


class Layout:
    pass


def add_into(C, dst):
    def evac(dve, i, bank):
        return dve.tensor_tensor(dst[:, i, :], dst[:, i, :], bank[:], ALU.add)
    return evac


def copy_to(dst, fn=ACT.Copy):
    def evac(act, i, bank):
        return act.activation(dst[:, i, :], bank[:, 0:dst.shape[2]], fn)
    return evac


def first_block(C):
    KB = 1024
    A = C.arena
    tiles = lambda buf, n: [buf[:, k, :] for k in range(n)]
    hk = tiles(C.H, KD)
    stage_norm(C, [tiles(C.X, KD)], lambda i: C.col("norm_g", i), lambda i: C.H[:, i, :], DM)

    L = Layout()
    L.XS = C.at("xs", [P, 16, T], A)
    L.BC = C.at("bc", [P, 8, T], A + 32 * KB)
    L.SZ = C.at("silu_z", [P, 16, T], A + 48 * KB)
    L.BT = C.at("b_tok", [P, T], A + 80 * KB)
    L.CBM = C.at("cb_masked", [P, T], A + 82 * KB)
    L.PV = C.at("prev_state", [P, 3, T], A + 84 * KB)
    L.DEC = C.at("decay", [P, 4, T], A + 90 * KB)
    L.CE = C.at("c_exp", [P, 4, T], C.ROOT_OFF)
    L.DT = C.at("dt", [32, T], A + 98 * KB)
    L.ACS = C.at("acs", [32, T], A + 100 * KB)
    L.END = C.at("acs_end", [32, P], A + 102 * KB)
    L.DTT = C.at("dt_tok", [P, P], A + 102 * KB + 512)
    L.ACST = C.at("acs_tok", [P, P], A + 103 * KB)
    L.DTE = C.at("dt_end", [P, P], A + 103 * KB + 512)
    L.CD = C.at("chunk_decay", [P, P], A + 104 * KB)
    L.AN = C.at("a_exp", [P, 1], A + 104 * KB + 512)
    L.S1, L.S2, L.S3, L.S4 = [C.at(f"dt_tmp{i}", [32, T], C.MG_OFF + 2 * KB * i) for i in range(4)]
    L.XDT = C.at("x_dt", [P, TC, T], C.MG_OFF)
    L.XDE = C.at("x_dt_end", [P, TC, T], C.MG_OFF + 8 * KB)
    L.E = C.at("rot", [P, 8, 2, T], A + 48 * KB)
    L.ET = C.at("rot_tmp", [P, 2, 8, T // 2], A + 80 * KB)
    stage_xbc(C, L, [0])
    stage_ssd(C, L)
    stage_mul(C, [(L.XS[:, i, :], L.SZ[:, i, :]) for i in range(16)])
    stage_norm(C, [[L.XS[:, 4 * g + j, :] for j in range(4)] for g in range(4)], lambda i: C.col("ssd_norm_g", i),
               lambda i: L.XS[:, i, :], 512)
    L.E = C.at("rot", [P, 8, 2, T], A + 32 * KB)
    L.ET = C.at("rot_tmp", [P, 2, 8, T // 2], A + 64 * KB)
    stage_merge(C, L, 0, tiles(L.XS, KS), [1])

    L = Layout()
    L.XL = C.at("lru_x", [P, KL, T], A)
    L.R = C.at("lru_r", [P, KL, T], A + 24 * KB)
    L.I = C.at("lru_i", [P, KL, T], A + 48 * KB)
    L.G = C.at("lru_g", [P, KL, T], A + 72 * KB)
    L.SPA, L.SPB, L.SPC, L.SPD, L.SPE = [C.at(f"sp{i}", [P, 12], A + 96 * KB + 64 * i) for i in range(5)]
    stage_lru(C, L)
    L.E = C.at("rot", [P, 8, 2, T], A + 32 * KB)
    L.ET = C.at("rot_tmp", [P, 2, 8, T // 2], A + 64 * KB)
    stage_merge(C, L, 1, tiles(L.XL, KL), [2])

    L = Layout()
    L.Q = C.at("mem_q", [P, KD, T], A)
    L.Y = C.at("mem_y", [P, KD, T], A + 16 * KB)
    L.M = C.at("mem", [P, KD, MEM], A + 32 * KB)
    L.K = C.at("mem_k", [P, KD, MEM], A + 40 * KB)
    L.V = C.at("mem_v", [P, 2, DM], A + 48 * KB)
    L.PR = C.at("probs", [P, TC, MEM], A + 56 * KB)
    L.PT = C.at("probs_t", [P, 2, T], A + 60 * KB)
    stage_memnorm(C, L)
    mk = tiles(L.M, KD)
    stage_gemm(C, KD, mk, copy_to(L.K), n=MEM)
    stage_tokmajor(C, 4, mk, lambda half, t: L.V[:, t, half * 512:half * 512 + 512], 2)
    stage_gemm(C, KD, hk, copy_to(L.Q))
    stage_mem_attention(C, L)
    L.E = C.at("rot", [P, 8, 2, T], A + 32 * KB)
    L.ET = C.at("rot_tmp", [P, 2, 8, T // 2], A + 64 * KB)
    stage_merge(C, L, 2, tiles(L.Y, KD), [3])
    stage_gemm(C, KD, tiles(C.MG, KD), add_into(C, C.X), "vector")
    stage_norm(C, [tiles(C.X, KD)], lambda i: C.col("final_g", i), lambda i: C.X[:, i, :], DM)


def stage_fetch(C, pairs):
    ld = C.reserve("fetched", 16 * len(pairs))
    with C.nc.Block(no_gpsimd_drain=True) as block:
        @block.sync
        def _(sp):
            for dst, src in pairs:
                sp.dma_start(dst, src).then_inc(ld.sem, 16)
            sp.wait_ge(ld.sem, ld.base + 16 * len(pairs))


class Tables:

    def __init__(self, C, L, batches):
        self.C, self.L, self.batches = C, L, batches
        self.made = C.reserve("tables", len(batches))
        self.kept = C.reserve("tables_kept", 16 * len(batches))

    def make(self, pool):
        for n, b in enumerate(self.batches):
            if n:
                pool.wait_ge(self.kept.sem, self.kept.base + 16 * n)
            rotation_tables(self.C, pool, b, self.L.E, self.L.ET, self.made)

    def store(self, sp):
        for n, b in enumerate(self.batches):
            sp.wait_ge(self.made.sem, self.made.at(n))
            sp.dma_start(self.C.io["rot"][8 * b:8 * b + 8].rearrange("j p a t -> p j (a t)"),
                         self.L.E[:].rearrange("p j a t -> p j (a t)")).then_inc(self.kept.sem, 16)
            sp.wait_ge(self.kept.sem, self.kept.base + 16 * (n + 1))


def stage_s5_coefficients(C):
    nc = C.nc
    K = C.s5
    lr, li = C.col("lam_re", 0, 32), C.col("lam_im", 0, 32)
    two_pi = 2 * np.pi
    c1 = 6.28125
    c2 = float(np.float32(np.round((two_pi - c1) * 2 ** 20) / 2 ** 20))
    c3 = float(np.float32(two_pi - c1 - c2))
    magic = 1.5 * 2 ** 23
    sg = C.reserve("s5coef", 4)
    t = lambda i: K.tmp[:, i, :]
    with nc.Block(no_gpsimd_drain=True) as block:
        @block.scalar
        def _(act):
            act.activation(t(0), C.col("log_dt", 0, 32), ACT.Exp).then_inc(sg.sem, 1)
            act.wait_ge(sg.sem, sg.at(1))
            C.achain.link(act, act.activation(K.mag[:], t(1), ACT.Exp))
            C.achain.link(act, act.activation(K.sin[:], t(2), ACT.Sin))
            act.activation(K.cos[:], t(3), ACT.Sin).then_inc(sg.sem, 1)

        @block.vector
        def _(dve):
            ln = lambda ins: C.vchain.link(dve, ins)
            tt, ts, stt = dve.tensor_tensor, dve.tensor_scalar, dve.scalar_tensor_tensor
            dve.wait_ge(sg.sem, sg.at(0))
            ln(tt(t(1), lr, t(0), ALU.mult))
            ln(tt(t(0), li, t(0), ALU.mult))
            ln(ts(t(3), t(0), 1.0 / two_pi, magic, ALU.mult, ALU.add))
            ln(ts(t(3), t(3), magic, None, ALU.subtract))
            for part in (c1, c2, c3):
                ln(stt(out=t(0), in0=t(3), scalar=-part, in1=t(0), op0=ALU.mult, op1=ALU.add))
            ln(ts(t(2), t(0), 3.1415925, -3.1415925, ALU.min, ALU.max))
            ln(stt(out=t(3), in0=t(2), scalar=-1.0, in1=t(2), op0=ALU.mult, op1=ALU.max))
            ts(t(3), t(3), -1.0, float(np.pi / 2), ALU.mult, ALU.add).then_inc(sg.sem, 1)
            dve.wait_ge(sg.sem, sg.at(2))
            ln(tt(t(0), K.mag[:], K.cos[:], ALU.mult))
            ln(ts(t(0), t(0), -1.0, None, ALU.add))
            ln(tt(t(1), K.mag[:], K.sin[:], ALU.mult))
            ln(tt(t(2), lr, lr, ALU.mult))
            ln(tt(t(3), li, li, ALU.mult))
            ln(tt(t(2), t(2), t(3), ALU.add))
            ln(dve.reciprocal(t(2), t(2)))
            ln(tt(K.fre[:], t(0), lr, ALU.mult))
            ln(tt(t(3), t(1), li, ALU.mult))
            ln(tt(K.fre[:], K.fre[:], t(3), ALU.add))
            ln(tt(K.fre[:], K.fre[:], t(2), ALU.mult))
            ln(tt(K.fim[:], t(1), lr, ALU.mult))
            ln(tt(t(3), t(0), li, ALU.mult))
            ln(tt(K.fim[:], K.fim[:], t(3), ALU.subtract))
            ln(tt(K.fim[:], K.fim[:], t(2), ALU.mult))


def rotation_tables(C, pool, batch, E, tmp, done):
    K = C.s5
    js = slice(8 * batch, 8 * batch + 8)
    s = [K.pw[:, i, :] for i in range(5)]
    tt = pool.tensor_tensor
    together = lambda *ops: C.gchain.together(pool, ops)
    together(pool.tensor_copy(s[0], K.cos[:, js]), pool.tensor_copy(s[1], K.sin[:, js]),
             pool.memset(E[:, :, 0, 0:1], 1.0), pool.memset(E[:, :, 1, 0:1], 0.0))
    w = 1
    while w < T:
        b = lambda a: a.unsqueeze(2).to_broadcast([P, 8, w])
        er, ei = E[:, :, 0, 0:w], E[:, :, 1, 0:w]
        nr, ni = E[:, :, 0, w:2 * w], E[:, :, 1, w:2 * w]
        t0, t1 = tmp[:, 0, :, 0:w], tmp[:, 1, :, 0:w]
        together(tt(nr, er, b(s[0]), ALU.mult), tt(t0, ei, b(s[1]), ALU.mult),
                 tt(ni, er, b(s[1]), ALU.mult), tt(t1, ei, b(s[0]), ALU.mult),
                 tt(s[2], s[0], s[0], ALU.mult), tt(s[3], s[1], s[1], ALU.mult), tt(s[4], s[0], s[1], ALU.mult))
        together(tt(nr, nr, t0, ALU.subtract), tt(ni, ni, t1, ALU.add),
                 tt(s[0], s[2], s[3], ALU.subtract), tt(s[1], s[4], s[4], ALU.add))
        w *= 2
    pool.sem_inc(done.sem, 1)


def stage_s5_b(C, L):
    nc = C.nc
    K = C.s5
    us = [C.take_bank() for _ in range(4)]
    zd = C.reserve("s5z", 3)
    with nc.Block(no_gpsimd_drain=True) as block:
        @block.sync
        def _(sp):
            C.load_slabs(sp)

        @block.gpsimd
        def _(pool):
            pool.memset(L.Z[:], 0.0).then_inc(zd.sem, 1)

        @block.vector
        def _(dve):
            ln = lambda ins: C.vchain.link(dve, ins)
            f = [a[:].unsqueeze(2).to_broadcast([P, 32, 16]) for a in (K.fre, K.fim)]
            ln(dve.tensor_tensor(L.BB[:, 0], L.BI[:, 0], f[0], ALU.mult))
            ln(dve.tensor_tensor(L.BB[:, 2], L.BI[:, 1], f[1], ALU.mult))
            ln(dve.tensor_tensor(L.BB[:, 0], L.BB[:, 0], L.BB[:, 2], ALU.subtract))
            ln(dve.tensor_tensor(L.BB[:, 1], L.BI[:, 1], f[0], ALU.mult))
            ln(dve.tensor_tensor(L.BB[:, 2], L.BI[:, 0], f[1], ALU.mult))
            ln(dve.tensor_tensor(L.BB[:, 1], L.BB[:, 1], L.BB[:, 2], ALU.add))
            dve.wait_ge(zd.sem, zd.at(0))
            for part in range(2):
                for e in range(2):
                    r = slice(64 * e, 64 * e + 64)
                    ln(dve.tensor_copy(L.Z[r, part, :, 16 * e:16 * e + 16], L.BB[r, part]))
                dve.sem_inc(zd.sem, 1)
            for n, u in enumerate(us):
                C.full(dve, u)
                dve.tensor_copy(L.BL[:, n // 2, n % 2 * 4:n % 2 * 4 + 4, :].rearrange("p j c -> p (j c)"), C.bank[u.b][:])\
                    .then_inc(C.bank_read[u.b], 1)

        @block.tensor
        def _(pe):
            for n, u in enumerate(us):
                C.open(pe, u)
                pe.wait_ge(zd.sem, zd.at(1 + n // 2))
                for q in range(4):
                    a = n % 2 * 4 + q
                    t = pe.transpose(C.bank[u.b][:, q * P:(q + 1) * P],
                                     L.Z[:, n // 2, 4 * a:4 * a + 4, :].rearrange("p b c -> p (b c)"), C.ident[:])
                t.then_inc(C.bank_full[u.b], 1)


def stage_s5_scan(C, L):
    nc = C.nc
    K = C.s5
    NT, NS = 32, 4
    bu, yb, zt = [], [], []
    for j in range(NT):
        if j % 4 == 0:
            yb.append(C.take_given(j // 4 % 2))
        bu.append([C.take_given(2 + (2 * j + part) % 5) for part in range(2)])
        if j % 4 == 1:
            u = C.take_given(7)
            zt.append((u, C.take_blocks(KD, u)))
    sgn = lambda n, k=1: C.reserve(n, NT * k)
    tb = [C.reserve(f"table{b}", 16 * NT // 4) for b in range(4)]
    pre, add, post, fin, outp = sgn("pre", 4), sgn("padd", 2), sgn("post", 5), sgn("fin", 3), sgn("outp", 2)
    neg = C.reserve("negc", 1)
    with nc.Block(no_gpsimd_drain=True) as block:
        @block.sync
        def _(sp):
            C.load_slabs(sp)

        def rows(j):
            return slice(32 * (j % 4), 32 * (j % 4) + 32)

        @block.tensor
        def _(pe):
            def inputs(j):
                for part in range(2):
                    u = bu[j][part]
                    C.open(pe, u)
                    pe.matmul(C.bank[u.b][:], L.BL[rows(j), part, j // 4, :], C.MG[rows(j), j // 4, :], start=True,
                              stop=True)\
                        .then_inc(C.bank_full[u.b], 1)

            seen = set()
            for j in range(4):
                inputs(j)
            pe.wait_ge(neg.sem, neg.at(0))
            for j in range(NT):
                if j + 4 < NT:
                    inputs(j + 4)
                if j % 4 == 1:
                    C.gemm(pe, zt[j // 4], [C.H[:, k, :] for k in range(KD)], seen)
                u = yb[j // 4]
                if j % 4 == 0:
                    C.open(pe, u)
                pe.wait_ge(fin.sem, fin.at(3 * j + 2))
                pe.matmul(C.bank[u.b][rows(j), :], L.CP[:, 0, j, :], L.W[:, j % NS, 0], start=True, stop=False)\
                    .then_inc(outp.sem, 1)
                mm = pe.matmul(C.bank[u.b][rows(j), :], L.CP[:, 1, j, :], L.W[:, j % NS, 3], start=False, stop=True)
                mm.then_inc(outp.sem, 1)
                if j % 4 == 3:
                    pe.wait_ge(outp.sem, outp.at(2 * j + 1))
                    pe.sem_inc(C.bank_full[u.b], 1)

        @block.vector
        def _(dve):
            for j in range(NT + 3):
                if j < NT:
                    W, (cs, sn) = L.W[:, j % NS], (L.TB[:, j % 4, 0], L.TB[:, j % 4, 1])
                    dve.wait_ge(tb[j % 4].sem, tb[j % 4].base + 16 * (j // 4 + 1))
                    if j >= NS:
                        dve.wait_ge(outp.sem, outp.at(2 * (j - NS) + 1))
                    C.full(dve, bu[j][0])
                    C.full(dve, bu[j][1])
                    re, im = C.bank[bu[j][0].b], C.bank[bu[j][1].b]
                    dve.tensor_tensor(W[:, 0], cs, re[:], ALU.mult).then_inc(pre.sem, 1)
                    dve.tensor_tensor(W[:, 1], sn, im[:], ALU.mult).then_inc(pre.sem, 1)
                    dve.tensor_tensor(W[:, 2], cs, im[:], ALU.mult).then_inc(pre.sem, 1)
                    dve.tensor_tensor(W[:, 3], sn, re[:], ALU.mult).then_inc(pre.sem, 1)
                    dve.wait_ge(pre.sem, pre.at(4 * j + 3))
                    dve.sem_inc(C.bank_read[bu[j][0].b], 1)
                    dve.sem_inc(C.bank_read[bu[j][1].b], 1)
                if 0 < j <= NT:
                    i = j - 1
                    W, (cs, sn) = L.W[:, i % NS], (L.TB[:, i % 4, 0], L.TB[:, i % 4, 1])
                    mag = K.mag[:, i:i + 1].to_broadcast([P, T])
                    dve.wait_ge(add.sem, add.at(2 * i))
                    dve.tensor_tensor_scan(W[:, 1], mag, W[:, 0], 0.0, ALU.mult, ALU.add).then_inc(post.sem, 1)
                    dve.wait_ge(add.sem, add.at(2 * i + 1))
                    dve.tensor_tensor_scan(W[:, 3], mag, W[:, 2], 0.0, ALU.mult, ALU.add).then_inc(post.sem, 1)
                    dve.wait_ge(post.sem, post.at(5 * i + 1))
                    dve.tensor_tensor(W[:, 0], cs, W[:, 1], ALU.mult).then_inc(post.sem, 1)
                    dve.tensor_tensor(W[:, 2], sn, W[:, 3], ALU.mult).then_inc(post.sem, 1)
                    dve.wait_ge(post.sem, post.at(5 * i + 2))
                    dve.tensor_tensor(W[:, 1], W[:, 1], sn, ALU.mult).then_inc(post.sem, 1)
                if j > 2:
                    i = j - 3
                    if i % 4 == 3:
                        u = yb[i // 4]
                        C.full(dve, u)
                        m = C.MG[:, i // 4, :]
                        dve.scalar_tensor_tensor(out=m, in0=m, scalar=C.col("a_d", i // 4), in1=C.bank[u.b][:],
                                                 op0=ALU.mult, op1=ALU.add).then_inc(C.bank_read[u.b], 1)

        @block.gpsimd
        def _(pool):
            for j in range(NT + 2):
                if j < NT:
                    W = L.W[:, j % NS]
                    pool.wait_ge(pre.sem, pre.at(4 * j + 1))
                    pool.tensor_tensor(W[:, 0], W[:, 0], W[:, 1], ALU.add).then_inc(add.sem, 1)
                    pool.wait_ge(pre.sem, pre.at(4 * j + 3))
                    pool.tensor_tensor(W[:, 2], W[:, 2], W[:, 3], ALU.subtract).then_inc(add.sem, 1)
                if j > 1:
                    i = j - 2
                    W, cs = L.W[:, i % NS], L.TB[:, i % 4, 0]
                    pool.wait_ge(post.sem, post.at(5 * i + 4))
                    pool.tensor_tensor(W[:, 3], W[:, 3], cs, ALU.mult).then_inc(fin.sem, 1)
                    pool.tensor_tensor(W[:, 0], W[:, 0], W[:, 2], ALU.subtract).then_inc(fin.sem, 1)
                    pool.wait_ge(fin.sem, fin.at(3 * i))
                    pool.tensor_tensor(W[:, 3], W[:, 3], W[:, 1], ALU.add).then_inc(fin.sem, 1)

        @block.scalar
        def _(act):
            act.activation(L.CP[:, 1], L.CP[:, 1], ACT.Copy, scale=-1.0).then_inc(neg.sem, 1)
            for j in range(NT + 7):
                if j < NT:
                    if j >= 4:
                        act.wait_ge(fin.sem, fin.at(3 * (j - 4) + 2))
                    act.dma_start(L.TB[:, j % 4], C.io["rot"][j]).then_inc(tb[j % 4].sem, 16)
                if j % 4 == 1 and 5 <= j < NT + 5:
                    i = (j - 5) // 4
                    u = zt[i][0]
                    C.full(act, u)
                    act.activation(C.zbuf[:, i, :], C.bank[u.b][:], ACT.Copy).then_inc(C.bank_read[u.b], 1)
                if j % 4 == 3 and j >= 7:
                    i = (j - 7) // 4
                    C.read(act, yb[i])
                    act.activation(C.MG[:, i, :], C.MG[:, i, :], ACT.Gelu_apprx_tanh)


def branch_s5(C):
    KB, A = 1024, C.arena
    L = Layout()
    L.BL = C.at("s5_b", [P, 2, 8, P], A)
    L.CP = C.at("s5_c", [P, 2, 32, 32], A + 8 * KB)
    L.Z = C.at("s5_z", [P, 2, 32, 32], A + 16 * KB)
    L.BB = C.at("s5_bb", [P, 3, 32, 16], A + 24 * KB)
    L.BI = C.at("s5_bi", [P, 2, 32, 16], A + 32 * KB)
    L.W = C.at("s5_work", [P, 4, 4, T], A + 16 * KB)
    L.TB = C.at("s5_tables", [P, 4, 2, T], A + 48 * KB)
    C.zbuf = C.at("z", [P, KD, T], A + 64 * KB)
    stage_fetch(C, [(L.BI[:], C.io["s5_b"]), (L.CP[:], C.io["s5_c"])])
    stage_s5_b(C, L)
    hk = [C.H[:, k, :] for k in range(KD)]
    stage_gemm(C, KD, hk, copy_to(C.MG))
    stage_s5_scan(C, L)
    L = Layout()
    L.Y = C.at("s5_y", [P, KD, T], A)

    def glu(act, i, bank):
        return act.activation(L.Y[:, i, :], bank[:], ACT.Sigmoid, bias=C.col("b_glu", i))

    def glu_mul(dve, i):
        return dve.tensor_tensor(L.Y[:, i, :], L.Y[:, i, :], C.MG[:, i, :], ALU.mult)
    stage_gemm(C, KD, [C.MG[:, k, :] for k in range(KD)], glu, then=glu_mul)
    gated_output(C, L.Y, C.zbuf, 0)


def gated_output(C, Y, Z, layer):
    tiles = [C.take_tile(KD) for _ in range(KD)]
    act_done, gated = C.reserve("zsilu", KD), C.reserve("gated", KD)
    with C.nc.Block(no_gpsimd_drain=True) as block:
        @block.sync
        def _(sp):
            C.load_slabs(sp)

        @block.tensor
        def _(pe):
            seen = set()
            for i, t in enumerate(tiles):
                ready = (lambda k: pe.wait_ge(gated.sem, gated.at(k))) if i == 0 else None
                C.gemm(pe, t, [Y[:, k, :] for k in range(KD)], seen, ready=ready)

        @block.vector
        def _(dve):
            for k in range(KD):
                dve.wait_ge(act_done.sem, act_done.at(k))
                dve.tensor_tensor(Y[:, k, :], Y[:, k, :], Z[:, k, :], ALU.mult).then_inc(gated.sem, 1)

        @block.scalar
        def _(act):
            for k in range(KD):
                act.activation(Z[:, k, :], Z[:, k, :], ACT.Silu).then_inc(act_done.sem, 1)
            for i, (u, _) in enumerate(tiles):
                C.full(act, u)
                act.activation(Z[:, i, :], C.bank[u.b][:], ACT.Copy).then_inc(C.bank_read[u.b], 1)
    stage_norm(C, [[Z[:, k, :] for k in range(KD)]], lambda i: C.col("post_norm", KD * layer + i), lambda i: C.X[:, i, :],
               DM, post=True)


def pre_norm(C, layer):
    stage_norm(C, [[C.X[:, k, :] for k in range(KD)]], lambda i: C.col("pre_norm", KD * layer + i),
               lambda i: C.H[:, i, :], DM)


def stage_swa_bias(C, L):
    nc = C.nc
    u = C.take_bank()
    s = C.reserve("swab", 1 + 16 * 2)
    with nc.Block(no_gpsimd_drain=True) as block:
        @block.tensor
        def _(pe):
            C.open(pe, u)
            pe.matmul(C.bank[u.b][0:16, 0:384], L.RB[:], L.OH[:], start=True, stop=True).then_inc(C.bank_full[u.b], 1)

        @block.vector
        def _(dve):
            C.full(dve, u)
            dve.tensor_tensor(L.BV[:], C.bank[u.b][0:16, 0:384], L.NR[:], ALU.add).then_inc(C.bank_read[u.b], 1)

        @block.sync
        def _(sp):
            C.read(sp, u)
            scr = C.io["bias_rows"]
            sp.dma_start(scr, L.BV[:].unsqueeze(1).to_broadcast([16, P, 384])).then_inc(s.sem, 16)
            sp.wait_ge(s.sem, s.base + 16)
            skewed = bass.AP(tensor=scr.tensor, offset=127, ap=[[383, P], [P * 384, 16], [1, 256]])
            sp.dma_start(L.BT[:], skewed).then_inc(s.sem, 16)
            sp.wait_ge(s.sem, s.base + 32)
            sp.sem_inc(s.sem, 1)


def stage_swa(C, L):
    nc = C.nc
    NJ = 8
    sb, pb, ob, zb = [[C.take_bank() for _ in range(TC)]], [], [], []
    for j in range(NJ):
        if j + 1 < NJ:
            sb.append([C.take_bank() for _ in range(TC)])
        zb.append(C.take_tile(KD))
        pb.append([C.take_bank() for _ in range(TC)])
        ob.append(C.take_bank())
    mx, ex, pn = C.reserve("mx", NJ), C.reserve("ex", NJ), C.reserve("pn", NJ)
    zr = C.reserve("swaz", 1)
    with nc.Block(no_gpsimd_drain=True) as block:
        @block.sync
        def _(sp):
            C.load_slabs(sp)

        @block.tensor
        def _(pe):
            def scores(j):
                for b, u in enumerate(sb[j]):
                    e = b // 2
                    C.open(pe, u)
                    for n in (2 * (b % 2), 2 * (b % 2) + 1):
                        lo = 0 if n else P
                        r = slice(64 * e, 64 * e + 64)
                        mm = pe.matmul(C.bank[u.b][:, n % 2 * 256 + lo:n % 2 * 256 + 256], L.Q[r, j, n * P:(n + 1) * P],
                                       L.K[r, 0, (n - 1) * P + lo:(n + 1) * P], start=True, stop=True)
                    mm.then_inc(C.bank_full[u.b], 1)

            seen = set()
            scores(0)
            for j in range(NJ):
                if j + 1 < NJ:
                    scores(j + 1)
                C.gemm(pe, zb[j], [C.H[:, k, :] for k in range(KD)], seen)
                pe.wait_ge(pn.sem, pn.at(j))
                for n, u in enumerate(pb[j]):
                    C.open(pe, u)
                    for e in range(2):
                        for kt in range(0 if n else 1, 2):
                            a = (2 * e + kt) * P
                            mm = pe.transpose(C.bank[u.b][:, a:a + P], L.S[:, j % 2, n, e, kt * P:(kt + 1) * P], C.ident[:])
                    mm.then_inc(C.bank_full[u.b], 1)
                u = ob[j]
                C.open(pe, u)
                for n in range(TC):
                    C.read(pe, pb[j][n])
                    for e in range(2):
                        first = 0 if n else 1
                        for kt in range(first, 2):
                            a = (2 * e + kt) * P
                            mm = pe.matmul(C.bank[u.b][64 * e:64 * e + 64, n * P:(n + 1) * P],
                                           L.V[:, n - 1 + kt, 64 * e:64 * e + 64], L.PT[:, n, a:a + P],
                                           start=(kt == first), stop=(kt == 1))
                mm.then_inc(C.bank_full[u.b], 1)

        @block.vector
        def _(dve):
            ln = lambda ins: C.vchain.link(dve, ins)

            def logits(j):
                if j >= 2:
                    C.full(dve, pb[j - 2][3])
                st = L.ST[:, j % 2]
                for b, u in enumerate(sb[j]):
                    e = b // 2
                    C.full(dve, u)
                    for n in (2 * (b % 2), 2 * (b % 2) + 1):
                        lo = 0 if n else P
                        ins = dve.scalar_tensor_tensor(
                            out=L.S[:, j % 2, n, e, lo:256], in0=C.bank[u.b][:, n % 2 * 256 + lo:n % 2 * 256 + 256],
                            scalar=64 ** -0.5, in1=L.BT[:, j + 8 * e, lo:256], op0=ALU.mult, op1=ALU.add)
                    ins.then_inc(C.bank_read[u.b], 1)
                for u in sb[j]:
                    C.read(dve, u)
                ln(dve.tensor_reduce(st[:, 0, 0, :], L.S[:, j % 2, 0, :, P:256], AX.X, ALU.max))
                ln(dve.tensor_reduce(st[:, 0, 1:4, :], L.S[:, j % 2, 1:4], AX.X, ALU.max))
                sink = C.col("sinks", 0, 16)[:, j::8].unsqueeze(1).to_broadcast([P, TC, 2])
                ln(dve.tensor_tensor(st[:, 0], st[:, 0], sink, ALU.max))
                ln(dve.tensor_tensor(st[:, 1], sink, st[:, 0], ALU.subtract))
                dve.tensor_scalar(st[:, 0], st[:, 0], -1.0, None, ALU.mult).then_inc(mx.sem, 1)

            def probs(j):
                st = L.ST[:, j % 2]
                dve.wait_ge(ex.sem, ex.at(j))
                ln(dve.tensor_tensor(st[:, 2], st[:, 2], st[:, 1], ALU.add))
                ln(dve.reciprocal(st[:, 2], st[:, 2]))
                r = st[:, 2].rearrange("p n e -> p (n e)").unsqueeze(2).to_broadcast([P, 8, 256])
                s = L.S[:, j % 2].rearrange("p n e k -> p (n e) k")
                dve.tensor_tensor(s, s, r, ALU.mult).then_inc(pn.sem, 1)

            for b in range(2):
                ln(dve.memset(L.S[:, b, 0, :, 0:P], 0.0))
            dve.sem_inc(zr.sem, 1)
            logits(0)
            for j in range(NJ):
                if j + 1 < NJ:
                    logits(j + 1)
                probs(j)

        @block.scalar
        def _(act):
            def exps(j):
                st = L.ST[:, j % 2]
                act.wait_ge(mx.sem, mx.at(j))
                act.activation(st[:, 1], st[:, 1], ACT.Exp)
                for n in range(TC):
                    lo = 0 if n else P
                    for e in range(2):
                        s = L.S[:, j % 2, n, e, lo:256]
                        ins = act.activation(s, s, ACT.Exp, bias=st[:, 0, n, e:e + 1], accum_out=st[:, 2, n, e:e + 1])
                ins.then_inc(ex.sem, 1)

            exps(0)
            for j in range(NJ):
                if j + 1 < NJ:
                    exps(j + 1)
                C.full(act, zb[j][0])
                act.activation(L.Z[:, j, :], C.bank[zb[j][0].b][:], ACT.Copy).then_inc(C.bank_read[zb[j][0].b], 1)
                if j > 0:
                    C.full(act, ob[j - 1])
                    act.activation(L.Y[:, j - 1, :], C.bank[ob[j - 1].b][:], ACT.Copy).then_inc(C.bank_read[ob[j - 1].b], 1)
                for n, u in enumerate(pb[j]):
                    C.full(act, u)
                    lo = 0 if n else 1
                    v = lambda ap: ap.rearrange("p (e t k) -> p e t k", e=2, t=2)[:, :, lo:2, :]
                    act.activation(v(L.PT[:, n, :]), v(C.bank[u.b][:]), ACT.Copy).then_inc(C.bank_read[u.b], 1)
            C.full(act, ob[NJ - 1])
            act.activation(L.Y[:, NJ - 1, :], C.bank[ob[NJ - 1].b][:], ACT.Copy).then_inc(C.bank_read[ob[NJ - 1].b], 1)


def branch_swa(C):
    KB, A = 1024, C.arena
    L = Layout()
    L.Q = C.at("swa_q", [P, KD, T], A)
    L.Y = C.at("swa_y", [P, KD, T], A + 16 * KB)
    L.K = C.at("swa_k", [P, 1, T], A + 32 * KB)
    L.V = C.at("swa_v", [P, TC, P], A + 34 * KB)
    L.BT = C.at("swa_bias", [P, 16, 256], A + 36 * KB)
    L.S = C.at("swa_s", [P, 2, TC, 2, 256], A + 52 * KB)
    L.PT = C.at("swa_pt", [P, TC, T], A + 68 * KB)
    L.Z = C.at("swa_z", [P, KD, T], A + 76 * KB)
    L.ST = C.at("swa_st", [P, 2, 3, TC, 2], A + 92 * KB)
    L.RB = C.at("rel_bias", [32, 16], A + 93 * KB)
    L.OH = C.at("bucket_onehot", [32, 384], A + 94 * KB)
    L.NR = C.at("neg_row", [16, 384], A + 96 * KB)
    L.BV = C.at("bias_row", [16, 384], A + 98 * KB)
    stage_fetch(C, [(L.RB[:], C.io["rel_bias"]), (L.OH[:], C.io["bucket_onehot"]), (L.NR[:], C.io["neg_row"])])
    stage_swa_bias(C, L)
    hk = [C.H[:, k, :] for k in range(KD)]
    stage_gemm(C, KD, hk, copy_to(L.Q))
    stage_gemm(C, 1, hk, copy_to(L.K))
    stage_tokmajor(C, 1, hk, lambda half, t: L.V[:, t, :], TC)
    stage_swa(C, L)
    gated_output(C, L.Y, L.Z, 1)


def stage_mla(C, L):
    nc = C.nc
    H = 16
    SC = 96 ** -0.5
    kb, sb, pb, ob, zb = [], [], [], [], []

    def take_scores(h):
        if h % 2 == 0:
            kb.append(C.take_tile(2))
        sb.append([C.take_bank() for _ in range(TC)])
        if h % 2 == 0:
            zb.append(C.take_tile(KD))

    C.pinned = (7,)
    take_scores(0)
    for h in range(H):
        if h + 1 < H:
            take_scores(h + 1)
        pb.append([C.take_bank() for _ in range(TC)])
        if h % 2 == 0:
            ob.append(C.take_given(7))
    C.pinned = ()
    mx, ex, pn = C.reserve("mx", H), C.reserve("ex", H), C.reserve("pn", H)
    kt_, pvd, scd = C.reserve("ktile", 2 * 8 + 4), C.reserve("pvd", H), C.reserve("scd", H)
    K0 = 4
    with nc.Block(no_gpsimd_drain=True) as block:
        @block.sync
        def _(sp):
            C.load_slabs(sp)

        @block.tensor
        def _(pe):
            seen = set()

            def scores(h):
                if h % 2 == 0:
                    C.gemm(pe, kb[h // 2], [C.MG[:, 6, :], C.MG[:, 7, :]], seen)
                pe.wait_ge(kt_.sem, kt_.at(K0 + h))
                for i, u in enumerate(sb[h]):
                    C.open(pe, u)
                    mm = pe.matmul(C.bank[u.b][:, 0:(i + 1) * P], L.Q[:, h, i * P:(i + 1) * P], L.K[:, h % 4, 0:(i + 1) * P],
                                   start=True, stop=True)
                    mm.then_inc(C.bank_full[u.b], 1)
                if h % 2 == 0:
                    C.gemm(pe, zb[h // 2], [C.H[:, k, :] for k in range(KD)], seen)

            scores(0)
            for h in range(H):
                if h + 1 < H:
                    scores(h + 1)
                pe.wait_ge(pn.sem, pn.at(h))
                for kt, u in enumerate(pb[h]):
                    C.open(pe, u)
                    for i in range(kt, TC):
                        mm = pe.transpose(C.bank[u.b][:, i * P:(i + 1) * P], L.S[:, h % 2, i, kt * P:(kt + 1) * P], C.ident[:])
                    mm.then_inc(C.bank_full[u.b], 1)
                u = ob[h // 2]
                if h % 2 == 0:
                    C.open(pe, u)
                e = h % 2
                for kt in range(TC):
                    C.read(pe, pb[h][kt])
                    mm = pe.matmul(C.bank[u.b][64 * e:64 * e + 64, kt * P:T], L.V[:, kt, 64 * h:64 * h + 64],
                                   L.PT[:, kt, kt * P:T], start=(kt == 0), stop=(kt == TC - 1))
                mm.then_inc(pvd.sem, 1)
                if e:
                    pe.wait_ge(pvd.sem, pvd.at(h))
                    pe.sem_inc(C.bank_full[u.b], 1)

        @block.vector
        def _(dve):
            ln = lambda ins: C.vchain.link(dve, ins)

            def logits(h):
                if h >= 2:
                    C.full(dve, pb[h - 2][3])
                st = L.ST[:, h % 2]
                for i, u in enumerate(sb[h]):
                    C.full(dve, u)
                    w = (i + 1) * P
                    dve.scalar_tensor_tensor(out=L.S[:, h % 2, i, 0:w], in0=C.bank[u.b][:, 0:w], scalar=SC,
                                             in1=L.MB[:, T - w:T], op0=ALU.mult, op1=ALU.add).then_inc(C.bank_read[u.b], 1)
                for i, u in enumerate(sb[h]):
                    C.read(dve, u)
                    ln(dve.tensor_reduce(st[:, 0, i:i + 1], L.S[:, h % 2, i, 0:(i + 1) * P], AX.X, ALU.max))
                dve.tensor_scalar(st[:, 0], st[:, 0], -1.0, None, ALU.mult).then_inc(mx.sem, 1)

            def probs(h):
                st = L.ST[:, h % 2]
                dve.wait_ge(ex.sem, ex.at(h))
                ln(dve.reciprocal(st[:, 1], st[:, 1]))
                for i in range(TC):
                    s = L.S[:, h % 2, i, 0:(i + 1) * P]
                    ins = dve.tensor_scalar(s, s, st[:, 1, i:i + 1], None, ALU.mult)
                ins.then_inc(pn.sem, 1)

            logits(0)
            for h in range(H):
                if h + 1 < H:
                    logits(h + 1)
                probs(h)
                for kt in (1, 3):
                    u = pb[h][kt]
                    C.full(dve, u)
                    dve.tensor_copy(L.PT[:, kt, kt * P:T], C.bank[u.b][:, kt * P:T]).then_inc(C.bank_read[u.b], 1)

        @block.gpsimd
        def _(pool):
            for b in range(4):
                r = slice(64, P) if b % 2 == 0 else slice(0, 64)
                pool.tensor_copy(L.K[r, b, :], L.KR[r, :]).then_inc(kt_.sem, 1)

        @block.scalar
        def _(act):
            def keys(h):
                u = kb[h // 2][0]
                C.full(act, u)
                if h == 0:
                    act.wait_ge(kt_.sem, kt_.at(3))
                if h >= 4:
                    C.full(act, sb[h - 3][3])
                for e in range(2):
                    r = slice(64 * e, 64 * e + 64)
                    act.activation(L.K[r, (h + e) % 4, :], C.bank[u.b][r, :], ACT.Copy).then_inc(kt_.sem, 1)
                act.wait_ge(kt_.sem, kt_.at(K0 + h + 1))
                act.sem_inc(C.bank_read[u.b], 1)

            def exps(h):
                st = L.ST[:, h % 2]
                act.wait_ge(mx.sem, mx.at(h))
                for i in range(TC):
                    s = L.S[:, h % 2, i, 0:(i + 1) * P]
                    ins = act.activation(s, s, ACT.Exp, bias=st[:, 0, i:i + 1], accum_out=st[:, 1, i:i + 1])
                ins.then_inc(ex.sem, 1)
                if h % 2 == 0:
                    u = zb[h // 2][0]
                    C.full(act, u)
                    act.activation(L.Z[:, h // 2, :], C.bank[u.b][:], ACT.Copy).then_inc(C.bank_read[u.b], 1)

            keys(0)
            exps(0)
            for h in range(H):
                if h + 1 < H:
                    if (h + 1) % 2 == 0:
                        keys(h + 1)
                    exps(h + 1)
                if h > 0:
                    act.wait_ge(pvd.sem, pvd.at(h - 1))
                if h > 0 and h % 2 == 0:
                    u = ob[h // 2 - 1]
                    C.full(act, u)
                    act.activation(L.Y[:, h // 2 - 1, :], C.bank[u.b][:], ACT.Copy).then_inc(C.bank_read[u.b], 1)
                for kt in (0, 2):
                    u = pb[h][kt]
                    C.full(act, u)
                    act.activation(L.PT[:, kt, kt * P:T], C.bank[u.b][:, kt * P:T], ACT.Copy).then_inc(C.bank_read[u.b], 1)
            u = ob[7]
            C.full(act, u)
            act.activation(L.Y[:, 7, :], C.bank[u.b][:], ACT.Copy).then_inc(C.bank_read[u.b], 1)


def branch_mla(C):
    KB, A = 1024, C.arena
    L = Layout()
    L.Q = C.at("mla_q", [P, 16, T], A)
    L.V = C.at("mla_v", [P, TC, DM], A + 32 * KB)
    L.K = C.at("mla_k", [P, 4, T], A + 48 * KB)
    L.KR = C.at("mla_kr", [P, T], A + 56 * KB)
    L.RT = C.at("rope_tables", [P, 4, T], A + 58 * KB)
    L.MB = C.at("causal_bias", [P, T], A + 66 * KB)
    L.S = C.at("mla_s", [P, 2, TC, T], A + 68 * KB)
    L.PT = C.at("mla_pt", [P, TC, T], A + 58 * KB)
    L.ST = C.at("mla_st", [P, 2, 2, TC], A + 100 * KB)
    L.T = C.at("mla_t", [P, T], A + 84 * KB)
    stage_fetch(C, [(L.RT[:], C.io["rope"]), (L.MB[:], C.io["causal"])])
    hk = [C.H[:, k, :] for k in range(KD)]
    stage_gemm(C, 8, hk, copy_to(C.MG))
    stage_norm(C, [[C.MG[:, k, :] for k in range(6)]], lambda i: C.col("q_norm", i), lambda i: C.MG[:, i, :], 768)
    stage_norm(C, [[C.MG[:, k, :] for k in (6, 7)]], lambda i: C.col("kv_norm", i), lambda i: C.MG[:, 6 + i, :], 256)

    def rotate_key(dve, i, bank):
        if i == 0:
            return dve.tensor_tensor(L.KR[:], bank[:], L.RT[:, 2], ALU.mult)
        C.vchain.link(dve, dve.tensor_tensor(L.T[:], bank[:], L.RT[:, 3], ALU.mult))
        return dve.tensor_tensor(L.KR[:], L.KR[:], L.T[:], ALU.add)

    def rotate_query(dve, h, bank):
        return dve.tensor_tensor(L.Q[:, h, :], bank[:], L.RT[:, h % 2], ALU.mult)
    stage_gemm(C, 2, hk, rotate_key, "vector")
    stage_gemm(C, 16, [C.MG[:, k, :] for k in range(6)], rotate_query, "vector")
    stage_tokmajor(C, 4, [C.MG[:, 6, :], C.MG[:, 7, :]], lambda half, t: L.V[:, t, half * 512:half * 512 + 512], TC)
    L.Y = L.Q
    L.Z = C.at("mla_z", [P, KD, T], A + 84 * KB)
    stage_mla(C, L)
    gated_output(C, L.Y, L.Z, 2)


def stage_sgu(C, L):
    nc = C.nc
    banks = [C.take_bank() for _ in range(KD)]
    vn = C.reserve("vn", TC)
    sq = C.reserve("lnsq", 2)
    wm = C.reserve("wm", 1)
    with nc.Block(no_gpsimd_drain=True) as block:
        @block.sync
        def _(sp):
            C.load_slabs(sp)

        @block.scalar
        def _(act):
            act.wait_ge(sq.sem, sq.at(0))
            act.activation(L.MV[:, :, 1:2], L.MV[:, :, 1:2], ACT.Sqrt, bias=C.eps[:]).then_inc(sq.sem, 1)

        @block.vector
        def _(dve):
            ln = lambda ins: C.vchain.link(dve, ins)
            for t in range(TC):
                for half in range(2):
                    ln(dve.bn_stats(L.BN[:, t, half], L.V[:, t, half * 512:half * 512 + 512]))
                ln(dve.bn_aggr(L.MV[:, t, :], L.BN[:, t]))
            dve.sem_inc(sq.sem, 1)
            dve.wait_ge(sq.sem, sq.at(1))
            ln(dve.reciprocal(L.MV[:, :, 1:2], L.MV[:, :, 1:2]))
            ln(dve.tensor_tensor(L.W[:], L.W[:], C.mask[:].unsqueeze(1).to_broadcast([P, 16, P]), ALU.mult))
            dve.sem_inc(wm.sem, 1)
            for t in range(TC):
                v = L.V[:, t, :]
                ln(dve.tensor_scalar(v, v, L.MV[:, t, 0:1], L.MV[:, t, 1:2], ALU.subtract, ALU.mult))
                ln(dve.tensor_tensor(v, v, L.LG[:, 0, :], ALU.mult))
                dve.tensor_tensor(v, v, L.LG[:, 1, :], ALU.add).then_inc(vn.sem, 1)
            for j, u in enumerate(banks):
                C.full(dve, u)
                v = lambda ap: ap.rearrange("p (n t) -> p n t", n=TC)
                b = L.BS[:, j, :].unsqueeze(1).to_broadcast([P, TC, P])
                s = C.sq[:, j % 4, :]
                ln(dve.tensor_tensor(v(s), v(C.bank[u.b][:]), b, ALU.add))
                dve.tensor_tensor(L.U[:, j, :], L.U[:, j, :], s, ALU.mult).then_inc(C.bank_read[u.b], 1)

        @block.tensor
        def _(pe):
            pe.wait_ge(wm.sem, wm.at(0))
            for j, u in enumerate(banks):
                C.open(pe, u)
                for n in range(TC):
                    if j == 0:
                        pe.wait_ge(vn.sem, vn.at(n))
                    for e in range(2):
                        g = 2 * j + e
                        mm = pe.matmul(C.bank[u.b][64 * e:64 * e + 64, n * P:(n + 1) * P], L.V[:, n, g * 64:g * 64 + 64],
                                       L.W[:, g, :], start=True, stop=True)
                mm.then_inc(C.bank_full[u.b], 1)


def branch_sgu(C):
    KB, A = 1024, C.arena
    L = Layout()
    L.U = C.at("sgu_u", [P, KD, T], A)
    L.V = C.at("sgu_v", [P, TC, DM], A + 16 * KB)
    L.Z = C.at("sgu_z", [P, KD, T], A + 32 * KB)
    L.W = C.at("sgu_w", [P, 16, P], A + 48 * KB)
    L.BS = C.at("sgu_bs", [P, KD, P], A + 56 * KB)
    L.LG = C.at("sgu_ln", [P, 2, DM], A + 60 * KB)
    L.BN = C.at("sgu_bn", [P, TC, 2, 6], A + 68 * KB)
    L.MV = C.at("sgu_mv", [P, TC, 2], A + 69 * KB)
    stage_fetch(C, [(L.W[:], C.io["sgu_w"]), (L.BS[:], C.io["sgu_bs"]), (L.LG[:], C.io["sgu_ln"])])
    hk = [C.H[:, k, :] for k in range(KD)]
    stage_tokmajor(C, 4, hk, lambda half, t: L.V[:, t, half * 512:half * 512 + 512], TC, ACT.Gelu_apprx_tanh)
    stage_gemm(C, KD, hk, copy_to(L.U, ACT.Gelu_apprx_tanh))
    stage_sgu(C, L)
    stage_gemm(C, KD, hk, copy_to(L.Z))
    gated_output(C, L.U, L.Z, 3)


def second_block(C, upto):
    for layer, branch in enumerate((branch_s5, branch_swa, branch_mla, branch_sgu)):
        if upto >= layer + 2:
            pre_norm(C, layer)
            branch(C)


def stage_store(C):
    st = C.reserve("stored", 16)
    with C.nc.Block(no_gpsimd_drain=True) as block:
        @block.sync
        def _(sp):
            sp.dma_start(C.io["yT"], C.X[:]).then_inc(st.sem, 16)
            sp.wait_ge(st.sem, st.base + 16)


def build(nc, io, upto=99):
    io["rot"] = nc.dram_tensor("rotation_tables", [32, P, 2, T], F32, kind="Internal").ap()
    io["bias_rows"] = nc.dram_tensor("bias_rows", [16, P, 384], F32, kind="Internal").ap()
    C = Core(nc, io)
    C.X = C.fixed("x", [P, KD, T])
    C.H = C.fixed("h", [P, KD, T])
    C.ring = C.fixed("ring", [P, RING, SLAB * P])
    C.MG_OFF = C.off
    C.MG = C.fixed("merged", [P, KD, T])
    C.sq = C.fixed("sq", [P, 4, T])
    C.ROOT_OFF = C.off
    C.root = C.fixed("root", [P, 4, T])
    C.cols = C.fixed("cols", [P, NCOL])
    C.ones = C.fixed("ones", [P, P])
    C.ident = C.fixed("ident", [P, P])
    C.mask = C.fixed("mask", [P, P])
    C.eps = C.fixed("eps", [P, 8])[:, 0:1]
    C.st = C.fixed("st", [P, 4, 8])
    C.s5 = Layout()
    C.s5.cos, C.s5.sin, C.s5.mag, C.s5.fre, C.s5.fim = [C.fixed(f"s5_{n}", [P, 32]) for n in ("cos", "sin", "mag", "fre", "fim")]
    C.s5.tmp = C.fixed("s5_tmp", [P, 4, 32])
    C.s5.pw = C.fixed("s5_pw", [P, 5, 8])
    C.arena = (C.off + 63) // 64 * 64
    C.ARENA_END = 229344
    stage_load(C)
    stage_s5_coefficients(C)
    first_block(C)
    if upto > 1:
        second_block(C, upto)
    stage_store(C)


def pack_slabs(w):
    out = []
    for blocks in weight_sections().values():
        for name, rows, cols in blocks:
            out.append((name, rows, cols))
    n = -(-len(out) // SLAB)
    slabs = np.zeros((n, P, SLAB * P), np.float32)
    for b, (name, rows, cols) in enumerate(out):
        s, i = divmod(b, SLAB)
        dst = slabs[s, :, i * P:(i + 1) * P]
        if name in ("lru_w_a", "lru_w_x"):
            for blk in range(LRU_W // LRU_B):
                lo, hi = blk * LRU_B, (blk + 1) * LRU_B
                r0, r1 = max(lo, rows[0]), min(hi, rows[-1] + 1)
                c0, c1 = max(lo, cols[0]), min(hi, cols[-1] + 1)
                if r0 < r1 and c0 < c1:
                    dst[r0 - rows[0]:r1 - rows[0], c0 - cols[0]:c1 - cols[0]] = w[name][blk, r0 - lo:r1 - lo, c0 - lo:c1 - lo]
            continue
        m = w[name]
        if np.all(cols >= 0):
            dst[:, :] = m[rows[:, None], cols[None, :]]
        else:
            ok = cols >= 0
            dst[:, ok] = m[rows[:, None], cols[ok][None, :]]
    return slabs


def pack_cols(v):
    out = np.zeros((P, NCOL), np.float32)
    for name, k in COLS:
        a = v[name]
        out[:a.shape[0], COL_AT[name]:COL_AT[name] + k] = a
    return out


def channels(a):
    a = np.asarray(a).reshape(-1)
    return np.ascontiguousarray(a.reshape(-1, P).T)


def shape_tables():
    j = np.arange(384)
    dist = 255 - j
    d = np.maximum(dist, 1).astype(np.float32)
    large = 16 + (np.log(d / 16) / np.float32(np.log(8.0)) * 16).astype(np.int32)
    bucket = np.where(dist < 16, dist, np.minimum(large, 31))
    valid = (dist >= 0) & (dist < 128)
    onehot = ((np.arange(32)[:, None] == bucket[None]) & valid[None]).astype(np.float32)
    neg = np.repeat(np.where(valid, 0.0, NEG).astype(np.float32)[None], 16, 0)
    inv = (np.float32(10000.0) ** (-np.arange(0, 32, 2, dtype=np.float32) / 32)).astype(np.float32)
    ang = inv[:, None] * np.arange(T, dtype=np.float32)[None]
    c, s = np.cos(ang), np.sin(ang)
    cos, sin, one = np.concatenate([c, c]), np.concatenate([-s, s]), np.ones((64, T), np.float32)
    rope = np.stack([np.concatenate([one, cos, sin]), np.concatenate([cos, sin, one]), np.tile(cos, (4, 1)),
                     np.tile(sin, (4, 1))], 1).astype(np.float32)
    causal = np.zeros((P, T), np.float32)
    causal[:, T - P:] = np.where(np.arange(P)[None] <= np.arange(P)[:, None], 0.0, NEG)
    return {"bucket_onehot": onehot, "neg_row": neg, "rope": rope, "causal": causal}


def pack_s5_c(c):
    out = np.zeros((P, 32, 32), np.float32)
    for g in range(64):
        j, e = divmod(g, 2)
        out[64 * e:64 * e + 64, j, 16 * e:16 * e + 16] = c[g].T
    return out


def host_arrays(i):
    i = {k: np.asarray(v) for k, v in i.items()}
    w = {"w_in": i["w_in"][0], "w_br_ssd": i["w_br_ssd"][0], "w_br_lru": i["w_br_lru"][0], "w_br_mem": i["w_br_mem"][0],
         "w_out": i["w_out"][0], "w_kv": i["w_kv"][0], "lru_w_a": i["lru_w_a"][0], "lru_w_x": i["lru_w_x"][0],
         "a_w_in": i["a_w_in_2"][0], "a_w_glu": i["a_w_glu_2"][0], "a_w_out": i["a_w_out_2"][0],
         "b_w_in": i["b_w_in_2"][0], "b_w_out": i["b_w_out_2"][0], "c_w_in": i["c_w_in_2"][0], "c_w_uq": i["c_w_uq_2"][0],
         "c_w_ukv": i["c_w_ukv_2"][0], "c_w_out": i["c_w_out_2"][0], "d_w_in": i["d_w_in_2"][0], "d_w_out": i["d_w_out_2"][0]}
    dup = lambda a: np.repeat(a.reshape(-1), 64)
    v = {"norm_g": channels(i["norm_g"]), "conv_w": channels(i["ssd_conv_w"]), "conv_b": channels(i["ssd_conv_b"]),
         "ssd_d": channels(dup(i["ssd_d"])), "ssd_norm_g": channels(i["ssd_norm_g"]),
         "dt_bias": i["ssd_dt_bias"].reshape(32, 1), "a_log": i["ssd_a_log"].reshape(32, 1),
         "lru_conv_w": channels(i["lru_conv_w"]), "lru_conv_b": channels(i["lru_conv_b"]),
         "b_a": channels(i["lru_b_a"]), "b_x": channels(i["lru_b_x"]), "lam": channels(i["lru_lambda"]),
         "mem_norm_g": channels(i["mem_norm_g"]), "final_g": channels(i["final_g"]),
         "pre_norm": channels(i["pre_norm_2"]), "post_norm": channels(i["post_norm_2"]), "a_d": channels(i["a_d_2"]),
         "b_glu": channels(i["a_b_glu_2"]), "lam_re": channels(i["a_lam_re_2"]), "lam_im": channels(i["a_lam_im_2"]),
         "log_dt": channels(dup(i["a_log_dt_2"])), "q_norm": channels(i["c_q_norm_2"]), "kv_norm": channels(i["c_kv_norm_2"]),
         "sinks": np.repeat(i["b_sinks_2"].reshape(1, 16), P, 0)}
    return {"xT": np.ascontiguousarray(i["x"][0].T.reshape(KD, P, T).transpose(1, 0, 2)),
            "memT": np.ascontiguousarray(i["mem"][0].T.reshape(KD, P, MEM).transpose(1, 0, 2)),
            "s5_b": np.stack([i[n][0].reshape(32, P, 16).transpose(1, 0, 2) for n in ("a_b_re_2", "a_b_im_2")], 1),
            "s5_c": np.stack([pack_s5_c(i[n][0]) for n in ("a_c_re_2", "a_c_im_2")], 1),
            "rel_bias": i["rel_bias_2"],
            "sgu_w": np.ascontiguousarray(i["d_w_s_2"][0].transpose(2, 0, 1)),
            "sgu_bs": np.ascontiguousarray(np.repeat(i["d_b_s_2"][0].reshape(8, 2, 1, P), 64, 2).reshape(8, P, P).transpose(1, 0, 2)),
            "sgu_ln": np.ascontiguousarray(np.repeat(np.stack([i["d_ln_g_2"][0], i["d_ln_b_2"][0]])[None], P, 0)),
            **shape_tables(), "slabs": pack_slabs(w), "cols": pack_cols(v)}


def kernel(**inputs):
    import concourse.bacc as bacc
    from concourse.bass_utils import run_bass_kernel_spmd

    nc = bacc.Bacc("TRN2", target_bir_lowering=False, num_devices=1)
    arrays = host_arrays(inputs)
    io = {k: nc.dram_tensor(k, a.shape, F32, kind="ExternalInput").ap() for k, a in arrays.items()}
    io["yT"] = nc.dram_tensor("yT", [P, KD, T], F32, kind="ExternalOutput").ap()
    build(nc, io)
    r = run_bass_kernel_spmd(nc, [arrays], core_ids=[0])
    y = r.results[0]["yT"]
    return np.ascontiguousarray(y.transpose(1, 0, 2).reshape(DM, T).T).reshape(1, T, DM)
```

```python
from contextlib import ExitStack

import numpy as np

import concourse.bass as bass
from concourse import mybir

F32 = mybir.dt.float32
F32R = mybir.dt.float32r
I32 = mybir.dt.int32
ALU = mybir.AluOpType
ACT = mybir.ActivationFunctionType
AX = mybir.AxisListType

P = 128
T = 512
TC = T // P
DM = 1024
KD = DM // P
EPS = 1e-6
SSD_W, SSD_H, SSD_G, SSD_P = 2048, 32, 4, 64
KS = SSD_W // P
LRU_W, LRU_B = 1536, 96
KL = LRU_W // P
MEM = 256
C_Z = 0
C_XBC = SSD_W
C_DT = C_XBC + SSD_W + 2 * SSD_G * P
C_LG = C_DT + SSD_H
C_LX = C_LG + LRU_W
C_Q = C_LX + LRU_W
C_GATE = C_Q + DM
NEG = -1e30

SLAB = 16
RING = 3
AHEAD = 2
PLAIN = ("lru_gates_lru_w_a", "lru_gates_lru_w_x")


def span(a, n=P):
    return np.arange(a, a + n)


def weight_sections():
    sec = {}

    def add(name, blocks):
        sec.setdefault(name, []).extend(blocks)

    def tile(w, nk, cols):
        return [(w, span(k * P), cols) for k in range(nk)]

    add("dt", tile("w_in", KD, np.r_[span(C_DT, SSD_H), np.full(P - SSD_H, -1)]))
    for m in range(24):
        add("xbc", tile("w_in", KD, span(C_XBC + m * P)))
    for m in range(KS):
        add("z", tile("w_in", KD, span(C_Z + m * P)))
    for m in range(KD):
        add("gates0", tile("w_in", KD, span(C_GATE + m * P)))
    for m in range(KD):
        add("merge0", tile("w_br_ssd", KS, span(m * P)))
    for m in range(KL):
        add("lru_x", tile("w_in", KD, span(C_LX + m * P)))
    for w in ("lru_w_a", "lru_w_x"):
        for m in range(KL):
            for k in lru_inputs(m):
                add("lru_gates_" + w, [(w, span(k * P), span(m * P))])
    for m in range(KL):
        add("lru_g", tile("w_in", KD, span(C_LG + m * P)))
    for m in range(KD):
        add("gates1", tile("w_in", KD, span(C_GATE + DM + m * P)))
    for m in range(KD):
        add("merge1", tile("w_br_lru", KL, span(m * P)))
    for m in range(KD):
        add("q", tile("w_in", KD, span(C_Q + m * P)))
    for m in range(KD):
        add("mem_k", tile("w_kv", KD, span(m * P)))
    for half in range(2):
        for k in range(KD):
            for j in range(4):
                add("mem_v", [("w_kv", span(k * P), span(DM + half * 512 + j * P))])
    for m in range(KD):
        add("merge2", tile("w_in", KD, span(C_GATE + 2 * DM + m * P)))
        add("merge2", tile("w_br_mem", KD, span(m * P)))
    for m in range(KD):
        add("out", tile("w_out", KD, span(m * P)))
    more_sections(add, tile)
    return sec


def lru_inputs(m):
    first = (m * P) // LRU_B * LRU_B
    last = ((m * P + P - 1) // LRU_B + 1) * LRU_B
    return range(first // P, (last - 1) // P + 1)


def swa_heads(j):
    return np.r_[span(j * 64, 64), span((j + 8) * 64, 64)]


def more_sections(add, tile):
    for m in range(KD):
        add("s5_u", tile("a_w_in", KD, span(m * P)))
    for m in range(KD):
        add("s5_z", tile("a_w_in", KD, span(DM + m * P)))
    for m in range(KD):
        add("s5_glu", tile("a_w_glu", KD, span(m * P)))
    for m in range(KD):
        add("s5_out", tile("a_w_out", KD, span(m * P)))
    for m in range(KD):
        add("swa_q", tile("b_w_in", KD, swa_heads(m)))
    add("swa_k", tile("b_w_in", KD, span(DM)))
    add("swa_v", tile("b_w_in", KD, span(DM + P)))
    for m in range(KD):
        add("swa_z", tile("b_w_in", KD, DM + 2 * P + swa_heads(m)))
    for m in range(KD):
        add("swa_out", [("b_w_out", swa_heads(k), span(m * P)) for k in range(KD)])
    for m in range(8):
        add("mla_c", tile("c_w_in", KD, span(m * P)))
    swap = np.r_[span(16, 16), span(0, 16)]
    add("mla_kr", tile("c_w_in", KD, np.tile(1024 + span(0, 32), 4)))
    add("mla_kr", tile("c_w_in", KD, np.tile(1024 + swap, 4)))
    for h in range(16):
        nope, rope, swapped = 96 * h + span(0, 64), 96 * h + 64 + span(0, 32), 96 * h + 64 + swap
        cols = np.r_[nope, rope, swapped] if h % 2 == 0 else np.r_[rope, swapped, nope]
        add("mla_q", [("c_w_uq", span(k * P), cols) for k in range(6)])
    for half in range(2):
        for k in range(2):
            for j in range(4):
                h = 8 * half + 2 * j
                add("mla_v", [("c_w_ukv", span(k * P), np.r_[128 * h + 64 + span(0, 64), 128 * h + 192 + span(0, 64)])])
    for j in range(9):
        if j < 8:
            cols = np.r_[256 * j + span(0, 64), 256 * j + 128 + span(0, 64)]
            add("mla_kz", [("c_w_ukv", span(k * P), cols) for k in range(2)])
        if j > 0:
            add("mla_kz", tile("c_w_in", KD, span(1056 + (j - 1) * P)))
    for m in range(KD):
        add("mla_out", tile("c_w_out", KD, span(m * P)))
    for m in range(KD):
        add("sgu_u", tile("d_w_in", KD, span(m * P)))
    for half in range(2):
        for k in range(KD):
            for j in range(4):
                add("sgu_v", [("d_w_in", span(k * P), span(DM + half * 512 + j * P))])
    for m in range(KD):
        add("sgu_z", tile("d_w_in", KD, span(2 * DM + m * P)))
    for m in range(KD):
        add("sgu_out", tile("d_w_out", KD, span(m * P)))


def weight_stream():
    out, plain = [], []
    kind = False
    for name, blocks in weight_sections().items():
        if (name in PLAIN) != kind:
            out += [None] * (-len(out) % SLAB)
            kind = name in PLAIN
        out += blocks
        plain += [kind] * (-(-len(out) // SLAB) - len(plain))
    return out, plain


COLS = [("norm_g", 8), ("conv_w", 96), ("conv_b", 24), ("ssd_d", 16), ("ssd_norm_g", 16), ("dt_bias", 1), ("a_log", 1),
        ("lru_conv_w", 48), ("lru_conv_b", 12), ("b_a", 12), ("b_x", 12), ("lam", 12), ("mem_norm_g", 8), ("final_g", 8),
        ("pre_norm", 32), ("post_norm", 32), ("a_d", 8), ("b_glu", 8), ("lam_re", 32), ("lam_im", 32), ("log_dt", 32),
        ("q_norm", 6), ("kv_norm", 2), ("sinks", 16)]
COL_AT = {}
_n = 0
for _name, _k in COLS:
    COL_AT[_name] = _n
    _n += _k
NCOL = _n


class Span:

    def __init__(self, sem, base):
        self.sem, self.base = sem, base

    def at(self, i):
        return self.base + i + 1


class Counter:

    def __init__(self, nc, name):
        self.sem, self.total = nc.alloc_semaphore(name), 0

    def take(self, n):
        s = Span(self.sem, self.total)
        self.total += n
        return s


class Chain:

    def __init__(self, nc, name):
        self.sem, self.n = nc.alloc_semaphore(name), 0

    def link(self, eng, ins):
        self.n += 1
        ins.then_inc(self.sem, 1)
        eng.wait_ge(self.sem, self.n)


    def together(self, eng, ops):
        for ins in ops:
            self.n += 1
            ins.then_inc(self.sem, 1)
        eng.wait_ge(self.sem, self.n)


class Use:

    def __init__(self, b, n):
        self.b, self.n = b, n


class SlabSpent:

    def __init__(self, n):
        self.n = n


class Pair:

    def __init__(self, high, low):
        self.high, self.low = high, low

    def tile(self, k):
        return self.high[:, k, :], self.low[:, k, :]

    def tiles(self, n):
        return [self.tile(k) for k in range(n)]


class Core:

    def __init__(self, nc, io):
        self.nc, self.io = nc, io
        self.off = 16512
        self.names = 0
        self.bank = [nc.alloc_psum_tensor(f"bank{b}", [P, 512], F32) for b in range(8)]
        self.bank_full = [nc.alloc_semaphore(f"bank_full{b}") for b in range(8)]
        self.bank_read = [nc.alloc_semaphore(f"bank_read{b}") for b in range(8)]
        self.bank_uses = [0] * 8
        self.next_bank = 0
        self.pinned = ()
        self.slab_loaded = [nc.alloc_semaphore(f"slab_loaded{s}") for s in range(RING)]
        self.vchain, self.achain, self.gchain = Chain(nc, "vchain"), Chain(nc, "achain"), Chain(nc, "gchain")
        self.totals = {}
        self.block_no = 0
        self.slab_issued = 0
        self.slab_use = {}
        self.nslab = io["slabs"].shape[0]
        self.plain = weight_stream()[1]
        self.splits_before = np.cumsum([0] + [not p for p in self.plain])
        self.high_made, self.low_made = nc.alloc_semaphore("high_made"), nc.alloc_semaphore("low_made")
        self.slab_spent, self.midway = nc.alloc_semaphore("slab_spent"), 0
        self.split_after = {}
        self.latest = None

    def fixed(self, name, shape, dt=F32):
        t = self.at(name, shape, self.off, dt)
        n = 1
        for d in shape[1:]:
            n *= d
        self.off += (n * 4 + 63) // 64 * 64
        return t

    def at(self, name, shape, off, dt=F32):
        self.names += 1
        return self.nc.alloc_sbuf_tensor_at(f"{name}_{self.names}", shape, dt, offset=off)

    def reserve(self, name, n):
        if name not in self.totals:
            self.totals[name] = Counter(self.nc, name)
        return self.totals[name].take(n)

    def take_bank(self):
        while self.next_bank in self.pinned:
            self.next_bank = (self.next_bank + 1) % 8
        b = self.next_bank
        self.next_bank = (b + 1) % 8
        self.bank_uses[b] += 1
        return Use(b, self.bank_uses[b])

    def take_given(self, b):
        self.bank_uses[b] += 1
        return Use(b, self.bank_uses[b])

    def open(self, pe, u):
        if u.n > 1:
            pe.wait_ge(self.bank_read[u.b], u.n - 1)

    def full(self, eng, u):
        eng.wait_ge(self.bank_full[u.b], u.n)

    def read(self, eng, u):
        eng.wait_ge(self.bank_read[u.b], u.n)

    def take_tile(self, nk):
        u = self.take_bank()
        blocks = self.take_blocks(nk, u)
        return u, blocks

    def end_slab(self, s, use):
        self.slab_use[s] = use
        self.split_after.setdefault(id(use), []).append(s + AHEAD)

    def take_blocks(self, n, u):
        out = []
        for _ in range(n):
            s, i = divmod(self.block_no, SLAB)
            out.append((s, i))
            self.block_no += 1
            if i == SLAB - 1:
                self.end_slab(s, u)
        self.latest = u
        return out

    def next_slab(self):
        s, i = divmod(self.block_no, SLAB)
        if i:
            self.end_slab(s, self.latest)
            self.block_no = (s + 1) * SLAB

    def block(self, s, i, n=1):
        cols = slice(i * P, (i + n) * P)
        if self.plain[s]:
            return self.ring[:, s % RING, cols]
        return self.ring_high[:, self.splits_before[s] % AHEAD, cols], self.ring_low[:, s % RING, cols]

    def wait_slab(self, pe, s, seen):
        if s not in seen:
            if self.plain[s]:
                pe.wait_ge(self.slab_loaded[s % RING], 16 * (s // RING + 1))
            else:
                pe.wait_ge(self.low_made, int(self.splits_before[s]) + 1)
            seen.add(s)

    def slab_done(self, eng, s):
        use = self.slab_use[s]
        if isinstance(use, Use):
            self.full(eng, use)
        else:
            eng.wait_ge(self.slab_spent, use.n)

    def load_slabs(self, sp):
        upto = min(self.block_no // SLAB + RING, self.nslab)
        while self.slab_issued < upto:
            s = self.slab_issued
            if s >= RING:
                self.slab_done(sp, s - RING)
            sp.dma_start(self.ring[:, s % RING, :], self.io["slabs"][s]).then_inc(self.slab_loaded[s % RING], 16)
            self.slab_issued += 1

    def make_high(self, act, s):
        act.wait_ge(self.slab_loaded[s % RING], 16 * (s // RING + 1))
        act.activation(self.ring_high[:, self.splits_before[s] % AHEAD, :], self.ring[:, s % RING, :], ACT.Copy)\
            .then_inc(self.high_made, 1)

    def make_low(self, dve, s):
        dve.wait_ge(self.high_made, int(self.splits_before[s]) + 1)
        dve.tensor_tensor(self.ring_low[:, s % RING, :], self.ring[:, s % RING, :],
                          self.ring_high[:, self.splits_before[s] % AHEAD, :].bitcast(F32), ALU.subtract)\
            .then_inc(self.low_made, 1)

    def to_split(self, use):
        return [s for s in self.split_after.get(id(use), []) if s < self.nslab and not self.plain[s]]

    def split_high(self, act, use):
        for s in self.to_split(use):
            self.slab_done(act, s - AHEAD)
            self.make_high(act, s)

    def split_low(self, dve, use):
        for s in self.to_split(use):
            self.make_low(dve, s)

    def lows_done(self, eng, uses):
        last = max([s for use in uses for s in self.to_split(use)], default=None)
        if last is not None:
            eng.wait_ge(self.low_made, int(self.splits_before[last]) + 1)

    def product(self, pe, out, w, x, start, stop):
        if not isinstance(w, tuple):
            return pe.matmul(out, w, x, start=start, stop=stop)
        pe.matmul(out, w[0], x[0], start=start, stop=False)
        pe.matmul(out, w[0], x[1], start=False, stop=False)
        return pe.matmul(out, w[1], x[0], start=False, stop=stop)

    def gemm(self, pe, tile, moving, seen, n=T, ready=None):
        u, blocks = tile
        self.open(pe, u)
        for k, (s, i) in enumerate(blocks):
            if ready is not None:
                ready(k)
            self.wait_slab(pe, s, seen)
            mm = self.product(pe, self.bank[u.b][:, 0:n], self.block(s, i), moving[k], k == 0, k == len(blocks) - 1)
        mm.then_inc(self.bank_full[u.b], 1)

    def col(self, name, i, n=1, rows=P):
        a = COL_AT[name] + i
        return self.cols[0:rows, a:a + n]


def stage_load(C):
    nc, io = C.nc, C.io
    loaded, cols = C.reserve("loaded", 16), C.reserve("cols_loaded", 16)
    s5_act, s5_dve = s5_coefficients(C)
    made = C.reserve("made", 16)
    with nc.Block(no_gpsimd_drain=True) as block:
        @block.sync
        def _(sp):
            sp.dma_start(C.X[:], io["xT"]).then_inc(loaded.sem, 16)
            C.load_slabs(sp)

        @block.scalar
        def _(act):
            act.dma_start(C.cols[:], io["cols"]).then_inc(cols.sem, 16)
            act.wait_ge(cols.sem, cols.base + 16)
            s5_act(act)
            act.wait_ge(loaded.sem, loaded.base + 16)
            for s in range(AHEAD):
                C.make_high(act, s)

        @block.vector
        def _(dve):
            dve.memset(C.ones[:], 1.0)
            dve.memset(C.eps[:], EPS)
            dve.wait_ge(cols.sem, cols.base + 16)
            s5_dve(dve)
            for s in range(AHEAD):
                C.make_low(dve, s)

        @block.gpsimd
        def _(pool):
            pool.memset(C.ident[:], 0.0).then_inc(made.sem, 1)
            pool.memset(C.mask[:], 1.0).then_inc(made.sem, 1)
            pool.wait_ge(made.sem, made.at(1))
            pool.affine_select(out=C.ident[:], in_=C.ident[:], compare_op=ALU.not_equal, fill=1.0, base=0,
                               pattern=[[-1, P]], channel_multiplier=1).then_inc(made.sem, 1)
            pool.affine_select(out=C.mask[:], in_=C.mask[:], compare_op=ALU.is_ge, fill=0.0, base=0,
                               pattern=[[1, P]], channel_multiplier=-1).then_inc(made.sem, 1)
            pool.wait_ge(made.sem, made.at(3))


class Gates:

    def __init__(self, C):
        self.C = C
        self.out = C.at("gates", [P, KD, T], C.X_OFF)
        self.tiles = [C.take_tile(KD) for _ in range(KD)]

    def on_pe(self, pe, seen):
        for t in self.tiles:
            self.C.gemm(pe, t, self.C.H.tiles(KD), seen)

    def on_act(self, act, m):
        C, u = self.C, self.tiles[m][0]
        C.split_high(act, u)
        C.full(act, u)
        act.activation(self.out[:, m, :], C.bank[u.b][:], ACT.Sigmoid).then_inc(C.bank_read[u.b], 1)

    def on_dve(self, dve, m):
        self.C.split_low(dve, self.tiles[m][0])


def stage_norm(C, groups, g, dim, pair, n=T, with_gates=False):
    nc = C.nc
    src = [t for grp in groups for t in grp]
    banks = [C.take_bank() for _ in groups]
    squared = C.reserve("squared", len(src))
    summed = C.reserve("summed", len(src))
    scaled, highs = C.reserve("scaled", len(src)), C.reserve("highs", len(src))
    lows = C.reserve("lows", len(src) // 2)
    gates = Gates(C) if with_gates else None
    with nc.Block(no_gpsimd_drain=True) as block:
        @block.scalar
        def _(act):
            for i, t in enumerate(src):
                if i >= 4:
                    act.wait_ge(summed.sem, summed.at(i - 4))
                act.activation(C.sq[:, i % 4, 0:n], t, ACT.Square).then_inc(squared.sem, 1)
            for gi, u in enumerate(banks):
                C.full(act, u)
                act.activation(C.root[:, gi % 4, 0:n], C.bank[u.b][:, 0:n], ACT.Sqrt, bias=C.eps[:], scale=1.0 / dim)\
                    .then_inc(C.bank_read[u.b], 1)
            for i, t in enumerate(src):
                act.wait_ge(scaled.sem, scaled.at(i))
                act.activation(pair.tile(i)[0], t, ACT.Copy).then_inc(highs.sem, 1)
                if gates and i % 2:
                    gates.on_act(act, i // 2)

        @block.tensor
        def _(pe):
            i = 0
            for gi, grp in enumerate(groups):
                u = banks[gi]
                C.open(pe, u)
                for k in range(len(grp)):
                    pe.wait_ge(squared.sem, squared.at(i))
                    pe.matmul(C.bank[u.b][:, 0:n], C.ones[:], C.sq[:, i % 4, 0:n], start=(k == 0),
                              stop=(k == len(grp) - 1)).then_inc(summed.sem, 1)
                    i += 1
                pe.wait_ge(summed.sem, summed.at(i - 1))
                pe.sem_inc(C.bank_full[u.b], 1)
            if gates:
                gates.on_pe(pe, set())

        def low(eng, i):
            eng.wait_ge(highs.sem, highs.at(i))
            return eng.tensor_tensor(pair.tile(i)[1], src[i], pair.tile(i)[0].bitcast(F32), ALU.subtract)

        @block.vector
        def _(dve):
            i = 0
            for gi, grp in enumerate(groups):
                root = C.root[:, gi % 4, 0:n]
                C.read(dve, banks[gi])
                C.vchain.link(dve, dve.reciprocal(root, root))
                for t in grp:
                    dve.scalar_tensor_tensor(out=t, in0=t, scalar=g(i), in1=root, op0=ALU.mult, op1=ALU.mult)\
                        .then_inc(scaled.sem, 1)
                    if i % 2:
                        C.vchain.link(dve, low(dve, i - 1))
                        if gates and i >= 3:
                            gates.on_dve(dve, i // 2 - 1)
                    i += 1
            if gates:
                gates.on_dve(dve, KD - 1)
            dve.wait_ge(lows.sem, lows.base + i // 2)

        @block.gpsimd
        def _(pool):
            for i in range(1, len(src), 2):
                low(pool, i).then_inc(lows.sem, 1)

        @block.sync
        def _(sp):
            C.load_slabs(sp)
    return gates


def conv_tile(C, dve, u, w, b, acc):
    x = C.bank[u.b]
    C.vchain.link(dve, dve.tensor_scalar(acc, x[:], w(3), b, ALU.mult, ALU.add))
    for d in range(1, 4):
        ins = dve.scalar_tensor_tensor(out=acc[:, d:T], in0=x[:, 0:T - d], scalar=w(3 - d), in1=acc[:, d:T],
                                       op0=ALU.mult, op1=ALU.add)
        if d == 3:
            ins.then_inc(C.bank_read[u.b], 1)
        else:
            C.vchain.link(dve, ins)


def log1p_small(C, dve, e, s, s2, acc):
    ln = C.vchain.link
    ln(dve, dve.tensor_scalar(s, e, 2.0, None, ALU.add))
    ln(dve, dve.reciprocal(s, s))
    ln(dve, dve.tensor_tensor(s, s, e, ALU.mult))
    ln(dve, dve.tensor_tensor(s2, s, s, ALU.mult))
    ln(dve, dve.tensor_scalar(acc, s2, 2.0 / 17, None, ALU.mult))
    for k in range(15, 1, -2):
        ln(dve, dve.scalar_tensor_tensor(out=acc, in0=acc, scalar=2.0 / k, in1=s2, op0=ALU.add, op1=ALU.mult))
    ln(dve, dve.scalar_tensor_tensor(out=e, in0=acc, scalar=2.0, in1=s, op0=ALU.add, op1=ALU.mult))


def stage_xbc(C, L, batches, norm):
    nc = C.nc
    dt = C.take_tile(KD)
    tiles = [C.take_tile(KD) for _ in range(24)]
    tables = Tables(C, L, batches)
    convolved = C.reserve("conv", 24)
    dts = C.reserve("dts", 9)
    tb = [C.take_bank() for _ in range(3)]
    with nc.Block(no_gpsimd_drain=True) as block:
        @block.sync
        def _(sp):
            C.load_slabs(sp)

        @block.gpsimd
        def _(pool):
            norm.on_pool(pool)
            tables.make(pool)

        @block.tensor
        def _(pe):
            seen = set()
            norm.on_pe(pe)
            C.gemm(pe, dt, C.H.tiles(KD), seen, ready=lambda k: norm.done(pe, k))
            for t in tiles:
                C.gemm(pe, t, C.H.tiles(KD), seen)
            pe.wait_ge(dts.sem, dts.at(5))
            for u, src in ((tb[0], L.DT), (tb[1], L.ACS)):
                C.open(pe, u)
                for c in range(TC):
                    t = pe.transpose(C.bank[u.b][:, c * 32:c * 32 + 32], src[:, c * P:(c + 1) * P], C.ident[0:32, 0:32])
                t.then_inc(C.bank_full[u.b], 1)
            u = tb[2]
            C.open(pe, u)
            pe.wait_ge(dts.sem, dts.at(6))
            pe.matmul(C.bank[u.b][:, 0:P], C.ones[0:32, :], L.END[:], start=True, stop=True)\
                .then_inc(C.bank_full[u.b], 1)

        @block.vector
        def _(dve):
            ln = C.vchain.link
            norm.on_dve(dve)
            norm.finish(dve)
            u = dt[0]
            C.full(dve, u)
            dve.tensor_scalar(L.DT[:], C.bank[u.b][0:32, :], C.col("dt_bias", 0, rows=32), None, ALU.add)\
                .then_inc(C.bank_read[u.b], 1)
            C.read(dve, u)
            ln(dve, dve.tensor_scalar(L.S1[:], L.DT[:], -1.0, None, ALU.mult))
            dve.tensor_tensor(L.S1[:], L.S1[:], L.DT[:], ALU.min).then_inc(dts.sem, 1)
            dve.wait_ge(dts.sem, dts.at(1))
            log1p_small(C, dve, L.S1[:], L.S2[:], L.S3[:], L.S4[:])
            ln(dve, dve.tensor_scalar(L.DT[:], L.DT[:], 0.0, None, ALU.max))
            ln(dve, dve.tensor_tensor(L.DT[:], L.DT[:], L.S1[:], ALU.add))
            ln(dve, dve.tensor_scalar(L.S1[:], L.DT[:], L.AN[0:32, :], -1.0, ALU.mult, ALU.mult))
            ln(dve, dve.memset(L.S2[:], 1.0))
            for c in range(TC):
                cs = slice(c * P, (c + 1) * P)
                dve.tensor_tensor_scan(L.ACS[:, cs], L.S2[:, cs], L.S1[:, cs], 0.0, ALU.mult, ALU.add)\
                    .then_inc(dts.sem, 1)
            dve.wait_ge(dts.sem, dts.at(5))
            ends = L.ACS[:].rearrange("h (c l) -> h c l", c=TC)[:, :, P - 1:P].to_broadcast([32, TC, 32])
            dve.tensor_tensor(L.END[:].rearrange("h (c k) -> h c k", c=TC), ends,
                              C.ident[0:32, 0:32].unsqueeze(1).to_broadcast([32, TC, 32]), ALU.mult)\
                .then_inc(dts.sem, 1)
            C.split_low(dve, u)
            for i, (u, _) in enumerate(tiles):
                C.full(dve, u)
                if i >= 4:
                    dve.wait_ge(convolved.sem, convolved.at(i - 4))
                conv_tile(C, dve, u, lambda j: C.col("conv_w", 24 * j + i), C.col("conv_b", i), C.sq[:, i % 4, :])
                C.split_low(dve, u)
            C.full(dve, tb[0])
            dve.tensor_copy(L.DTT[:], C.bank[tb[0].b][:, 0:P]).then_inc(C.bank_read[tb[0].b], 1)
            C.full(dve, tb[1])
            dve.tensor_copy(L.ACST[:], C.bank[tb[1].b][:, 0:P]).then_inc(C.bank_read[tb[1].b], 1)
            C.read(dve, tb[1])
            C.full(dve, tb[2])
            dve.tensor_copy(L.CD[:], C.bank[tb[2].b][:, 0:P]).then_inc(C.bank_read[tb[2].b], 1)
            C.read(dve, tb[2])
            dve.tensor_tensor(L.DTE[:], L.CD[:], L.ACST[:], ALU.subtract).then_inc(dts.sem, 1)
            C.read(dve, tb[0])
            dve.wait_ge(dts.sem, dts.at(8))
            ln(dve, dve.tensor_tensor(L.DTE[:], L.DTE[:], L.DTT[:], ALU.mult))

        @block.scalar
        def _(act):
            norm.on_act(act)
            C.split_high(act, dt[0])
            act.wait_ge(dts.sem, dts.at(0))
            C.achain.link(act, act.activation(L.AN[:], C.col("a_log", 0), ACT.Exp))
            act.activation(L.S1[:], L.S1[:], ACT.Exp).then_inc(dts.sem, 1)
            for i, (u, _) in enumerate(tiles):
                C.split_high(act, u)
                C.read(act, u)
                dst = L.XS[:, i, :] if i < 16 else L.BC[:, i - 16, :]
                act.activation(dst, C.sq[:, i % 4, :], ACT.Silu).then_inc(convolved.sem, 1)
            act.wait_ge(dts.sem, dts.at(7))
            C.achain.link(act, act.activation(L.DTE[:], L.DTE[:], ACT.Exp))
            act.activation(L.CD[:], L.CD[:], ACT.Exp).then_inc(dts.sem, 1)


def stage_ssd(C, L):
    nc = C.nc
    G, NH = SSD_G, 8
    B = {}

    def take_inputs(g):
        B["bt", g] = C.take_bank()
        for c in range(TC):
            B["xt", g, c] = C.take_bank()
        B["cb", g] = C.take_bank()

    take_inputs(0)
    for g in range(G):
        B["z", g, 0] = C.take_tile(KD)
        for c in range(3):
            B["st", g, c] = C.take_bank()
        for j in range(4):
            for e in range(2):
                B["abc", g, 2 * j + e] = C.take_bank()
            if j < 3:
                B["z", g, j + 1] = C.take_tile(KD)
            elif g + 1 < G:
                take_inputs(g + 1)
            B["y", g, j] = C.take_bank()
    ea = C.reserve("ea", 32)
    ce = C.reserve("ce", 32)
    seg = C.reserve("seg", 32)
    dec = C.reserve("dec", 32)
    mr = C.reserve("mr", 32)
    xd = C.reserve("xd", G * 8)
    pv = C.reserve("pv", G * 6)
    zused = C.reserve("zused", KS)

    def prev(c):
        return L.PV[:, c - 1, :]

    with nc.Block(no_gpsimd_drain=True) as block:
        @block.sync
        def _(sp):
            C.load_slabs(sp)

        @block.tensor
        def _(pe):
            seen = set()

            def inputs(g):
                bg, cg = L.BC[:, g, :], L.BC[:, 4 + g, :]
                u = B["bt", g]
                C.open(pe, u)
                for c in range(TC):
                    t = pe.transpose(C.bank[u.b][:, c * P:(c + 1) * P], bg[:, c * P:(c + 1) * P], C.ident[:])
                t.then_inc(C.bank_full[u.b], 1)
                for c in range(TC):
                    u = B["xt", g, c]
                    C.open(pe, u)
                    for j in range(4):
                        t = pe.transpose(C.bank[u.b][:, j * P:(j + 1) * P], L.XS[:, 4 * g + j, c * P:(c + 1) * P],
                                         C.ident[:])
                    t.then_inc(C.bank_full[u.b], 1)
                u = B["cb", g]
                C.open(pe, u)
                for c in range(TC):
                    cs = slice(c * P, (c + 1) * P)
                    t = pe.matmul(C.bank[u.b][:, cs], bg[:, cs], cg[:, cs], start=True, stop=True)
                t.then_inc(C.bank_full[u.b], 1)

            inputs(0)
            for g in range(G):
                C.gemm(pe, B["z", g, 0], C.H.tiles(KD), seen)
                C.read(pe, B["bt", g])
                for c in range(3):
                    u = B["st", g, c]
                    C.open(pe, u)
                    pe.wait_ge(xd.sem, xd.at(8 * g + 2 * c + 1))
                    pe.matmul(C.bank[u.b][:], L.BT[:, c * P:(c + 1) * P], L.XDE[:, c, :], start=True, stop=True)\
                        .then_inc(C.bank_full[u.b], 1)
                for j in range(4):
                    for e in range(2):
                        h = 8 * g + 2 * j + e
                        u = B["abc", g, 2 * j + e]
                        C.open(pe, u)
                        pe.matmul(C.bank[u.b][:], C.ident[0:32, h:h + 1].to_broadcast([32, P]), L.ACS[:], start=True,
                                  stop=True).then_inc(C.bank_full[u.b], 1)
                    if j < 3:
                        C.gemm(pe, B["z", g, j + 1], C.H.tiles(KD), seen)
                    elif g + 1 < G:
                        inputs(g + 1)
                    u = B["y", g, j]
                    C.open(pe, u)
                    pe.wait_ge(xd.sem, xd.at(8 * g + 7))
                    pe.wait_ge(pv.sem, pv.at(6 * g + 5))
                    for e in range(2):
                        h = 8 * g + 2 * j + e
                        pe.wait_ge(mr.sem, mr.at(h))
                        pe.wait_ge(ce.sem, ce.at(h))
                        hp = slice((2 * j + e) * 64, (2 * j + e) * 64 + 64)
                        for c in range(TC):
                            cs = slice(c * P, (c + 1) * P)
                            dst = C.bank[u.b][64 * e:64 * e + 64, cs]
                            t = pe.matmul(dst, L.XDT[:, c, hp], L.DEC[:, h % 4, cs], start=True, stop=(c == 0))
                            if c > 0:
                                t = pe.matmul(dst, prev(c)[:, hp], L.CE[:, h % 4, cs], start=False, stop=True)
                    t.then_inc(C.bank_full[u.b], 1)

        @block.vector
        def _(dve):
            ln = C.vchain.link

            def heads(v, c, g):
                return v[:, c * 32 + 8 * g:c * 32 + 8 * g + 8].unsqueeze(2).to_broadcast([P, 8, 64])

            def v3(ap):
                return ap.rearrange("p (h q) -> p h q", h=8)

            def add_y(g, j):
                u = B["y", g, j]
                C.full(dve, u)
                xs = L.XS[:, 4 * g + j, :]
                dve.scalar_tensor_tensor(out=xs, in0=xs, scalar=C.col("ssd_d", 4 * g + j), in1=C.bank[u.b][:],
                                         op0=ALU.mult, op1=ALU.add).then_inc(C.bank_read[u.b], 1)
                C.read(dve, u)
                z = B["z", g, j][0]
                C.read(dve, z)
                dve.tensor_tensor(xs, xs, L.SZ[:, j, :], ALU.mult).then_inc(zused.sem, 1)

            for g in range(G):
                if g > 0:
                    add_y(g - 1, 3)
                for c in range(TC):
                    u = B["xt", g, c]
                    C.full(dve, u)
                    dve.tensor_tensor(v3(L.XDT[:, c, :]), v3(C.bank[u.b][:]), heads(L.DTT[:], c, g), ALU.mult)\
                        .then_inc(xd.sem, 1)
                    dve.wait_ge(xd.sem, xd.at(8 * g + 2 * c))
                    dve.tensor_tensor(v3(L.XDE[:, c, :]), v3(C.bank[u.b][:]), heads(L.DTE[:], c, g), ALU.mult)\
                        .then_inc(xd.sem, 1)
                    dve.wait_ge(xd.sem, xd.at(8 * g + 2 * c + 1))
                    dve.sem_inc(C.bank_read[u.b], 1)
                u = B["cb", g]
                C.full(dve, u)
                dve.tensor_tensor(L.CBM[:].rearrange("s (c l) -> s c l", c=TC),
                                  C.bank[u.b][:].rearrange("s (c l) -> s c l", c=TC),
                                  C.mask[:].unsqueeze(1).to_broadcast([P, TC, P]), ALU.mult)\
                    .then_inc(C.bank_read[u.b], 1)
                C.split_low(dve, B["z", g, 0][0])
                for c in range(3):
                    u = B["st", g, c]
                    C.full(dve, u)
                    if c > 0:
                        dve.tensor_tensor(v3(prev(c + 1)), v3(prev(c)), heads(L.CD[:], c, g), ALU.mult)\
                            .then_inc(pv.sem, 1)
                        dve.wait_ge(pv.sem, pv.at(6 * g + 2 * c))
                        dve.tensor_tensor(prev(c + 1), prev(c + 1), C.bank[u.b][:], ALU.add).then_inc(pv.sem, 1)
                        dve.wait_ge(pv.sem, pv.at(6 * g + 2 * c + 1))
                    else:
                        dve.tensor_copy(prev(1), C.bank[u.b][:]).then_inc(pv.sem, 1)
                        dve.wait_ge(pv.sem, pv.at(6 * g))
                        dve.sem_inc(pv.sem, 1)
                    dve.sem_inc(C.bank_read[u.b], 1)
                C.read(dve, B["cb", g])
                for j in range(4):
                    for e in range(2):
                        h = 8 * g + 2 * j + e
                        u = B["abc", g, 2 * j + e]
                        dve.wait_ge(ea.sem, ea.at(h))
                        if h >= 4:
                            C.full(dve, B["y", (h - 4) // 8, (h - 4) % 8 // 2])
                        acs = L.ACST[:].rearrange("s (c h) -> s c h", c=TC)[:, :, h:h + 1].to_broadcast([P, TC, P])
                        dve.tensor_tensor(L.DEC[:, h % 4, :].rearrange("s (c l) -> s c l", c=TC),
                                          C.bank[u.b][:].rearrange("s (c l) -> s c l", c=TC), acs, ALU.min)\
                            .then_inc(C.bank_read[u.b], 1)
                    if j > 0:
                        add_y(g, j - 1)
                    for e in range(2):
                        h = 8 * g + 2 * j + e
                        dve.wait_ge(dec.sem, dec.at(h))
                        dve.tensor_tensor(L.DEC[:, h % 4, :], L.DEC[:, h % 4, :], L.CBM[:], ALU.mult)\
                            .then_inc(mr.sem, 1)
                    if j < 3:
                        C.split_low(dve, B["z", g, j + 1][0])
            add_y(G - 1, 3)

        @block.gpsimd
        def _(pool):
            for g in range(G):
                for j in range(4):
                    for e in range(2):
                        h = 8 * g + 2 * j + e
                        acs = L.ACST[:].rearrange("s (c h) -> s c h", c=TC)[:, :, h:h + 1].to_broadcast([P, TC, P])
                        d = L.DEC[:, h % 4, :].rearrange("s (c l) -> s c l", c=TC)
                        C.read(pool, B["abc", g, 2 * j + e])
                        pool.tensor_tensor(d, d, acs, ALU.subtract).then_inc(seg.sem, 1)
                    for e in range(2):
                        h = 8 * g + 2 * j + e
                        pool.wait_ge(ea.sem, ea.at(h))
                        pool.tensor_tensor(L.CE[:, h % 4, :], L.CE[:, h % 4, :], L.BC[:, 4 + g, :], ALU.mult)\
                            .then_inc(ce.sem, 1)

        @block.scalar
        def _(act):
            def silu_z(g, j):
                u = B["z", g, j][0]
                C.split_high(act, u)
                C.full(act, u)
                if g > 0:
                    act.wait_ge(zused.sem, zused.at(4 * g + j - 4))
                act.activation(L.SZ[:, j, :], C.bank[u.b][:], ACT.Silu).then_inc(C.bank_read[u.b], 1)

            for g in range(G):
                u = B["bt", g]
                C.full(act, u)
                act.activation(L.BT[:], C.bank[u.b][:], ACT.Copy).then_inc(C.bank_read[u.b], 1)
                silu_z(g, 0)
                for j in range(4):
                    for e in range(2):
                        h = 8 * g + 2 * j + e
                        u = B["abc", g, 2 * j + e]
                        C.full(act, u)
                        if h >= 4:
                            C.full(act, B["y", (h - 4) // 8, (h - 4) % 8 // 2])
                        act.activation(L.CE[:, h % 4, :], C.bank[u.b][:], ACT.Exp).then_inc(ea.sem, 1)
                    for e in range(2):
                        h = 8 * g + 2 * j + e
                        act.wait_ge(seg.sem, seg.at(h))
                        act.activation(L.DEC[:, h % 4, :], L.DEC[:, h % 4, :], ACT.Exp).then_inc(dec.sem, 1)
                    if j < 3:
                        silu_z(g, j + 1)


def split_tile(C, dve, x, parts):
    C.vchain.link(dve, dve.tensor_copy(parts[0], x))
    return dve.tensor_tensor(parts[1], x, parts[0].bitcast(F32), ALU.subtract)


def stage_merge(C, L, br, moving, batches=(), pair=None, gates=None, load=None):
    nc = C.nc
    nk = len(moving)
    gate, prod = [], []
    for m in range(KD):
        if gates is None:
            gate.append(C.take_tile(KD))
        prod.append(C.take_tile(nk))
    tables = Tables(C, L, batches)
    with nc.Block(no_gpsimd_drain=True) as block:
        @block.sync
        def _(sp):
            C.load_slabs(sp)

        @block.gpsimd
        def _(pool):
            if load is not None:
                load(pool)
            tables.make(pool)

        @block.tensor
        def _(pe):
            seen = set()
            for m in range(KD):
                if gates is None:
                    C.gemm(pe, gate[m], C.H.tiles(KD), seen)
                C.gemm(pe, prod[m], moving, seen)

        @block.scalar
        def _(act):
            for m in range(KD):
                if gates is None:
                    u = gate[m][0]
                    C.split_high(act, u)
                    C.full(act, u)
                    if m >= 4:
                        C.read(act, prod[m - 4][0])
                    act.activation(C.sq[:, m % 4, :], C.bank[u.b][:], ACT.Sigmoid).then_inc(C.bank_read[u.b], 1)
                C.split_high(act, prod[m][0])

        @block.vector
        def _(dve):
            for m in range(KD):
                u = prod[m][0]
                C.full(dve, u)
                if gates is None:
                    C.read(dve, gate[m][0])
                g = C.sq[:, m % 4, :] if gates is None else gates.out[:, m, :]
                if br == 0:
                    dve.tensor_tensor(C.MG[:, m, :], g, C.bank[u.b][:], ALU.mult)\
                        .then_inc(C.bank_read[u.b], 1)
                else:
                    C.vchain.link(dve, dve.tensor_tensor(g, g, C.bank[u.b][:], ALU.mult))
                    dve.tensor_tensor(C.MG[:, m, :], C.MG[:, m, :], g, ALU.add).then_inc(C.bank_read[u.b], 1)
                if pair is not None:
                    C.read(dve, u)
                    C.vchain.link(dve, split_tile(C, dve, C.MG[:, m, :], pair.tile(m)))
                if gates is None:
                    C.split_low(dve, gate[m][0])
                C.split_low(dve, u)


class Norm:

    def __init__(self, C, src, g, dim, bank, root=0, pair=None, keep=False, add=None, early=False, after=None, w=T):
        self.C, self.src, self.g, self.dim, self.u = C, src, g, dim, bank
        self.pair, self.add, self.early, self.after = pair, add, early, after
        self.tmp = [C.sq[:, i % 4, :] if keep else t for i, t in enumerate(src)]
        self.keep = keep
        self.root, self.w = C.root[:, root, 0:w], w
        n = len(src)
        self.squared, self.summed, self.scaled = [C.reserve(x, n) for x in ("squared", "summed", "scaled")]
        if pair is not None:
            self.highs = C.reserve("highs", n)
        if pair is not None or add is not None:
            self.even, self.odd = C.reserve("norm_even", (n + 1) // 2), C.reserve("norm_odd", n // 2)

    def square(self, act, i):
        if i >= 4:
            act.wait_ge(self.summed.sem, self.summed.at(i - 4))
        act.activation(self.C.sq[:, i % 4, 0:self.w], self.src[i], ACT.Square).then_inc(self.squared.sem, 1)

    def sum(self, pe, i):
        C, u, n = self.C, self.u, len(self.src)
        if i == 0:
            C.open(pe, u)
        pe.wait_ge(self.squared.sem, self.squared.at(i))
        pe.matmul(C.bank[u.b][:, 0:self.w], C.ones[:], C.sq[:, i % 4, 0:self.w], start=(i == 0), stop=(i == n - 1))\
            .then_inc(self.summed.sem, 1)
        if i == n - 1:
            pe.wait_ge(self.summed.sem, self.summed.at(i))
            pe.sem_inc(C.bank_full[u.b], 1)

    def done(self, eng, i):
        if self.pair is None and self.add is None:
            eng.wait_ge(self.scaled.sem, self.scaled.at(i))
        else:
            part = self.odd if i % 2 else self.even
            eng.wait_ge(part.sem, part.at(i // 2))

    def on_act(self, act):
        C, u = self.C, self.u
        if not self.early:
            for i in range(len(self.src)):
                if self.after is not None:
                    self.after(act, i)
                self.square(act, i)
        C.full(act, u)
        act.activation(self.root, C.bank[u.b][:, 0:self.w], ACT.Sqrt, bias=C.eps[:], scale=1.0 / self.dim).then_inc(C.bank_read[u.b], 1)
        if self.pair is not None:
            for i in range(len(self.src)):
                act.wait_ge(self.scaled.sem, self.scaled.at(i))
                act.activation(self.pair.tile(i)[0], self.tmp[i], ACT.Copy).then_inc(self.highs.sem, 1)

    def on_pe(self, pe):
        if not self.early:
            for i in range(len(self.src)):
                self.sum(pe, i)

    def last_step(self, eng, i):
        part = self.odd if i % 2 else self.even
        if self.add is not None:
            eng.wait_ge(self.scaled.sem, self.scaled.at(i))
            ins = eng.tensor_tensor(self.add(i), self.add(i), self.tmp[i], ALU.add)
        else:
            eng.wait_ge(self.highs.sem, self.highs.at(i))
            ins = eng.tensor_tensor(self.pair.tile(i)[1], self.tmp[i], self.pair.tile(i)[0].bitcast(F32), ALU.subtract)
        ins.then_inc(part.sem, 1)

    def on_dve(self, dve):
        C, n = self.C, len(self.src)
        last = self.pair is not None or self.add is not None
        C.read(dve, self.u)
        C.vchain.link(dve, dve.reciprocal(self.root, self.root))
        for i in range(n):
            if self.keep and i >= 4:
                self.done(dve, i - 4)
            dve.scalar_tensor_tensor(out=self.tmp[i], in0=self.src[i], scalar=self.g(i), in1=self.root, op0=ALU.mult,
                                     op1=ALU.mult).then_inc(self.scaled.sem, 1)
            if last and i % 2:
                self.last_step(dve, i - 1)
        if last and n % 2:
            self.last_step(dve, n - 1)

    def on_pool(self, pool):
        if self.pair is not None or self.add is not None:
            for i in range(1, len(self.src), 2):
                self.last_step(pool, i)

    def finish(self, dve):
        if self.pair is not None or self.add is not None:
            self.done(dve, len(self.src) // 2 * 2 - 1)


class Side:

    def __init__(self, tensor={}, act={}, pool=None, sync=None, dve_first=None, dve_last=None, ready=None):
        self.tensor, self.act = tensor, act
        self.pool, self.sync, self.dve_first, self.dve_last, self.ready = pool, sync, dve_first, dve_last, ready


def stage_gemm(C, nt, moving, evac, engine="scalar", n=T, then=None, norms=(), stats=(), side=Side()):
    nc = C.nc
    tiles = [C.take_tile(len(moving)) for _ in range(nt)]
    ready = side.ready
    if norms and norms[-1].keep:
        ready = norms[-1].done
    with nc.Block(no_gpsimd_drain=True) as block:
        @block.sync
        def _(sp):
            if side.sync is not None:
                side.sync(sp)
            C.load_slabs(sp)

        @block.gpsimd
        def _(pool):
            for x in norms:
                x.on_pool(pool)
            if side.pool is not None:
                side.pool(pool)

        @block.tensor
        def _(pe):
            seen = set()
            for x in norms:
                x.on_pe(pe)
            for i, t in enumerate(tiles):
                C.gemm(pe, t, moving, seen, n=n, ready=(lambda k: ready(pe, k)) if ready is not None and i == 0 else None)
                if stats and i > 0:
                    stats[i - 1][0].sum(pe, stats[i - 1][1])
                if i in side.tensor:
                    side.tensor[i](pe)
            if stats:
                stats[-1][0].sum(pe, stats[-1][1])

        @block.scalar
        def _(act):
            for x in norms:
                x.on_act(act)
            for i, (u, _) in enumerate(tiles):
                C.split_high(act, u)
                if engine == "scalar":
                    C.full(act, u)
                    evac(act, i, C.bank[u.b]).then_inc(C.bank_read[u.b], 1)
                if stats:
                    C.read(act, u)
                    stats[i][0].square(act, stats[i][1])
                if i in side.act:
                    side.act[i](act)

        @block.vector
        def _(dve):
            for x in norms:
                x.on_dve(dve)
            for x in norms:
                x.finish(dve)
            if side.dve_first is not None:
                side.dve_first(dve)
            for i, (u, _) in enumerate(tiles):
                if engine == "vector":
                    C.full(dve, u)
                    evac(dve, i, C.bank[u.b]).then_inc(C.bank_read[u.b], 1)
                if then is not None:
                    C.read(dve, u)
                    then(dve, i)
                C.split_low(dve, u)
            if side.dve_last is not None:
                side.dve_last(dve)


def stage_tokmajor(C, wide, src, dst, n_tok, act_fn=ACT.Copy):
    nc = C.nc
    nk = len(src)
    halves = []
    for _ in range(2 if wide == 4 else 1):
        us = [C.take_bank() for _ in range(n_tok)]
        blocks, ends = [], {}
        for k in range(nk):
            use = us[-1]
            if k < nk - 1 and C.block_no % SLAB + wide >= SLAB:
                C.midway += 1
                use = ends[k] = SlabSpent(C.midway)
            blocks.append(C.take_blocks(wide, use))
        halves.append((us, blocks, ends))
    with nc.Block(no_gpsimd_drain=True) as block:
        @block.sync
        def _(sp):
            C.load_slabs(sp)

        @block.tensor
        def _(pe):
            seen = set()
            for us, blocks, ends in halves:
                for u in us:
                    C.open(pe, u)
                for k in range(nk):
                    s, i = blocks[k][0]
                    assert blocks[k][-1][0] == s
                    C.wait_slab(pe, s, seen)
                    for t, u in enumerate(us):
                        mm = C.product(pe, C.bank[u.b][:, 0:wide * P], tuple(x[:, t * P:(t + 1) * P] for x in src[k]),
                                       C.block(s, i, wide), k == 0, k == nk - 1)
                        if k == nk - 1:
                            mm.then_inc(C.bank_full[u.b], 1)
                    if k in ends:
                        mm.then_inc(C.slab_spent, 1)

        @block.vector
        def _(dve):
            for us, _, ends in halves:
                for use in ends.values():
                    C.split_low(dve, use)
                C.split_low(dve, us[-1])

        @block.scalar
        def _(act):
            for half, (us, _, ends) in enumerate(halves):
                for use in ends.values():
                    C.split_high(act, use)
                for t, u in enumerate(us):
                    C.full(act, u)
                    act.activation(dst(half, t), C.bank[u.b][:, 0:wide * P], act_fn).then_inc(C.bank_read[u.b], 1)
                C.split_high(act, us[-1])


def stage_lru(C, L):
    nc = C.nc

    def evac(dve, i, bank):
        acc = L.XL[:, i, :]
        C.vchain.link(dve, dve.tensor_scalar(acc, bank[:], C.col("lru_conv_w", 36 + i), C.col("lru_conv_b", i),
                                             ALU.mult, ALU.add))
        for d in range(1, 4):
            ins = dve.scalar_tensor_tensor(out=acc[:, d:T], in0=bank[:, 0:T - d],
                                           scalar=C.col("lru_conv_w", 12 * (3 - d) + i), in1=acc[:, d:T],
                                           op0=ALU.mult, op1=ALU.add)
            if d < 3:
                C.vchain.link(dve, ins)
        return ins

    stage_gemm(C, KL, C.H.tiles(KD), evac, "vector", side=Side(pool=Tables(C, L, [3]).make))

    C.next_slab()
    sp_ = C.reserve("sps", 2)
    r_tiles = [C.take_tile(len(lru_inputs(m))) for m in range(KL)]
    i_tiles = [C.take_tile(len(lru_inputs(m))) for m in range(KL)]
    C.next_slab()
    tables = Tables(C, L, [4])
    with nc.Block(no_gpsimd_drain=True) as block:
        @block.sync
        def _(sp):
            C.load_slabs(sp)

        @block.gpsimd
        def _(pool):
            tables.make(pool)

        @block.tensor
        def _(pe):
            seen = set()
            for tiles in (r_tiles, i_tiles):
                for m, t in enumerate(tiles):
                    C.gemm(pe, t, [L.XL[:, k, :] for k in lru_inputs(m)], seen)

        @block.vector
        def _(dve):
            ln = C.vchain.link
            lam = C.col("lam", 0, 12)
            ln(dve, dve.tensor_scalar(L.SPA, lam, -1.0, None, ALU.mult))
            dve.tensor_tensor(L.SPB, L.SPA, lam, ALU.min).then_inc(sp_.sem, 1)
            dve.wait_ge(sp_.sem, sp_.at(1))
            log1p_small(C, dve, L.SPB, L.SPC, L.SPD, L.SPE)
            ln(dve, dve.tensor_scalar(L.SPA, L.SPA, 0.0, None, ALU.max))
            ln(dve, dve.tensor_tensor(L.SPA, L.SPA, L.SPB, ALU.add))
            ln(dve, dve.tensor_scalar(L.SPA, L.SPA, -8.0, None, ALU.mult))
            for m, (u, _) in enumerate(r_tiles):
                C.read(dve, u)
                dve.tensor_scalar(L.R[:, m, :], L.R[:, m, :], L.SPA[:, m:m + 1], None, ALU.mult)
                C.split_low(dve, u)
            for u, _ in i_tiles:
                C.split_low(dve, u)

        @block.scalar
        def _(act):
            act.wait_ge(sp_.sem, sp_.at(0))
            act.activation(L.SPB, L.SPB, ACT.Exp).then_inc(sp_.sem, 1)
            for tiles, b, dst in ((r_tiles, "b_a", L.R), (i_tiles, "b_x", L.I)):
                for m, (u, _) in enumerate(tiles):
                    C.split_high(act, u)
                    C.full(act, u)
                    act.activation(dst[:, m, :], C.bank[u.b][:], ACT.Sigmoid, bias=C.col(b, m))\
                        .then_inc(C.bank_read[u.b], 1)

    g = [C.take_tile(KD) for _ in range(KL)]
    gates = Gates(C)
    ix = C.reserve("ix", 2)
    th, rt, sr, scanned, gused = [C.reserve(n, KL) for n in ("th", "rt", "sr", "scanned", "gused")]
    NB, BUFS = 2, 4
    with nc.Block(no_gpsimd_drain=True) as block:
        @block.sync
        def _(sp):
            C.load_slabs(sp)

        @block.tensor
        def _(pe):
            seen = set()
            for t in g:
                C.gemm(pe, t, C.H.tiles(KD), seen)
            gates.on_pe(pe, seen)

        @block.gpsimd
        def _(pool):
            for m in range(KL):
                C.gchain.link(pool, pool.tensor_tensor(L.I[:, m, :], L.I[:, m, :], L.XL[:, m, :], ALU.mult))
            pool.sem_inc(ix.sem, 1)
            for m in range(KL):
                x = L.XL[:, m, :]
                pool.wait_ge(scanned.sem, scanned.at(m))
                C.read(pool, g[m][0])
                pool.tensor_tensor(x, x, L.G[:, m % BUFS, :], ALU.mult).then_inc(gused.sem, 1)
                pool.wait_ge(gused.sem, gused.at(m))
                C.gchain.link(pool, pool.tensor_copy(L.OUT.high[:, m, :], x))
                C.gchain.link(pool, pool.tensor_tensor(L.OUT.low[:, m, :], x, L.OUT.high[:, m, :].bitcast(F32), ALU.subtract))
            pool.sem_inc(ix.sem, 1)

        @block.vector
        def _(dve):
            ln = C.vchain.link

            def ratios(b):
                for m in range(b, b + NB):
                    t, q = C.sq[:, m % BUFS, :], C.root[:, m % BUFS, :]
                    dve.wait_ge(th.sem, th.at(m))
                    ln(dve, dve.tensor_scalar(q, t, 1.0, None, ALU.add))
                    ln(dve, dve.reciprocal(q, q))
                    dve.scalar_tensor_tensor(out=q, in0=t, scalar=2.0, in1=q, op0=ALU.mult, op1=ALU.mult)\
                        .then_inc(rt.sem, 1)

            ratios(0)
            dve.wait_ge(ix.sem, ix.at(0))
            for b in range(0, KL, NB):
                if b + NB < KL:
                    ratios(b + NB)
                for m in range(b, b + NB):
                    q = C.root[:, m % BUFS, :]
                    dve.wait_ge(sr.sem, sr.at(m))
                    ln(dve, dve.tensor_tensor(q, q, L.I[:, m, :], ALU.mult))
                    dve.tensor_tensor_scan(L.XL[:, m, :], L.R[:, m, :], q, 0.0, ALU.mult, ALU.add)\
                        .then_inc(scanned.sem, 1)
                for m in range(b, b + NB):
                    C.split_low(dve, g[m][0])
            for m in range(KD):
                gates.on_dve(dve, m)
            dve.wait_ge(ix.sem, ix.at(1))

        @block.scalar
        def _(act):
            def decays(b):
                for m in range(b, b + NB):
                    t = C.sq[:, m % BUFS, :]
                    if m >= BUFS:
                        act.wait_ge(rt.sem, rt.at(m - BUFS))
                    C.achain.link(act, act.activation(t, L.R[:, m, :], ACT.Tanh, scale=-1.0))
                    act.activation(L.R[:, m, :], L.R[:, m, :], ACT.Exp).then_inc(th.sem, 1)

            decays(0)
            for b in range(0, KL, NB):
                if b + NB < KL:
                    decays(b + NB)
                for m in range(b, b + NB):
                    q = C.root[:, m % BUFS, :]
                    act.wait_ge(rt.sem, rt.at(m))
                    act.activation(q, q, ACT.Sqrt).then_inc(sr.sem, 1)
                for m in range(b, b + NB):
                    u = g[m][0]
                    C.split_high(act, u)
                    C.full(act, u)
                    if m >= BUFS:
                        act.wait_ge(gused.sem, gused.at(m - BUFS))
                    act.activation(L.G[:, m % BUFS, :], C.bank[u.b][:], ACT.Silu).then_inc(C.bank_read[u.b], 1)
            for m in range(KD):
                gates.on_act(act, m)
    return gates


def stage_mem_attention(C, L):
    nc = C.nc
    H, D = 4, 256
    sc = [[C.take_bank() for _ in range(2)] + [C.take_bank() for _ in range(4)] for _ in range(H)]
    mx = C.reserve("mx", 2 * H)
    ex = C.reserve("ex", 4 * H)
    pn = C.reserve("pn", 4 * H)
    yh = C.reserve("yhigh", 2 * H)
    with nc.Block(no_gpsimd_drain=True) as block:
        @block.sync
        def _(sp):
            C.load_slabs(sp)

        @block.tensor
        def _(pe):
            def scores(h):
                for t in range(TC):
                    u = sc[h][t // 2]
                    if t % 2 == 0:
                        C.open(pe, u)
                    for d in range(2):
                        mm = pe.matmul(C.bank[u.b][:, t % 2 * MEM:t % 2 * MEM + MEM], L.Q[:, 2 * h + d, t * P:(t + 1) * P],
                                       L.K[:, 2 * h + d, :], start=(d == 0), stop=(d == 1))
                    if t % 2:
                        mm.then_inc(C.bank_full[u.b], 1)

            scores(0)
            for h in range(H):
                if h + 1 < H:
                    scores(h + 1)
                for mt in range(2):
                    u = sc[h][2 + mt]
                    C.open(pe, u)
                    for t in range(TC):
                        pe.wait_ge(pn.sem, pn.at(4 * h + t))
                        mm = pe.transpose(C.bank[u.b][:, t * P:(t + 1) * P], L.PR[:, t, mt * P:(mt + 1) * P], C.ident[:])
                    mm.then_inc(C.bank_full[u.b], 1)
                for d in range(2):
                    u = sc[h][4 + d]
                    C.open(pe, u)
                    for mt in range(2):
                        C.read(pe, sc[h][2 + mt])
                        a = h * D + d * P
                        mm = pe.matmul(C.bank[u.b][:], L.V[:, mt, a:a + P], L.PT[:, mt, :], start=(mt == 0), stop=(mt == 1))
                    mm.then_inc(C.bank_full[u.b], 1)

        @block.vector
        def _(dve):
            ln = C.vchain.link

            def low(h):
                for d in range(2):
                    u = sc[h][4 + d]
                    dve.wait_ge(yh.sem, yh.at(2 * h + d))
                    dve.tensor_tensor(L.Y.low[:, 2 * h + d, :], C.bank[u.b][:], L.Y.high[:, 2 * h + d, :].bitcast(F32),
                                      ALU.subtract).then_inc(C.bank_read[u.b], 1)

            for h in range(H):
                for t in (0, 2):
                    u = sc[h][t // 2]
                    C.full(dve, u)
                    ln(dve, dve.tensor_reduce(C.st[:, 0, t:t + 2], C.bank[u.b][:].rearrange("p (t m) -> p t m", t=2),
                                              AX.X, ALU.max))
                    dve.tensor_scalar(C.st[:, 1, t:t + 2], C.st[:, 0, t:t + 2], -(D ** -0.5), None, ALU.mult)\
                        .then_inc(mx.sem, 1)
                if h > 0:
                    low(h - 1)
                for t in range(TC):
                    dve.wait_ge(ex.sem, ex.at(4 * h + t))
                    ln(dve, dve.reciprocal(C.st[:, 3, t:t + 1], C.st[:, 2, t:t + 1]))
                    dve.tensor_scalar(L.PR[:, t, :], L.PR[:, t, :], C.st[:, 3, t:t + 1], None, ALU.mult)\
                        .then_inc(pn.sem, 1)
                for mt in range(2):
                    u = sc[h][2 + mt]
                    C.full(dve, u)
                    dve.tensor_copy(L.PT[:, mt, :], C.bank[u.b][:]).then_inc(C.bank_read[u.b], 1)
            low(H - 1)

        @block.scalar
        def _(act):
            for h in range(H):
                for t in range(TC):
                    u = sc[h][t // 2]
                    act.wait_ge(mx.sem, mx.at(2 * h + t // 2))
                    if h > 0:
                        C.full(act, sc[h - 1][3])
                    act.activation(L.PR[:, t, :], C.bank[u.b][:, t % 2 * MEM:t % 2 * MEM + MEM], ACT.Exp,
                                   bias=C.st[:, 1, t:t + 1], scale=D ** -0.5, accum_out=C.st[:, 2, t:t + 1])\
                        .then_inc(ex.sem, 1)
                    if t % 2:
                        act.wait_ge(ex.sem, ex.at(4 * h + t))
                        act.sem_inc(C.bank_read[u.b], 1)
                for d in range(2):
                    u = sc[h][4 + d]
                    C.full(act, u)
                    act.activation(L.Y.high[:, 2 * h + d, :], C.bank[u.b][:], ACT.Copy).then_inc(yh.sem, 1)


class Layout:
    pass


def add_into(C, dst):
    def evac(dve, i, bank):
        return dve.tensor_tensor(dst[:, i, :], dst[:, i, :], bank[:], ALU.add)
    return evac


def copy_to(dst, fn=ACT.Copy):
    def evac(act, i, bank):
        return act.activation(dst[:, i, :], bank[:, 0:dst.shape[2]], fn)
    return evac


def first_block(C):
    KB = 1024
    A = C.arena
    tiles = lambda buf, n: [buf[:, k, :] for k in range(n)]
    hk = C.H.tiles(KD)
    first = Norm(C, tiles(C.X, KD), lambda i: C.col("norm_g", i), DM, C.take_bank(), pair=C.H, keep=True)

    L = Layout()
    L.XS = C.at("xs", [P, 16, T], A)
    L.BC = C.at("bc", [P, 8, T], A + 32 * KB)
    L.SZ = C.at("silu_z", [P, 4, T], A + 48 * KB)
    L.PV = C.at("prev_state", [P, 3, T], A + 56 * KB)
    L.BT = C.at("b_tok", [P, T], C.X_OFF)
    L.CBM = C.at("cb_masked", [P, T], C.X_OFF + 2 * KB)
    L.DEC = C.at("decay", [P, 4, T], C.X_OFF + 4 * KB)
    L.DT = C.at("dt", [32, T], C.X_OFF + 12 * KB)
    L.ACS = C.at("acs", [32, T], C.X_OFF + 14 * KB)
    L.CE = C.at("c_exp", [P, 4, T], C.ROOT_OFF)
    small = A + 76 * KB
    L.END = C.at("acs_end", [32, P], small)
    L.DTT = C.at("dt_tok", [P, P], small + 512)
    L.ACST = C.at("acs_tok", [P, P], small + 1024)
    L.DTE = C.at("dt_end", [P, P], small + 1536)
    L.CD = C.at("chunk_decay", [P, P], small + 2048)
    L.AN = C.at("a_exp", [P, 1], small + 2560)
    L.S1, L.S2, L.S3, L.S4 = [C.at(f"dt_tmp{i}", [32, T], C.MG_OFF + 2 * KB * i) for i in range(4)]
    L.XDT = C.at("x_dt", [P, TC, T], C.MG_OFF)
    L.XDE = C.at("x_dt_end", [P, TC, T], C.MG_OFF + 8 * KB)
    L.E = C.at("rot", [P, NR, 2, T], A + 48 * KB)
    L.ET = C.at("rot_tmp", [P, 2, NR, T // 2], A + 64 * KB)
    stage_xbc(C, L, [0, 1], first)
    stage_ssd(C, L)
    XP = Pair(C.at("xs_high", [P, 16, T], A + 32 * KB, F32R), C.at("xs_low", [P, 16, T], A, F32R))
    gates = stage_norm(C, [[L.XS[:, 4 * g + j, :] for j in range(4)] for g in range(4)], lambda i: C.col("ssd_norm_g", i), 512,
               XP, with_gates=True)

    def table_room(at, tmp_at):
        L.E = C.at("rot", [P, NR, 2, T], at)
        L.ET = C.at("rot_tmp", [P, 2, NR, T // 2], tmp_at)

    table_room(A + 64 * KB, C.SQ_OFF)
    stage_merge(C, L, 0, XP.tiles(KS), [2], gates=gates)

    L = Layout()
    L.XL = C.at("lru_x", [P, KL, T], A)
    L.R = C.at("lru_r", [P, KL, T], A + 24 * KB)
    L.I = C.at("lru_i", [P, KL, T], A + 48 * KB)
    L.G = C.at("lru_g", [P, 4, T], A + 72 * KB)
    L.OUT = Pair(C.at("lru_high", [P, KL, T], A + 24 * KB, F32R), C.at("lru_low", [P, KL, T], A, F32R))
    L.SPA, L.SPB, L.SPC, L.SPD, L.SPE = [C.lru_tmp[:, i, :] for i in range(5)]
    table_room(C.X_OFF, C.SQ_OFF)
    gates = stage_lru(C, L)
    table_room(A + 64 * KB, C.SQ_OFF)
    M = C.at("mem", [P, KD, MEM], A + 48 * KB)
    mem_in = C.reserve("mem_loaded", 16)
    stage_merge(C, L, 1, L.OUT.tiles(KL), [5], gates=gates,
                load=lambda pool: pool.dma_start(M[:], C.io["memT"]).then_inc(mem_in.sem, 16))

    L = Layout()
    L.Y = Pair(C.at("mem_y_high", [P, KD, T], A, F32R), C.at("mem_y_low", [P, KD, T], A + 16 * KB, F32R))
    L.K = C.at("mem_k", [P, KD, MEM], A + 32 * KB)
    MP = Pair(C.at("mem_high", [P, KD, MEM], A + 40 * KB, F32R), C.at("mem_low", [P, KD, MEM], A + 48 * KB, F32R))
    L.V = C.at("mem_v", [P, 2, DM], A + 56 * KB)
    L.Q = C.at("mem_q", [P, KD, T], A + 64 * KB)
    L.PR = C.at("probs", [P, TC, MEM], A + 40 * KB)
    L.PT = C.at("probs_t", [P, 2, T], A + 44 * KB)
    mem_norm = Norm(C, [M[:, k, :] for k in range(KD)], lambda i: C.col("mem_norm_g", i), DM, C.take_bank(), pair=MP,
                    after=lambda act, i: act.wait_ge(mem_in.sem, mem_in.base + 16), w=MEM)
    table_room(C.X_OFF, A)
    stage_gemm(C, KD, hk, copy_to(L.Q), norms=[mem_norm], side=Side(pool=Tables(C, L, [6]).make))
    mk = MP.tiles(KD)
    stage_gemm(C, KD, mk, copy_to(L.K), n=MEM)
    stage_tokmajor(C, 4, mk, lambda half, t: L.V[:, t, half * 512:half * 512 + 512], 2)
    stage_mem_attention(C, L)
    table_room(A + 48 * KB, A + 64 * KB)
    MP = Pair(C.at("merged_high", [P, KD, T], A + 32 * KB, F32R), C.at("merged_low", [P, KD, T], C.MG_OFF, F32R))
    stage_merge(C, L, 2, L.Y.tiles(KD), [7], pair=MP)
    back = C.reserve("xback", 16)
    C.pinned = (7,)
    final = Norm(C, tiles(C.X, KD), lambda i: C.col("final_g", i), DM, C.take_given(7), early=True)
    stage_gemm(C, KD, MP.tiles(KD), add_into(C, C.X), "vector", stats=[(final, i) for i in range(KD)],
               side=Side(sync=lambda sp: sp.dma_start(C.X[:], C.io["xT"]).then_inc(back.sem, 16),
                         dve_first=lambda dve: dve.wait_ge(back.sem, back.base + 16), pool=lambda pool: load_s5(C, pool)))
    C.pinned = ()
    return final


def fetch(C, pool, pairs):
    ld = C.reserve("fetched", 16 * len(pairs))
    for dst, src in pairs:
        pool.dma_start(dst, src).then_inc(ld.sem, 16)
    return ld.sem, ld.base + 16 * len(pairs)


def pre_norm(C, last, layer):
    return [last, Norm(C, [C.X[:, k, :] for k in range(KD)], lambda i: C.col("pre_norm", KD * layer + i), DM, C.take_bank(),
                       root=1, pair=C.H, keep=True, after=last.done)]


NR = 4


class Tables:

    def __init__(self, C, L, batches):
        self.C, self.L, self.batches = C, L, batches
        self.kept = C.reserve("tables_kept", 16 * len(batches))

    def make(self, pool):
        for n, b in enumerate(self.batches):
            rotation_tables(self.C, pool, b, self.L.E, self.L.ET)
            pool.dma_start(self.C.io["rot"][NR * b:NR * b + NR].rearrange("j p a t -> p j (a t)"),
                           self.L.E[:].rearrange("p j a t -> p j (a t)")).then_inc(self.kept.sem, 16)
            pool.wait_ge(self.kept.sem, self.kept.base + 16 * (n + 1))


def s5_coefficients(C):
    nc = C.nc
    K = C.s5
    lr, li = C.col("lam_re", 0, 32), C.col("lam_im", 0, 32)
    two_pi = 2 * np.pi
    c1 = 6.28125
    c2 = float(np.float32(np.round((two_pi - c1) * 2 ** 20) / 2 ** 20))
    c3 = float(np.float32(two_pi - c1 - c2))
    magic = 1.5 * 2 ** 23
    sg = C.reserve("s5coef", 3)
    t = lambda i: K.tmp[:, i, :]
    def on_act(act):
        act.activation(t(0), C.col("log_dt", 0, 32), ACT.Exp).then_inc(sg.sem, 1)
        act.wait_ge(sg.sem, sg.at(1))
        C.achain.link(act, act.activation(K.mag[:], t(1), ACT.Exp))
        C.achain.link(act, act.activation(K.sin[:], t(2), ACT.Sin))
        act.activation(K.cos[:], t(3), ACT.Sin).then_inc(sg.sem, 1)

    def on_dve(dve):
        ln = lambda ins: C.vchain.link(dve, ins)
        tt, ts, stt = dve.tensor_tensor, dve.tensor_scalar, dve.scalar_tensor_tensor
        dve.wait_ge(sg.sem, sg.at(0))
        ln(tt(t(1), lr, t(0), ALU.mult))
        ln(tt(t(0), li, t(0), ALU.mult))
        ln(ts(t(3), t(0), 1.0 / two_pi, magic, ALU.mult, ALU.add))
        ln(ts(t(3), t(3), magic, None, ALU.subtract))
        for part in (c1, c2, c3):
            ln(stt(out=t(0), in0=t(3), scalar=-part, in1=t(0), op0=ALU.mult, op1=ALU.add))
        ln(ts(t(2), t(0), 3.1415925, -3.1415925, ALU.min, ALU.max))
        ln(stt(out=t(3), in0=t(2), scalar=-1.0, in1=t(2), op0=ALU.mult, op1=ALU.max))
        ts(t(3), t(3), -1.0, float(np.pi / 2), ALU.mult, ALU.add).then_inc(sg.sem, 1)
        dve.wait_ge(sg.sem, sg.at(2))
        ln(tt(t(0), K.mag[:], K.cos[:], ALU.mult))
        ln(ts(t(0), t(0), -1.0, None, ALU.add))
        ln(tt(t(1), K.mag[:], K.sin[:], ALU.mult))
        ln(tt(t(2), lr, lr, ALU.mult))
        ln(tt(t(3), li, li, ALU.mult))
        ln(tt(t(2), t(2), t(3), ALU.add))
        ln(dve.reciprocal(t(2), t(2)))
        ln(tt(K.fre[:], t(0), lr, ALU.mult))
        ln(tt(t(3), t(1), li, ALU.mult))
        ln(tt(K.fre[:], K.fre[:], t(3), ALU.add))
        ln(tt(K.fre[:], K.fre[:], t(2), ALU.mult))
        ln(tt(K.fim[:], t(1), lr, ALU.mult))
        ln(tt(t(3), t(0), li, ALU.mult))
        ln(tt(K.fim[:], K.fim[:], t(3), ALU.subtract))
        ln(tt(K.fim[:], K.fim[:], t(2), ALU.mult))
    return on_act, on_dve


def rotation_tables(C, pool, batch, E, tmp):
    K = C.s5
    js = slice(NR * batch, NR * batch + NR)
    s = [K.pw[:, i, :] for i in range(5)]
    tt = pool.tensor_tensor
    together = lambda *ops: C.gchain.together(pool, ops)
    together(pool.tensor_copy(s[0], K.cos[:, js]), pool.tensor_copy(s[1], K.sin[:, js]),
             pool.memset(E[:, :, 0, 0:1], 1.0), pool.memset(E[:, :, 1, 0:1], 0.0))
    w = 1
    while w < T:
        b = lambda a: a.unsqueeze(2).to_broadcast([P, NR, w])
        er, ei = E[:, :, 0, 0:w], E[:, :, 1, 0:w]
        nr, ni = E[:, :, 0, w:2 * w], E[:, :, 1, w:2 * w]
        t0, t1 = tmp[:, 0, :, 0:w], tmp[:, 1, :, 0:w]
        together(tt(nr, er, b(s[0]), ALU.mult), tt(t0, ei, b(s[1]), ALU.mult),
                 tt(ni, er, b(s[1]), ALU.mult), tt(t1, ei, b(s[0]), ALU.mult),
                 tt(s[2], s[0], s[0], ALU.mult), tt(s[3], s[1], s[1], ALU.mult), tt(s[4], s[0], s[1], ALU.mult))
        together(tt(nr, nr, t0, ALU.subtract), tt(ni, ni, t1, ALU.add),
                 tt(s[0], s[2], s[3], ALU.subtract), tt(s[1], s[4], s[4], ALU.add))
        w *= 2


def s5_places(C):
    KB, A = 1024, C.arena
    L = Layout()
    L.BL = C.at("s5_b", [P, 2, 8, P], A)
    L.CP = C.at("s5_c", [P, 2, 32, 32], A + 8 * KB)
    L.Z = C.at("s5_z", [P, 2, 32, 32], A + 16 * KB)
    L.BB = C.at("s5_bb", [P, 3, 32, 16], A + 24 * KB)
    L.BI = C.at("s5_bi", [P, 2, 32, 16], A + 48 * KB)
    L.W = C.at("s5_work", [P, 4, 4, T], A + 16 * KB)
    L.TB = C.at("s5_tables", [P, 4, 2, T], A + 48 * KB)
    return L


def load_s5(C, pool):
    C.s5_at = s5_places(C)
    pool.wait_ge(*fetch(C, pool, [(C.s5_at.BI[:], C.io["s5_b"]), (C.s5_at.CP[:], C.io["s5_c"])]))
    C.gchain.link(pool, pool.memset(C.s5_at.Z[:], 0.0))
    pool.sem_inc(C.reserve("s5_loaded", 1).sem, 1)


def s5_b(C, L):
    K = C.s5
    us = [C.take_given(6 + n % 2) for n in range(4)]
    zd = C.reserve("s5z", 2)
    ready = C.totals["s5_loaded"]

    def spread(dve):
        ln = lambda ins: C.vchain.link(dve, ins)
        dve.wait_ge(ready.sem, ready.total)
        f = [a[:].unsqueeze(2).to_broadcast([P, 32, 16]) for a in (K.fre, K.fim)]
        ln(dve.tensor_tensor(L.BB[:, 0], L.BI[:, 0], f[0], ALU.mult))
        ln(dve.tensor_tensor(L.BB[:, 2], L.BI[:, 1], f[1], ALU.mult))
        ln(dve.tensor_tensor(L.BB[:, 0], L.BB[:, 0], L.BB[:, 2], ALU.subtract))
        ln(dve.tensor_tensor(L.BB[:, 1], L.BI[:, 1], f[0], ALU.mult))
        ln(dve.tensor_tensor(L.BB[:, 2], L.BI[:, 0], f[1], ALU.mult))
        ln(dve.tensor_tensor(L.BB[:, 1], L.BB[:, 1], L.BB[:, 2], ALU.add))
        for part in range(2):
            for e in range(2):
                r = slice(64 * e, 64 * e + 64)
                ln(dve.tensor_copy(L.Z[r, part, :, 16 * e:16 * e + 16], L.BB[r, part]))
            dve.sem_inc(zd.sem, 1)

    def read_out(dve):
        for n, u in enumerate(us):
            C.full(dve, u)
            dve.tensor_copy(L.BL[:, n // 2, n % 2 * 4:n % 2 * 4 + 4, :].rearrange("p j c -> p (j c)"), C.bank[u.b][:])\
                .then_inc(C.bank_read[u.b], 1)

    def transposes(pe):
        for n, u in enumerate(us):
            C.open(pe, u)
            pe.wait_ge(zd.sem, zd.at(n // 2))
            for q in range(4):
                a = n % 2 * 4 + q
                t = pe.transpose(C.bank[u.b][:, q * P:(q + 1) * P],
                                 L.Z[:, n // 2, 4 * a:4 * a + 4, :].rearrange("p b c -> p (b c)"), C.ident[:])
            t.then_inc(C.bank_full[u.b], 1)

    return Side({KD - 1: transposes}, dve_first=spread, dve_last=read_out)


def stage_s5_scan(C, L):
    nc = C.nc
    K = C.s5
    NT, NS = 32, 4
    bu, yb, zt = [], [], []
    for j in range(NT):
        if j % 4 == 0:
            yb.append(C.take_given(j // 4 % 2))
        bu.append([C.take_given(2 + (2 * j + part) % 5) for part in range(2)])
        if j % 4 == 1:
            u = C.take_given(7)
            zt.append((u, C.take_blocks(KD, u)))
    sgn = lambda n, k=1: C.reserve(n, NT * k)
    tb = [C.reserve(f"table{b}", 16 * NT // 4) for b in range(4)]
    pre, add, post, fin, outp = sgn("pre", 4), sgn("padd", 2), sgn("post", 5), sgn("fin", 2), sgn("outp", 3)
    neg = C.reserve("negc", 1)
    with nc.Block(no_gpsimd_drain=True) as block:
        @block.sync
        def _(sp):
            C.load_slabs(sp)

        def rows(j):
            return slice(32 * (j % 4), 32 * (j % 4) + 32)

        @block.tensor
        def _(pe):
            def inputs(j):
                for part in range(2):
                    u = bu[j][part]
                    C.open(pe, u)
                    pe.matmul(C.bank[u.b][:], L.BL[rows(j), part, j // 4, :], C.MG[rows(j), j // 4, :], start=True,
                              stop=True)\
                        .then_inc(C.bank_full[u.b], 1)

            seen = set()
            for j in range(4):
                inputs(j)
            pe.wait_ge(neg.sem, neg.at(0))
            for j in range(NT):
                if j + 4 < NT:
                    inputs(j + 4)
                if j % 4 == 1:
                    C.gemm(pe, zt[j // 4], C.H.tiles(KD), seen)
                u = yb[j // 4]
                if j % 4 == 0:
                    C.open(pe, u)
                pe.wait_ge(fin.sem, fin.at(2 * j + 1))
                for n, (part, w) in enumerate(((1, 1), (1, 3), (0, 0))):
                    pe.matmul(C.bank[u.b][rows(j), :], L.CP[:, part, j, :], L.W[:, j % NS, w], start=(n == 0),
                              stop=(n == 2)).then_inc(outp.sem, 1)
                if j % 4 == 3:
                    pe.wait_ge(outp.sem, outp.at(3 * j + 2))
                    pe.sem_inc(C.bank_full[u.b], 1)

        @block.vector
        def _(dve):
            for j in range(NT + 3):
                if j < NT:
                    W, (cs, sn) = L.W[:, j % NS], (L.TB[:, j % 4, 0], L.TB[:, j % 4, 1])
                    dve.wait_ge(tb[j % 4].sem, tb[j % 4].base + 16 * (j // 4 + 1))
                    if j >= NS:
                        dve.wait_ge(outp.sem, outp.at(3 * (j - NS) + 2))
                    C.full(dve, bu[j][0])
                    C.full(dve, bu[j][1])
                    re, im = C.bank[bu[j][0].b], C.bank[bu[j][1].b]
                    dve.tensor_tensor(W[:, 0], cs, re[:], ALU.mult).then_inc(pre.sem, 1)
                    dve.tensor_tensor(W[:, 1], sn, im[:], ALU.mult).then_inc(pre.sem, 1)
                    dve.tensor_tensor(W[:, 2], cs, im[:], ALU.mult).then_inc(pre.sem, 1)
                    dve.tensor_tensor(W[:, 3], sn, re[:], ALU.mult).then_inc(pre.sem, 1)
                    dve.wait_ge(pre.sem, pre.at(4 * j + 3))
                    dve.sem_inc(C.bank_read[bu[j][0].b], 1)
                    dve.sem_inc(C.bank_read[bu[j][1].b], 1)
                if 0 < j <= NT:
                    i = j - 1
                    W, (cs, sn) = L.W[:, i % NS], (L.TB[:, i % 4, 0], L.TB[:, i % 4, 1])
                    mag = K.mag[:, i:i + 1].to_broadcast([P, T])
                    dve.wait_ge(add.sem, add.at(2 * i))
                    dve.tensor_tensor_scan(W[:, 1], mag, W[:, 0], 0.0, ALU.mult, ALU.add).then_inc(post.sem, 1)
                    dve.wait_ge(add.sem, add.at(2 * i + 1))
                    dve.tensor_tensor_scan(W[:, 3], mag, W[:, 2], 0.0, ALU.mult, ALU.add).then_inc(post.sem, 1)
                    dve.wait_ge(post.sem, post.at(5 * i + 1))
                    dve.tensor_tensor(W[:, 0], cs, W[:, 1], ALU.mult).then_inc(post.sem, 1)
                    dve.tensor_tensor(W[:, 2], sn, W[:, 3], ALU.mult).then_inc(post.sem, 1)
                    dve.wait_ge(post.sem, post.at(5 * i + 2))
                    dve.tensor_tensor(W[:, 1], W[:, 1], sn, ALU.mult).then_inc(post.sem, 1)
                if j % 4 == 1 and j >= 5:
                    C.split_low(dve, zt[(j - 5) // 4][0])
                if j > 2:
                    i = j - 3
                    if i % 4 == 3:
                        u = yb[i // 4]
                        C.full(dve, u)
                        m = C.MG[:, i // 4, :]
                        dve.scalar_tensor_tensor(out=m, in0=m, scalar=C.col("a_d", i // 4), in1=C.bank[u.b][:],
                                                 op0=ALU.mult, op1=ALU.add).then_inc(C.bank_read[u.b], 1)

        @block.gpsimd
        def _(pool):
            for j in range(NT + 2):
                if j < NT:
                    W = L.W[:, j % NS]
                    pool.wait_ge(pre.sem, pre.at(4 * j + 1))
                    pool.tensor_tensor(W[:, 0], W[:, 0], W[:, 1], ALU.add).then_inc(add.sem, 1)
                    pool.wait_ge(pre.sem, pre.at(4 * j + 3))
                    pool.tensor_tensor(W[:, 2], W[:, 2], W[:, 3], ALU.subtract).then_inc(add.sem, 1)
                if j > 1:
                    i = j - 2
                    W, cs = L.W[:, i % NS], L.TB[:, i % 4, 0]
                    pool.wait_ge(post.sem, post.at(5 * i + 4))
                    pool.tensor_tensor(W[:, 3], W[:, 3], cs, ALU.mult).then_inc(fin.sem, 1)
                    pool.tensor_tensor(W[:, 0], W[:, 0], W[:, 2], ALU.subtract).then_inc(fin.sem, 1)

        @block.scalar
        def _(act):
            act.activation(L.CP[:, 1], L.CP[:, 1], ACT.Copy, scale=-1.0).then_inc(neg.sem, 1)
            for j in range(NT + 7):
                if j < NT:
                    if j >= 4:
                        act.wait_ge(fin.sem, fin.at(2 * (j - 4) + 1))
                    act.dma_start(L.TB[:, j % 4], C.io["rot"][j]).then_inc(tb[j % 4].sem, 16)
                if j % 4 == 1 and 5 <= j < NT + 5:
                    i = (j - 5) // 4
                    u = zt[i][0]
                    C.split_high(act, u)
                    C.full(act, u)
                    act.activation(C.zbuf[:, i, :], C.bank[u.b][:], ACT.Copy).then_inc(C.bank_read[u.b], 1)
                if j % 4 == 3 and j >= 7:
                    i = (j - 7) // 4
                    C.read(act, yb[i])
                    act.activation(C.MG[:, i, :], C.MG[:, i, :], ACT.Gelu_apprx_tanh)


def branch_s5(C, last):
    KB, A = 1024, C.arena
    L = C.s5_at
    C.zbuf = C.at("z", [P, KD, T], A + 64 * KB)
    norms = pre_norm(C, last, 0)
    C.pinned = (6, 7)
    stage_gemm(C, KD, C.H.tiles(KD), copy_to(C.MG), norms=norms, side=s5_b(C, L))
    C.pinned = ()
    stage_s5_scan(C, L)
    L = Layout()
    L.G = Pair(C.at("gelu_high", [P, KD, T], A, F32R), C.at("gelu_low", [P, KD, T], A + 16 * KB, F32R))
    L.Y = C.at("s5_y", [P, KD, T], A + 32 * KB)
    done = C.reserve("glusplit", KD)

    def split_all(dve):
        for k in range(KD):
            split_tile(C, dve, C.MG[:, k, :], L.G.tile(k)).then_inc(done.sem, 1)

    def glu(act, i, bank):
        return act.activation(L.Y[:, i, :], bank[:], ACT.Sigmoid, bias=C.col("b_glu", i))

    def glu_mul(dve, i):
        return dve.tensor_tensor(L.Y[:, i, :], L.Y[:, i, :], C.MG[:, i, :], ALU.mult)
    stage_gemm(C, KD, L.G.tiles(KD), glu, then=glu_mul,
               side=Side(dve_first=split_all, ready=lambda pe, k: pe.wait_ge(done.sem, done.at(k))))
    return gated_output(C, L.Y, A + 32 * KB, A, C.zbuf, 0)


def gated_output(C, Y, at, high_at, Z, layer):
    YP = Pair(C.at("gated_high", [P, KD, T], high_at, F32R), C.at("gated_low", [P, KD, T], at, F32R))
    C.pinned = (7,)
    tiles = [C.take_tile(KD) for _ in range(KD)]
    C.pinned = ()
    post = Norm(C, [Z[:, k, :] for k in range(KD)], lambda i: C.col("post_norm", KD * layer + i), DM, C.take_given(7),
                add=lambda i: C.X[:, i, :], early=True)
    act_done, mul, high, gated = [C.reserve(n, KD) for n in ("zsilu", "gmul", "ghigh", "gated")]
    with C.nc.Block(no_gpsimd_drain=True) as block:
        @block.sync
        def _(sp):
            C.load_slabs(sp)

        @block.tensor
        def _(pe):
            seen = set()
            for i, t in enumerate(tiles):
                ready = (lambda k: pe.wait_ge(gated.sem, gated.at(k))) if i == 0 else None
                C.gemm(pe, t, YP.tiles(KD), seen, ready=ready)
                if i > 0:
                    post.sum(pe, i - 1)
            post.sum(pe, KD - 1)

        @block.vector
        def _(dve):
            for k in range(KD + 1):
                if k < KD:
                    dve.wait_ge(act_done.sem, act_done.at(k))
                    dve.tensor_tensor(Y[:, k, :], Y[:, k, :], Z[:, k, :], ALU.mult).then_inc(mul.sem, 1)
                if k > 0:
                    dve.wait_ge(high.sem, high.at(k - 1))
                    dve.tensor_tensor(YP.low[:, k - 1, :], Y[:, k - 1, :], YP.high[:, k - 1, :].bitcast(F32), ALU.subtract)\
                        .then_inc(gated.sem, 1)
            for u, _ in tiles:
                C.split_low(dve, u)

        @block.scalar
        def _(act):
            for k in range(KD + 1):
                if k < KD:
                    act.activation(Z[:, k, :], Z[:, k, :], ACT.Silu).then_inc(act_done.sem, 1)
                if k > 0:
                    act.wait_ge(mul.sem, mul.at(k - 1))
                    act.activation(YP.high[:, k - 1, :], Y[:, k - 1, :], ACT.Copy).then_inc(high.sem, 1)
            for i, (u, _) in enumerate(tiles):
                C.split_high(act, u)
                C.full(act, u)
                act.activation(Z[:, i, :], C.bank[u.b][:], ACT.Copy).then_inc(C.bank_read[u.b], 1)
                C.read(act, u)
                post.square(act, i)
    return post


def swa_bias(C, L):
    u = C.take_given(7)
    s = C.reserve("swab", 16 * 2)
    ld = C.reserve("swa_loaded", 16 * 3)
    made = C.reserve("bias_made", 1)

    def product(pe):
        C.open(pe, u)
        pe.wait_ge(ld.sem, ld.base + 48)
        pe.matmul(C.bank[u.b][0:16, 0:384], L.RB[:], L.OH[:], start=True, stop=True).then_inc(C.bank_full[u.b], 1)

    def pool_part(pool):
        for dst, src in ((L.RB, C.io["rel_bias"]), (L.OH, C.io["bucket_onehot"]), (L.NR, C.io["neg_row"])):
            pool.dma_start(dst[:], src).then_inc(ld.sem, 16)
        C.read(pool, u)
        pool.wait_ge(ld.sem, ld.base + 48)
        pool.tensor_tensor(L.BV[:], L.BV[:], L.NR[:], ALU.add).then_inc(made.sem, 1)
        pool.wait_ge(made.sem, made.at(0))
        scr = C.io["bias_rows"]
        pool.dma_start(scr, L.BV[:].unsqueeze(1).to_broadcast([16, P, 384])).then_inc(s.sem, 16)
        pool.wait_ge(s.sem, s.base + 16)
        skewed = bass.AP(tensor=scr.tensor, offset=127, ap=[[383, P], [P * 384, 16], [1, 256]])
        pool.dma_start(L.BT[:], skewed).then_inc(s.sem, 16)

    def copy(act):
        C.full(act, u)
        act.activation(L.BV[:], C.bank[u.b][0:16, 0:384], ACT.Copy).then_inc(C.bank_read[u.b], 1)

    return Side({1: product}, pool=pool_part, act={1: copy}, dve_last=lambda dve: dve.wait_ge(s.sem, s.base + 32))


def stage_swa(C, L):
    nc = C.nc
    NJ = 8
    sb, pb, ob, zb = [[C.take_bank() for _ in range(TC)] for _ in range(2)], [], [], []
    for j in range(NJ):
        pb.append([C.take_bank() for _ in range(TC)])
        if j + 2 < NJ:
            sb.append([C.take_bank() for _ in range(TC)])
        zb.append(C.take_tile(KD))
        ob.append(C.take_bank())
    mx, ex, pn = C.reserve("mx", NJ), C.reserve("ex", NJ), C.reserve("pn", NJ)
    zr = C.reserve("swaz", 1)
    with nc.Block(no_gpsimd_drain=True) as block:
        @block.sync
        def _(sp):
            C.load_slabs(sp)

        @block.tensor
        def _(pe):
            def scores(j):
                for b, u in enumerate(sb[j]):
                    e = b // 2
                    C.open(pe, u)
                    for n in (2 * (b % 2), 2 * (b % 2) + 1):
                        lo = 0 if n else P
                        r = slice(64 * e, 64 * e + 64)
                        mm = pe.matmul(C.bank[u.b][:, n % 2 * 256 + lo:n % 2 * 256 + 256], L.Q[r, j, n * P:(n + 1) * P],
                                       L.K[r, 0, (n - 1) * P + lo:(n + 1) * P], start=True, stop=True)
                    mm.then_inc(C.bank_full[u.b], 1)

            seen = set()
            scores(0)
            scores(1)
            for j in range(NJ):
                pe.wait_ge(pn.sem, pn.at(j))
                for n, u in enumerate(pb[j]):
                    C.open(pe, u)
                    for e in range(2):
                        for kt in range(0 if n else 1, 2):
                            a = (2 * e + kt) * P
                            mm = pe.transpose(C.bank[u.b][:, a:a + P], L.S[:, j % 2, n, e, kt * P:(kt + 1) * P], C.ident[:])
                    mm.then_inc(C.bank_full[u.b], 1)
                if j + 2 < NJ:
                    scores(j + 2)
                C.gemm(pe, zb[j], C.H.tiles(KD), seen)
                u = ob[j]
                C.open(pe, u)
                for n in range(TC):
                    C.read(pe, pb[j][n])
                    for e in range(2):
                        first = 0 if n else 1
                        for kt in range(first, 2):
                            a = (2 * e + kt) * P
                            mm = pe.matmul(C.bank[u.b][64 * e:64 * e + 64, n * P:(n + 1) * P],
                                           L.V[:, n - 1 + kt, 64 * e:64 * e + 64], L.PT[:, n, a:a + P],
                                           start=(kt == first), stop=(kt == 1))
                mm.then_inc(C.bank_full[u.b], 1)

        @block.vector
        def _(dve):
            ln = lambda ins: C.vchain.link(dve, ins)

            def logits(j):
                if j >= 2:
                    C.full(dve, pb[j - 2][3])
                st = L.ST[:, j % 2]
                for b, u in enumerate(sb[j]):
                    e = b // 2
                    C.full(dve, u)
                    for n in (2 * (b % 2), 2 * (b % 2) + 1):
                        lo = 0 if n else P
                        ins = dve.scalar_tensor_tensor(
                            out=L.S[:, j % 2, n, e, lo:256], in0=C.bank[u.b][:, n % 2 * 256 + lo:n % 2 * 256 + 256],
                            scalar=64 ** -0.5, in1=L.BT[:, j + 8 * e, lo:256], op0=ALU.mult, op1=ALU.add)
                    ins.then_inc(C.bank_read[u.b], 1)
                for u in sb[j]:
                    C.read(dve, u)
                ln(dve.tensor_reduce(st[:, 0, 0, :], L.S[:, j % 2, 0, :, P:256], AX.X, ALU.max))
                ln(dve.tensor_reduce(st[:, 0, 1:4, :], L.S[:, j % 2, 1:4], AX.X, ALU.max))
                sink = C.col("sinks", 0, 16)[:, j::8].unsqueeze(1).to_broadcast([P, TC, 2])
                ln(dve.tensor_tensor(st[:, 0], st[:, 0], sink, ALU.max))
                ln(dve.tensor_tensor(st[:, 1], sink, st[:, 0], ALU.subtract))
                dve.tensor_scalar(st[:, 0], st[:, 0], -1.0, None, ALU.mult).then_inc(mx.sem, 1)

            def probs(j):
                st = L.ST[:, j % 2]
                dve.wait_ge(ex.sem, ex.at(j))
                ln(dve.tensor_tensor(st[:, 2], st[:, 2], st[:, 1], ALU.add))
                ln(dve.reciprocal(st[:, 2], st[:, 2]))
                r = st[:, 2].rearrange("p n e -> p (n e)").unsqueeze(2).to_broadcast([P, 8, 256])
                s = L.S[:, j % 2].rearrange("p n e k -> p (n e) k")
                dve.tensor_tensor(s, s, r, ALU.mult).then_inc(pn.sem, 1)

            for b in range(2):
                ln(dve.memset(L.S[:, b, 0, :, 0:P], 0.0))
            dve.sem_inc(zr.sem, 1)
            logits(0)
            logits(1)
            probs(0)
            for j in range(NJ):
                if j + 1 < NJ:
                    probs(j + 1)
                if j + 2 < NJ:
                    logits(j + 2)
            C.lows_done(dve, [u for u, _ in zb])

        @block.gpsimd
        def _(pool):
            for u, _ in zb:
                C.split_low(pool, u)

        @block.scalar
        def _(act):
            def exps(j):
                st = L.ST[:, j % 2]
                act.wait_ge(mx.sem, mx.at(j))
                act.activation(st[:, 1], st[:, 1], ACT.Exp)
                for n in range(TC):
                    lo = 0 if n else P
                    for e in range(2):
                        s = L.S[:, j % 2, n, e, lo:256]
                        ins = act.activation(s, s, ACT.Exp, bias=st[:, 0, n, e:e + 1], accum_out=st[:, 2, n, e:e + 1])
                ins.then_inc(ex.sem, 1)

            exps(0)
            exps(1)
            for j in range(NJ):
                if j > 0:
                    C.full(act, ob[j - 1])
                    act.activation(L.Y[:, j - 1, :], C.bank[ob[j - 1].b][:], ACT.Copy).then_inc(C.bank_read[ob[j - 1].b], 1)
                for n, u in enumerate(pb[j]):
                    C.full(act, u)
                    lo = 0 if n else 1
                    v = lambda ap: ap.rearrange("p (e t k) -> p e t k", e=2, t=2)[:, :, lo:2, :]
                    act.activation(v(L.PT[:, n, :]), v(C.bank[u.b][:]), ACT.Copy).then_inc(C.bank_read[u.b], 1)
                if j + 2 < NJ:
                    exps(j + 2)
                C.split_high(act, zb[j][0])
                C.full(act, zb[j][0])
                act.activation(L.Z[:, j, :], C.bank[zb[j][0].b][:], ACT.Copy).then_inc(C.bank_read[zb[j][0].b], 1)
            C.full(act, ob[NJ - 1])
            act.activation(L.Y[:, NJ - 1, :], C.bank[ob[NJ - 1].b][:], ACT.Copy).then_inc(C.bank_read[ob[NJ - 1].b], 1)


def branch_swa(C, last):
    KB, A = 1024, C.arena
    L = Layout()
    L.Q = C.at("swa_q", [P, KD, T], A)
    L.Y = C.at("swa_y", [P, KD, T], A + 16 * KB)
    L.K = C.at("swa_k", [P, 1, T], A + 32 * KB)
    L.V = C.at("swa_v", [P, TC, P], A + 34 * KB)
    L.BT = C.at("swa_bias", [P, 16, 256], A + 36 * KB)
    L.S = C.at("swa_s", [P, 2, TC, 2, 256], A + 52 * KB)
    L.PT = C.at("swa_pt", [P, TC, T], C.SQ_OFF)
    L.Z = C.at("swa_z", [P, KD, T], C.MG_OFF)
    L.ST = C.at("swa_st", [P, 2, 3, TC, 2], A + 68 * KB)
    L.RB = C.at("rel_bias", [32, 16], A + 69 * KB)
    L.OH = C.at("bucket_onehot", [32, 384], A + 70 * KB)
    L.NR = C.at("neg_row", [16, 384], A + 72 * KB)
    L.BV = C.at("bias_row", [16, 384], A + 74 * KB)
    hk = C.H.tiles(KD)
    norms = pre_norm(C, last, 1)
    C.pinned = (7,)
    stage_gemm(C, KD, hk, copy_to(L.Q), norms=norms, side=swa_bias(C, L))
    C.pinned = ()
    stage_gemm(C, 1, hk, copy_to(L.K))
    stage_tokmajor(C, 1, hk, lambda half, t: L.V[:, t, :], TC)
    stage_swa(C, L)
    return gated_output(C, L.Y, A + 16 * KB, A, L.Z, 1)


def stage_mla(C, L):
    nc = C.nc
    H = 16
    SC = 96 ** -0.5
    kb, sb, pb, ob, zb = [], [], [], [], []

    def take_scores(h):
        if h % 2 == 0:
            kb.append(C.take_tile(2))
        sb.append([C.take_bank() for _ in range(TC)])

    C.pinned = (7,)
    take_scores(0)
    take_scores(1)
    for h in range(H):
        pb.append([C.take_bank() for _ in range(TC)])
        if h + 2 < H:
            take_scores(h + 2)
        if h % 2 == 0:
            zb.append(C.take_tile(KD))
        if h % 2 == 0:
            ob.append(C.take_given(7))
    C.pinned = ()
    mx, ex, pn = C.reserve("mx", TC * H), C.reserve("ex", H), C.reserve("pn", H)
    kt_, pvd, scd = C.reserve("ktile", 2 * 8 + 4), C.reserve("pvd", H), C.reserve("scd", H)
    K0 = 4
    with nc.Block(no_gpsimd_drain=True) as block:
        @block.sync
        def _(sp):
            C.load_slabs(sp)

        @block.tensor
        def _(pe):
            seen = set()

            def scores(h):
                if h % 2 == 0:
                    C.gemm(pe, kb[h // 2], L.KV.tiles(2), seen)
                pe.wait_ge(kt_.sem, kt_.at(K0 + h))
                for i, u in enumerate(sb[h]):
                    C.open(pe, u)
                    mm = pe.matmul(C.bank[u.b][:, 0:(i + 1) * P], L.Q[:, h, i * P:(i + 1) * P], L.K[:, h % 4, 0:(i + 1) * P],
                                   start=True, stop=True)
                    mm.then_inc(C.bank_full[u.b], 1)

            scores(0)
            scores(1)
            for h in range(H):
                pe.wait_ge(pn.sem, pn.at(h))
                for kt, u in enumerate(pb[h]):
                    C.open(pe, u)
                    for i in range(kt, TC):
                        mm = pe.transpose(C.bank[u.b][:, i * P:(i + 1) * P], L.S[:, h % 2, i, kt * P:(kt + 1) * P], C.ident[:])
                    mm.then_inc(C.bank_full[u.b], 1)
                if h + 2 < H:
                    scores(h + 2)
                if h % 2 == 0:
                    C.gemm(pe, zb[h // 2], C.H.tiles(KD), seen)
                u = ob[h // 2]
                if h % 2 == 0:
                    C.open(pe, u)
                e = h % 2
                for kt in range(TC):
                    C.read(pe, pb[h][kt])
                    mm = pe.matmul(C.bank[u.b][64 * e:64 * e + 64, kt * P:T], L.V[:, kt, 64 * h:64 * h + 64],
                                   L.PT[:, kt, kt * P:T], start=(kt == 0), stop=(kt == TC - 1))
                mm.then_inc(pvd.sem, 1)
                if e:
                    pe.wait_ge(pvd.sem, pvd.at(h))
                    pe.sem_inc(C.bank_full[u.b], 1)

        @block.vector
        def _(dve):
            ln = lambda ins: C.vchain.link(dve, ins)

            def logits(h):
                if h >= 2:
                    C.full(dve, pb[h - 2][3])
                st = L.ST[:, h % 2]
                for i, u in enumerate(sb[h]):
                    C.full(dve, u)
                    w = (i + 1) * P
                    dve.scalar_tensor_tensor(out=L.S[:, h % 2, i, 0:w], in0=C.bank[u.b][:, 0:w], scalar=SC,
                                             in1=L.MB[:, T - w:T], op0=ALU.mult, op1=ALU.add).then_inc(C.bank_read[u.b], 1)
                for i, u in enumerate(sb[h]):
                    C.read(dve, u)
                    ln(dve.tensor_reduce(st[:, 0, i:i + 1], L.S[:, h % 2, i, 0:(i + 1) * P], AX.X, ALU.max))
                    dve.tensor_scalar(st[:, 0, i:i + 1], st[:, 0, i:i + 1], -1.0, None, ALU.mult).then_inc(mx.sem, 1)

            def probs(h):
                st = L.ST[:, h % 2]
                dve.wait_ge(ex.sem, ex.at(h))
                ln(dve.reciprocal(st[:, 1], st[:, 1]))
                for i in range(TC):
                    s = L.S[:, h % 2, i, 0:(i + 1) * P]
                    ins = dve.tensor_scalar(s, s, st[:, 1, i:i + 1], None, ALU.mult)
                ins.then_inc(pn.sem, 1)

            logits(0)
            logits(1)
            probs(0)
            for h in range(H):
                for kt in (1, 3):
                    u = pb[h][kt]
                    C.full(dve, u)
                    dve.tensor_copy(L.PT[:, kt, kt * P:T], C.bank[u.b][:, kt * P:T]).then_inc(C.bank_read[u.b], 1)
                if h + 1 < H:
                    probs(h + 1)
                if h + 2 < H:
                    logits(h + 2)
            C.lows_done(dve, [u for u, _ in kb + zb])

        @block.gpsimd
        def _(pool):
            for b in range(4):
                r = slice(64, P) if b % 2 == 0 else slice(0, 64)
                pool.tensor_copy(L.K[r, b, :], L.KR[r, :]).then_inc(kt_.sem, 1)
            C.split_low(pool, kb[0][0])
            for k, z in zip(kb[1:] + [None], zb):
                if k is not None:
                    C.split_low(pool, k[0])
                C.split_low(pool, z[0])

        @block.scalar
        def _(act):
            def keys(h):
                u = kb[h // 2][0]
                C.split_high(act, u)
                C.full(act, u)
                if h == 0:
                    act.wait_ge(kt_.sem, kt_.at(3))
                if h >= 4:
                    C.full(act, sb[h - 3][3])
                for e in range(2):
                    r = slice(64 * e, 64 * e + 64)
                    act.activation(L.K[r, (h + e) % 4, :], C.bank[u.b][r, :], ACT.Copy).then_inc(kt_.sem, 1)
                act.wait_ge(kt_.sem, kt_.at(K0 + h + 1))
                act.sem_inc(C.bank_read[u.b], 1)

            def exps(h):
                st = L.ST[:, h % 2]
                for i in range(TC):
                    act.wait_ge(mx.sem, mx.at(TC * h + i))
                    s = L.S[:, h % 2, i, 0:(i + 1) * P]
                    ins = act.activation(s, s, ACT.Exp, bias=st[:, 0, i:i + 1], accum_out=st[:, 1, i:i + 1])
                ins.then_inc(ex.sem, 1)

            keys(0)
            exps(0)
            exps(1)
            for h in range(H):
                if h > 0:
                    act.wait_ge(pvd.sem, pvd.at(h - 1))
                if h > 0 and h % 2 == 0:
                    u = ob[h // 2 - 1]
                    C.full(act, u)
                    act.activation(L.Y[:, h // 2 - 1, :], C.bank[u.b][:], ACT.Copy).then_inc(C.bank_read[u.b], 1)
                for kt in (0, 2):
                    u = pb[h][kt]
                    C.full(act, u)
                    act.activation(L.PT[:, kt, kt * P:T], C.bank[u.b][:, kt * P:T], ACT.Copy).then_inc(C.bank_read[u.b], 1)
                if h + 2 < H:
                    if h % 2 == 0:
                        keys(h + 2)
                    exps(h + 2)
                if h % 2 == 0:
                    u = zb[h // 2][0]
                    C.split_high(act, u)
                    C.full(act, u)
                    act.activation(L.Z[:, h // 2, :], C.bank[u.b][:], ACT.Copy).then_inc(C.bank_read[u.b], 1)
            u = ob[7]
            C.full(act, u)
            act.activation(L.Y[:, 7, :], C.bank[u.b][:], ACT.Copy).then_inc(C.bank_read[u.b], 1)


def branch_mla(C, last):
    KB, A = 1024, C.arena
    L = Layout()
    L.Q = C.at("mla_q", [P, 16, T], A)
    L.V = C.at("mla_v", [P, TC, DM], A + 32 * KB)
    L.K = C.at("mla_k", [P, 4, T], A + 48 * KB)
    L.KR = C.at("mla_kr", [P, T], A + 56 * KB)
    L.RT = C.at("rope_tables", [P, 4, T], A + 58 * KB)
    L.T = C.at("mla_t", [P, T], A + 66 * KB)
    L.S = C.at("mla_s", [P, 2, TC, T], A + 58 * KB)
    L.MB = C.at("causal_bias", [P, T], A + 74 * KB)
    L.KV = Pair(C.at("kv_high", [P, 2, T], A + 76 * KB, F32R), C.at("kv_low", [P, 2, T], C.ROOT_OFF + 4 * KB, F32R))
    L.PT = C.at("mla_pt", [P, TC, T], C.SQ_OFF)
    L.ST = C.at("mla_st", [P, 2, 2, TC], C.ROOT_OFF)
    QP = Pair(C.at("q_latent_high", [P, 6, T], A + 32 * KB, F32R), C.at("q_latent_low", [P, 6, T], C.MG_OFF, F32R))
    hk = C.H.tiles(KD)
    norms = pre_norm(C, last, 2)
    ml = C.reserve("mla_loaded", 32)

    def load_tables(pool):
        for dst, src in ((L.RT, C.io["rope"]), (L.MB, C.io["causal"])):
            pool.dma_start(dst[:], src).then_inc(ml.sem, 16)
    C.pinned = (6, 7)
    latents = [C.MG[:, k, :] for k in range(KD)]
    qn = Norm(C, latents[:6], lambda i: C.col("q_norm", i), 768, C.take_given(7), pair=QP, early=True)
    kvn = Norm(C, latents[6:], lambda i: C.col("kv_norm", i), 256, C.take_given(6), root=1, pair=L.KV, early=True)
    stage_gemm(C, 8, hk, copy_to(C.MG), norms=norms, stats=[(qn, i) for i in range(6)] + [(kvn, i) for i in range(2)],
               side=Side(pool=load_tables, dve_last=lambda dve: dve.wait_ge(ml.sem, ml.base + 32)))
    C.pinned = ()

    def rotate_key(dve, i, bank):
        if i == 0:
            return dve.tensor_tensor(L.KR[:], bank[:], L.RT[:, 2], ALU.mult)
        C.vchain.link(dve, dve.tensor_tensor(L.T[:], bank[:], L.RT[:, 3], ALU.mult))
        return dve.tensor_tensor(L.KR[:], L.KR[:], L.T[:], ALU.add)

    def rotate_query(dve, h, bank):
        return dve.tensor_tensor(L.Q[:, h, :], bank[:], L.RT[:, h % 2], ALU.mult)
    stage_gemm(C, 2, hk, rotate_key, "vector", norms=[qn, kvn])
    stage_gemm(C, 16, QP.tiles(6), rotate_query, "vector")
    stage_tokmajor(C, 4, L.KV.tiles(2), lambda half, t: L.V[:, t, half * 512:half * 512 + 512], TC)
    L.Y = L.Q
    L.Z = C.at("mla_z", [P, KD, T], C.MG_OFF)
    stage_mla(C, L)
    return gated_output(C, L.Y, A, A + 32 * KB, L.Z, 2)


def stage_sgu(C, L):
    nc = C.nc
    C.pinned = (4, 5, 6, 7)
    tiles = [C.take_tile(KD) for _ in range(KD)]
    C.pinned = ()
    banks = [C.take_given(4 + j % 4) for j in range(KD)]
    vn = C.reserve("vn", TC)
    sq = C.reserve("lnsq", 2)
    wm = C.reserve("wm", 1)
    with nc.Block(no_gpsimd_drain=True) as block:
        @block.sync
        def _(sp):
            C.load_slabs(sp)

        @block.scalar
        def _(act):
            act.wait_ge(sq.sem, sq.at(0))
            act.activation(L.MV[:, :, 1:2], L.MV[:, :, 1:2], ACT.Sqrt, bias=C.eps[:]).then_inc(sq.sem, 1)
            for i, (u, _) in enumerate(tiles):
                C.split_high(act, u)
                C.full(act, u)
                act.activation(L.Z[:, i, :], C.bank[u.b][:], ACT.Copy).then_inc(C.bank_read[u.b], 1)

        @block.vector
        def _(dve):
            ln = lambda ins: C.vchain.link(dve, ins)
            for t in range(TC):
                for half in range(2):
                    ln(dve.bn_stats(L.BN[:, t, half], L.V[:, t, half * 512:half * 512 + 512]))
                ln(dve.bn_aggr(L.MV[:, t, :], L.BN[:, t]))
            dve.sem_inc(sq.sem, 1)
            dve.wait_ge(sq.sem, sq.at(1))
            ln(dve.reciprocal(L.MV[:, :, 1:2], L.MV[:, :, 1:2]))
            for i, (u, _) in enumerate(tiles):
                if i < TC:
                    v = L.V[:, i, :]
                    ln(dve.tensor_scalar(v, v, L.MV[:, i, 0:1], L.MV[:, i, 1:2], ALU.subtract, ALU.mult))
                    ln(dve.tensor_tensor(v, v, L.LG[:, 0, :], ALU.mult))
                    dve.tensor_tensor(v, v, L.LG[:, 1, :], ALU.add).then_inc(vn.sem, 1)
                if i == TC:
                    dve.tensor_tensor(L.W[:], L.W[:], C.mask[:].unsqueeze(1).to_broadcast([P, 16, P]), ALU.mult)\
                        .then_inc(wm.sem, 1)
                C.split_low(dve, u)
            for j, u in enumerate(banks):
                C.full(dve, u)
                v = lambda ap: ap.rearrange("p (n t) -> p n t", n=TC)
                b = L.BS[:, j, :].unsqueeze(1).to_broadcast([P, TC, P])
                s = C.sq[:, j % 4, :]
                ln(dve.tensor_tensor(v(s), v(C.bank[u.b][:]), b, ALU.add))
                dve.tensor_tensor(L.U[:, j, :], L.U[:, j, :], s, ALU.mult).then_inc(C.bank_read[u.b], 1)

        @block.tensor
        def _(pe):
            seen = set()
            for t in tiles:
                C.gemm(pe, t, C.H.tiles(KD), seen)
            pe.wait_ge(wm.sem, wm.at(0))
            for j, u in enumerate(banks):
                C.open(pe, u)
                for n in range(TC):
                    if j == 0:
                        pe.wait_ge(vn.sem, vn.at(n))
                    for e in range(2):
                        g = 2 * j + e
                        mm = pe.matmul(C.bank[u.b][64 * e:64 * e + 64, n * P:(n + 1) * P], L.V[:, n, g * 64:g * 64 + 64],
                                       L.W[:, g, :], start=True, stop=True)
                mm.then_inc(C.bank_full[u.b], 1)


def branch_sgu(C, last):
    KB, A = 1024, C.arena
    L = Layout()
    L.U = C.at("sgu_u", [P, KD, T], A)
    L.V = C.at("sgu_v", [P, TC, DM], A + 16 * KB)
    L.Z = C.at("sgu_z", [P, KD, T], A + 32 * KB)
    L.W = C.at("sgu_w", [P, 16, P], A + 48 * KB)
    L.BS = C.at("sgu_bs", [P, KD, P], A + 56 * KB)
    L.LG = C.at("sgu_ln", [P, 2, DM], A + 60 * KB)
    L.BN = C.at("sgu_bn", [P, TC, 2, 6], A + 68 * KB)
    L.MV = C.at("sgu_mv", [P, TC, 2], A + 69 * KB)
    hk = C.H.tiles(KD)
    norms = pre_norm(C, last, 3)
    ld = C.reserve("sgu_loaded", 48)

    def load(pool):
        for dst, src in ((L.W, C.io["sgu_w"]), (L.BS, C.io["sgu_bs"]), (L.LG, C.io["sgu_ln"])):
            pool.dma_start(dst[:], src).then_inc(ld.sem, 16)
    stage_gemm(C, KD, hk, copy_to(L.U, ACT.Gelu_apprx_tanh), norms=norms,
               side=Side(pool=load, dve_last=lambda dve: dve.wait_ge(ld.sem, ld.base + 48)))
    stage_tokmajor(C, 4, hk, lambda half, t: L.V[:, t, half * 512:half * 512 + 512], TC, ACT.Gelu_apprx_tanh)
    stage_sgu(C, L)
    return gated_output(C, L.U, A, C.MG_OFF, L.Z, 3)


def second_block(C, upto, last):
    for layer, branch in enumerate((branch_s5, branch_swa, branch_mla, branch_sgu)):
        if upto >= layer + 2:
            last = branch(C, last)
    return last


def stage_finish(C, last):
    st = C.reserve("stored", 16 * KD)
    with C.nc.Block(no_gpsimd_drain=True) as block:
        @block.scalar
        def _(act):
            last.on_act(act)

        @block.vector
        def _(dve):
            last.on_dve(dve)

        @block.gpsimd
        def _(pool):
            last.on_pool(pool)

        @block.sync
        def _(sp):
            for k in range(KD):
                last.done(sp, k)
                sp.dma_start(C.io["yT"][:, k, :], C.X[:, k, :]).then_inc(st.sem, 16)
            sp.wait_ge(st.sem, st.base + 16 * KD)


def build(nc, io, upto=99):
    io["rot"] = nc.dram_tensor("rotation_tables", [32, P, 2, T], F32, kind="Internal").ap()
    io["bias_rows"] = nc.dram_tensor("bias_rows", [16, P, 384], F32, kind="Internal").ap()
    C = Core(nc, io)
    C.X_OFF = C.off
    C.X = C.fixed("x", [P, KD, T])
    C.H = Pair(C.fixed("h_high", [P, KD, T], F32R), C.fixed("h_low", [P, KD, T], F32R))
    ring_at = C.off
    C.ring = C.fixed("ring", [P, RING, SLAB * P])
    C.ring_low = C.at("ring_low", [P, RING, SLAB * P], ring_at, F32R)
    C.ring_high = C.fixed("ring_high", [P, AHEAD, SLAB * P], F32R)
    C.MG_OFF = C.off
    C.MG = C.fixed("merged", [P, KD, T])
    C.SQ_OFF = C.off
    C.sq = C.fixed("sq", [P, 4, T])
    C.ROOT_OFF = C.off
    C.root = C.fixed("root", [P, 4, T])
    C.cols = C.fixed("cols", [P, NCOL])
    C.ones = C.fixed("ones", [P, P])
    C.ident = C.fixed("ident", [P, P])
    C.mask = C.fixed("mask", [P, P])
    C.eps = C.fixed("eps", [P, 8])[:, 0:1]
    C.st = C.fixed("st", [P, 4, 8])
    C.s5 = Layout()
    C.s5.cos, C.s5.sin, C.s5.mag, C.s5.fre, C.s5.fim = [C.fixed(f"s5_{n}", [P, 32]) for n in ("cos", "sin", "mag", "fre", "fim")]
    C.s5.tmp = C.fixed("s5_tmp", [P, 4, 32])
    C.lru_tmp = C.fixed("lru_tmp", [P, 5, 12])
    C.s5.pw = C.fixed("s5_pw", [P, 5, NR])
    C.arena = (C.off + 63) // 64 * 64
    C.ARENA_END = 229344
    stage_load(C)
    last = first_block(C)
    if upto > 1:
        last = second_block(C, upto, last)
    stage_finish(C, last)


def pack_slabs(w):
    out, plain = weight_stream()
    n = len(plain)
    slabs = np.zeros((n, P, SLAB * P), np.float32)
    for b, blk in enumerate(out):
        if blk is None:
            continue
        name, rows, cols = blk
        s, i = divmod(b, SLAB)
        dst = slabs[s, :, i * P:(i + 1) * P]
        if name in ("lru_w_a", "lru_w_x"):
            for blk in range(LRU_W // LRU_B):
                lo, hi = blk * LRU_B, (blk + 1) * LRU_B
                r0, r1 = max(lo, rows[0]), min(hi, rows[-1] + 1)
                c0, c1 = max(lo, cols[0]), min(hi, cols[-1] + 1)
                if r0 < r1 and c0 < c1:
                    dst[r0 - rows[0]:r1 - rows[0], c0 - cols[0]:c1 - cols[0]] = w[name][blk, r0 - lo:r1 - lo, c0 - lo:c1 - lo]
            continue
        m = w[name]
        if np.all(cols >= 0):
            dst[:, :] = m[rows[:, None], cols[None, :]]
        else:
            ok = cols >= 0
            dst[:, ok] = m[rows[:, None], cols[ok][None, :]]
    return slabs


def pack_cols(v):
    out = np.zeros((P, NCOL), np.float32)
    for name, k in COLS:
        a = v[name]
        out[:a.shape[0], COL_AT[name]:COL_AT[name] + k] = a
    return out


def channels(a):
    a = np.asarray(a).reshape(-1)
    return np.ascontiguousarray(a.reshape(-1, P).T)


def shape_tables():
    j = np.arange(384)
    dist = 255 - j
    d = np.maximum(dist, 1).astype(np.float32)
    large = 16 + (np.log(d / 16) / np.float32(np.log(8.0)) * 16).astype(np.int32)
    bucket = np.where(dist < 16, dist, np.minimum(large, 31))
    valid = (dist >= 0) & (dist < 128)
    onehot = ((np.arange(32)[:, None] == bucket[None]) & valid[None]).astype(np.float32)
    neg = np.repeat(np.where(valid, 0.0, NEG).astype(np.float32)[None], 16, 0)
    inv = (np.float32(10000.0) ** (-np.arange(0, 32, 2, dtype=np.float32) / 32)).astype(np.float32)
    ang = inv[:, None] * np.arange(T, dtype=np.float32)[None]
    c, s = np.cos(ang), np.sin(ang)
    cos, sin, one = np.concatenate([c, c]), np.concatenate([-s, s]), np.ones((64, T), np.float32)
    rope = np.stack([np.concatenate([one, cos, sin]), np.concatenate([cos, sin, one]), np.tile(cos, (4, 1)),
                     np.tile(sin, (4, 1))], 1).astype(np.float32)
    causal = np.zeros((P, T), np.float32)
    causal[:, T - P:] = np.where(np.arange(P)[None] <= np.arange(P)[:, None], 0.0, NEG)
    return {"bucket_onehot": onehot, "neg_row": neg, "rope": rope, "causal": causal}


def pack_s5_c(c):
    out = np.zeros((P, 32, 32), np.float32)
    for g in range(64):
        j, e = divmod(g, 2)
        out[64 * e:64 * e + 64, j, 16 * e:16 * e + 16] = c[g].T
    return out


def host_arrays(i):
    i = {k: np.asarray(v) for k, v in i.items()}
    w = {"w_in": i["w_in"][0], "w_br_ssd": i["w_br_ssd"][0], "w_br_lru": i["w_br_lru"][0], "w_br_mem": i["w_br_mem"][0],
         "w_out": i["w_out"][0], "w_kv": i["w_kv"][0], "lru_w_a": i["lru_w_a"][0], "lru_w_x": i["lru_w_x"][0],
         "a_w_in": i["a_w_in_2"][0], "a_w_glu": i["a_w_glu_2"][0], "a_w_out": i["a_w_out_2"][0],
         "b_w_in": i["b_w_in_2"][0], "b_w_out": i["b_w_out_2"][0], "c_w_in": i["c_w_in_2"][0], "c_w_uq": i["c_w_uq_2"][0],
         "c_w_ukv": i["c_w_ukv_2"][0], "c_w_out": i["c_w_out_2"][0], "d_w_in": i["d_w_in_2"][0], "d_w_out": i["d_w_out_2"][0]}
    dup = lambda a: np.repeat(a.reshape(-1), 64)
    v = {"norm_g": channels(i["norm_g"]), "conv_w": channels(i["ssd_conv_w"]), "conv_b": channels(i["ssd_conv_b"]),
         "ssd_d": channels(dup(i["ssd_d"])), "ssd_norm_g": channels(i["ssd_norm_g"]),
         "dt_bias": i["ssd_dt_bias"].reshape(32, 1), "a_log": i["ssd_a_log"].reshape(32, 1),
         "lru_conv_w": channels(i["lru_conv_w"]), "lru_conv_b": channels(i["lru_conv_b"]),
         "b_a": channels(i["lru_b_a"]), "b_x": channels(i["lru_b_x"]), "lam": channels(i["lru_lambda"]),
         "mem_norm_g": channels(i["mem_norm_g"]), "final_g": channels(i["final_g"]),
         "pre_norm": channels(i["pre_norm_2"]), "post_norm": channels(i["post_norm_2"]), "a_d": channels(i["a_d_2"]),
         "b_glu": channels(i["a_b_glu_2"]), "lam_re": channels(i["a_lam_re_2"]), "lam_im": channels(i["a_lam_im_2"]),
         "log_dt": channels(dup(i["a_log_dt_2"])), "q_norm": channels(i["c_q_norm_2"]), "kv_norm": channels(i["c_kv_norm_2"]),
         "sinks": np.repeat(i["b_sinks_2"].reshape(1, 16), P, 0)}
    return {"xT": np.ascontiguousarray(i["x"][0].T.reshape(KD, P, T).transpose(1, 0, 2)),
            "memT": np.ascontiguousarray(i["mem"][0].T.reshape(KD, P, MEM).transpose(1, 0, 2)),
            "s5_b": np.stack([i[n][0].reshape(32, P, 16).transpose(1, 0, 2) for n in ("a_b_re_2", "a_b_im_2")], 1),
            "s5_c": np.stack([pack_s5_c(i[n][0]) for n in ("a_c_re_2", "a_c_im_2")], 1),
            "rel_bias": i["rel_bias_2"],
            "sgu_w": np.ascontiguousarray(i["d_w_s_2"][0].transpose(2, 0, 1)),
            "sgu_bs": np.ascontiguousarray(np.repeat(i["d_b_s_2"][0].reshape(8, 2, 1, P), 64, 2).reshape(8, P, P).transpose(1, 0, 2)),
            "sgu_ln": np.ascontiguousarray(np.repeat(np.stack([i["d_ln_g_2"][0], i["d_ln_b_2"][0]])[None], P, 0)),
            **shape_tables(), "slabs": pack_slabs(w), "cols": pack_cols(v)}


def kernel(**inputs):
    import concourse.bacc as bacc
    from concourse.bass_utils import run_bass_kernel_spmd

    nc = bacc.Bacc("TRN2", target_bir_lowering=False, num_devices=1)
    arrays = host_arrays(inputs)
    io = {k: nc.dram_tensor(k, a.shape, F32, kind="ExternalInput").ap() for k, a in arrays.items()}
    io["yT"] = nc.dram_tensor("yT", [P, KD, T], F32, kind="ExternalOutput").ap()
    build(nc, io)
    r = run_bass_kernel_spmd(nc, [arrays], core_ids=[0])
    y = r.results[0]["yT"]
    return np.ascontiguousarray(y.transpose(1, 0, 2).reshape(DM, T).T).reshape(1, T, DM)
```
